# Optimizing a Trainium2 kernel written in Bass

```python
import math
import jax, jax.numpy as jnp
from jax import lax
import numpy as np

D_MODEL = 2048
BATCH = 1
SEQ = 256
DEPTH = 1

GRID_W = 64
CTX_LEN = 256
EPS = 1e-6
N_MOD = 6

D_MIX = D_MODEL
D_FOURIER = D_MIX // 2
N_FOURIER_GROUPS = 4
FOURIER_GROUP = D_FOURIER // N_FOURIER_GROUPS
D_SSM = D_MIX - D_FOURIER
SSM_HEAD_DIM = 64
SSM_HEADS = D_SSM // SSM_HEAD_DIM
SSM_GROUPS = 2
SSM_STATE = 128
SSM_CONV = 3
SSM_CHUNK = 128
D_BC = SSM_GROUPS * SSM_STATE
D_XBC = D_SSM + 2 * D_BC
OFF_Z = D_FOURIER
OFF_XBC = OFF_Z + D_SSM
OFF_DT = OFF_XBC + D_XBC
D_IN_PROJ = OFF_DT + 2 * SSM_HEADS

PEER_HEADS = 8
PEER_TOPK = 16
PEER_N_KEYS = 128
PEER_EXPERTS = PEER_N_KEYS * PEER_N_KEYS
PEER_KEY_DIM = 128
PEER_HALF = PEER_KEY_DIM // 2
PEER_TOKEN_BLOCK = 128

kernel_name = 'fourier_ssd_peer_hybrid_dit'

def rms_norm(u, g):
    uf = u.astype(jnp.float32)
    y = uf * lax.rsqrt(jnp.mean(uf * uf, axis=-1, keepdims=True) + EPS)
    return (y * g.astype(jnp.float32)).astype(u.dtype)

def group_rms_norm(u, g, n_groups):
    shp = u.shape
    ug = u.reshape(*shp[:-1], n_groups, shp[-1] // n_groups).astype(jnp.float32)
    y = ug * lax.rsqrt(jnp.mean(ug * ug, axis=-1, keepdims=True) + EPS)
    return (y.reshape(shp) * g.astype(jnp.float32)).astype(u.dtype)

def adaln_params(cond, w_mod, b_mod):
    m = jax.nn.silu(cond) @ w_mod + b_mod
    return jnp.split(m[:, None, :], N_MOD, axis=-1)

def modulate(h, shift, scale):
    return h * (1 + scale) + shift

def centred_dwconv(u, w, b):
    k = w.shape[0]
    pad = k // 2
    length = u.shape[1]
    up = jnp.pad(u, ((0, 0), (pad, k - 1 - pad), (0, 0)))
    return sum(up[:, i:i + length] * w[i] for i in range(k)) + b

def segsum(a):
    t = a.shape[-1]
    cs = jnp.cumsum(a, axis=-1)
    diff = cs[..., :, None] - cs[..., None, :]
    mask = jnp.tril(jnp.ones((t, t), dtype=bool))
    return jnp.where(mask, diff, -jnp.inf)

def ssd_chunked(xs, dt, a, bm, cm, init):
    bsz, length, h, p = xs.shape
    nc = length // SSM_CHUNK
    ch = lambda t: t.reshape(bsz, nc, SSM_CHUNK, *t.shape[2:])
    xdt = ch(xs * dt[..., None])
    bc, cc = ch(bm), ch(cm)
    a_dt = jnp.moveaxis(ch(dt * a), -1, 1)
    a_cum = jnp.cumsum(a_dt, axis=-1)
    l_mat = jnp.exp(segsum(a_dt))
    y_diag = jnp.einsum('bclhn,bcshn,bhcls,bcshp->bclhp', cc, bc, l_mat, xdt)
    decay_states = jnp.exp(a_cum[..., -1:] - a_cum)
    states = jnp.einsum('bclhn,bhcl,bclhp->bchpn', bc, decay_states, xdt)
    states = jnp.concatenate([init[:, None], states], axis=1)
    chunk_decay = jnp.exp(segsum(jnp.pad(a_cum[..., -1], ((0, 0), (0, 0), (1, 0)))))
    new_states = jnp.einsum('bhzc,bchpn->bzhpn', chunk_decay, states)
    states, final = new_states[:, :-1], new_states[:, -1]
    y_off = jnp.einsum('bclhn,bchpn,bhcl->bclhp', cc, states, jnp.exp(a_cum))
    return (y_diag + y_off).reshape(bsz, length, h, p), final

def fourier_branch(proj, w_fmix):
    bsz, length, _ = proj.shape
    f = proj[..., :OFF_Z].reshape(bsz, length, N_FOURIER_GROUPS, FOURIER_GROUP)
    fr = jnp.fft.fftn(f.astype(jnp.float32), axes=(1, 3), norm='ortho').real.astype(proj.dtype)
    return jnp.einsum('blgc,gcd->blgd', fr, w_fmix).reshape(bsz, length, D_FOURIER)

def ssd_branch(proj, conv_w, conv_b, dt_bias_f, dt_bias_b, a_log_f, a_log_b,
               d_skip_f, d_skip_b, ssm_norm_w, init_f, init_b):
    bsz, length, _ = proj.shape
    f32 = jnp.float32
    z = proj[..., OFF_Z:OFF_XBC]
    xbc = jax.nn.silu(centred_dwconv(proj[..., OFF_XBC:OFF_DT], conv_w, conv_b)).astype(f32)
    dt_raw = proj[..., OFF_DT:].astype(f32)
    rep = SSM_HEADS // SSM_GROUPS
    xs = xbc[..., :D_SSM].reshape(bsz, length, SSM_HEADS, SSM_HEAD_DIM)
    bm = jnp.repeat(xbc[..., D_SSM:D_SSM + D_BC].reshape(bsz, length, SSM_GROUPS, SSM_STATE), rep, axis=2)
    cm = jnp.repeat(xbc[..., D_SSM + D_BC:].reshape(bsz, length, SSM_GROUPS, SSM_STATE), rep, axis=2)
    dt_f = jax.nn.softplus(dt_raw[..., :SSM_HEADS] + dt_bias_f.astype(f32))
    dt_b = jax.nn.softplus(dt_raw[..., SSM_HEADS:] + dt_bias_b.astype(f32))
    a_f = -jnp.exp(a_log_f.astype(f32))
    a_b = -jnp.exp(a_log_b.astype(f32))
    flip = lambda t: jnp.flip(t, axis=1)
    y_f, fin_f = ssd_chunked(xs, dt_f, a_f, bm, cm, init_f)
    y_b, fin_b = ssd_chunked(flip(xs), flip(dt_b), a_b, flip(bm), flip(cm), init_b)
    y = y_f + flip(y_b) + (d_skip_f + d_skip_b).astype(f32)[:, None] * xs
    y = y.reshape(bsz, length, D_SSM).astype(proj.dtype)
    y = group_rms_norm(y * jax.nn.silu(z), ssm_norm_w, SSM_GROUPS)
    return y, fin_f, fin_b

def peer_ffn(h, w_query, sub_keys_1, sub_keys_2, expert_u, expert_v):
    bsz, length, d = h.shape
    tokens = h.reshape(-1, PEER_TOKEN_BLOCK, d)

    def block(tb):
        tbn = tb.shape[0]
        q = (tb @ w_query).reshape(tbn, PEER_HEADS, PEER_KEY_DIM)
        s1 = jnp.einsum('thd,hkd->thk', q[..., :PEER_HALF], sub_keys_1)
        s2 = jnp.einsum('thd,hkd->thk', q[..., PEER_HALF:], sub_keys_2)
        v1, i1 = lax.top_k(s1, PEER_TOPK)
        v2, i2 = lax.top_k(s2, PEER_TOPK)
        cand = (v1[..., :, None] + v2[..., None, :]).reshape(tbn, PEER_HEADS, PEER_TOPK * PEER_TOPK)
        cand_idx = (i1[..., :, None] * PEER_N_KEYS + i2[..., None, :]).reshape(tbn, PEER_HEADS, PEER_TOPK * PEER_TOPK)
        top_s, pos = lax.top_k(cand, PEER_TOPK)
        idx = jnp.take_along_axis(cand_idx, pos, axis=-1)
        gate = jax.nn.softmax(top_s.astype(jnp.float32), axis=-1).astype(tb.dtype)
        u = expert_u[idx]
        v = expert_v[idx]
        act = jax.nn.gelu(jnp.einsum('td,thkd->thk', tb, u), approximate=False)
        return jnp.einsum('thk,thkd->td', gate * act, v)

    out = lax.map(block, tokens)
    return out.reshape(bsz, length, d)

def setup_inputs(seed: int = 0) -> dict:
    key = jax.random.key(seed)
    ks = jax.random.split(key, 32)
    nrm = lambda k, shp, s: jax.random.normal(k, shp, jnp.float32) * s
    dt0 = jnp.exp(jax.random.uniform(ks[14], (DEPTH, SSM_HEADS), minval=math.log(1e-3), maxval=math.log(1e-1)))
    dt1 = jnp.exp(jax.random.uniform(ks[15], (DEPTH, SSM_HEADS), minval=math.log(1e-3), maxval=math.log(1e-1)))
    return {
        'x': nrm(ks[0], (BATCH, SEQ, D_MODEL), 1.0),
        'c': nrm(ks[1], (BATCH, D_MODEL), 1.0),
        'ctx': nrm(ks[2], (BATCH, CTX_LEN, D_MODEL), 1.0),
        'c_ctx': nrm(ks[3], (D_MODEL,), 1.0),
        'w_mod': nrm(ks[4], (DEPTH, D_MODEL, N_MOD * D_MODEL), 0.5 * D_MODEL ** -0.5),
        'b_mod': nrm(ks[5], (DEPTH, N_MOD * D_MODEL), 0.01),
        'g_pre_mix': 1.0 + nrm(ks[6], (DEPTH, D_MODEL), 0.01),
        'g_post_mix': 1.0 + nrm(ks[7], (DEPTH, D_MODEL), 0.01),
        'g_pre_ffn': 1.0 + nrm(ks[8], (DEPTH, D_MODEL), 0.01),
        'g_post_ffn': 1.0 + nrm(ks[9], (DEPTH, D_MODEL), 0.01),
        'w_in': nrm(ks[10], (DEPTH, D_MODEL, D_IN_PROJ), D_MODEL ** -0.5),
        'w_fmix': nrm(ks[11], (DEPTH, N_FOURIER_GROUPS, FOURIER_GROUP, FOURIER_GROUP), FOURIER_GROUP ** -0.5),
        'conv_w': nrm(ks[12], (DEPTH, SSM_CONV, D_XBC), SSM_CONV ** -0.5),
        'conv_b': nrm(ks[13], (DEPTH, D_XBC), 0.01),
        'dt_bias_f': dt0 + jnp.log(-jnp.expm1(-dt0)),
        'dt_bias_b': dt1 + jnp.log(-jnp.expm1(-dt1)),
        'a_log_f': jnp.log(jax.random.uniform(ks[16], (DEPTH, SSM_HEADS), minval=1.0, maxval=16.0)),
        'a_log_b': jnp.log(jax.random.uniform(ks[17], (DEPTH, SSM_HEADS), minval=1.0, maxval=16.0)),
        'd_skip_f': 1.0 + nrm(ks[18], (DEPTH, SSM_HEADS), 0.1),
        'd_skip_b': 1.0 + nrm(ks[19], (DEPTH, SSM_HEADS), 0.1),
        'ssm_norm_w': 1.0 + nrm(ks[20], (DEPTH, D_SSM), 0.01),
        'w_out': nrm(ks[21], (DEPTH, D_MIX, D_MODEL), D_MIX ** -0.5),
        'w_query': nrm(ks[22], (DEPTH, D_MODEL, PEER_HEADS * PEER_KEY_DIM), D_MODEL ** -0.5),
        'sub_keys_1': nrm(ks[23], (DEPTH, PEER_HEADS, PEER_N_KEYS, PEER_HALF), PEER_HALF ** -0.5),
        'sub_keys_2': nrm(ks[24], (DEPTH, PEER_HEADS, PEER_N_KEYS, PEER_HALF), PEER_HALF ** -0.5),
        'expert_u': nrm(ks[25], (DEPTH, PEER_EXPERTS, D_MODEL), D_MODEL ** -0.5),
        'expert_v': nrm(ks[26], (DEPTH, PEER_EXPERTS, D_MODEL), D_MODEL ** -0.5),
    }

def reference(x, c, ctx, c_ctx, w_mod, b_mod, g_pre_mix, g_post_mix, g_pre_ffn, g_post_ffn,
              w_in, w_fmix, conv_w, conv_b, dt_bias_f, dt_bias_b, a_log_f, a_log_b,
              d_skip_f, d_skip_b, ssm_norm_w, w_out, w_query, sub_keys_1, sub_keys_2,
              expert_u, expert_v):
    bsz = x.shape[0]
    for layer in range(DEPTH):
        sm_x, cm_x, gm_x, sf_x, cf_x, gf_x = adaln_params(c, w_mod[layer], b_mod[layer])
        sm_c, cm_c, gm_c, sf_c, cf_c, gf_c = adaln_params(c_ctx[None], w_mod[layer], b_mod[layer])
        ssd_args = (conv_w[layer], conv_b[layer], dt_bias_f[layer], dt_bias_b[layer], a_log_f[layer],
                    a_log_b[layer], d_skip_f[layer], d_skip_b[layer], ssm_norm_w[layer])

        hc = modulate(rms_norm(ctx, g_pre_mix[layer]), sm_c, cm_c)
        proj_c = hc @ w_in[layer]
        zero_state = jnp.zeros((bsz, SSM_HEADS, SSM_HEAD_DIM, SSM_STATE), jnp.float32)
        y_c_ssm, fin_f, fin_b = ssd_branch(proj_c, *ssd_args, zero_state, zero_state)

        hx = modulate(rms_norm(x, g_pre_mix[layer]), sm_x, cm_x)
        proj_x = hx @ w_in[layer]
        y_x_ssm, _, _ = ssd_branch(proj_x, *ssd_args, fin_f, fin_b)
        y_x = jnp.concatenate([fourier_branch(proj_x, w_fmix[layer]), y_x_ssm], axis=-1) @ w_out[layer]
        x = x + gm_x * rms_norm(y_x, g_post_mix[layer])

        if layer + 1 < DEPTH:
            y_c = jnp.concatenate([fourier_branch(proj_c, w_fmix[layer]), y_c_ssm], axis=-1) @ w_out[layer]
            ctx = ctx + gm_c * rms_norm(y_c, g_post_mix[layer])
            hc2 = modulate(rms_norm(ctx, g_pre_ffn[layer]), sf_c, cf_c)
            ctx = ctx + gf_c * rms_norm(peer_ffn(hc2, w_query[layer], sub_keys_1[layer], sub_keys_2[layer],
                                                 expert_u[layer], expert_v[layer]), g_post_ffn[layer])

        hx2 = modulate(rms_norm(x, g_pre_ffn[layer]), sf_x, cf_x)
        y_f = peer_ffn(hx2, w_query[layer], sub_keys_1[layer], sub_keys_2[layer], expert_u[layer], expert_v[layer])
        x = x + gf_x * rms_norm(y_f, g_post_ffn[layer])
    return x


_drawn_inputs = setup_inputs


def setup_inputs(seed=0):
    import zlib

    import numpy as np

    out = dict(_drawn_inputs(seed))
    spreads = {}
    factors = {'g_pre_mix': 2.974,
     'g_post_mix': 3.303,
     'g_post_ffn': 50.699,
     'conv_b': 3.29,
     'ssm_norm_w': 3.975,
     'd_skip_f': 2.979,
     'd_skip_b': 3.087}
    for name, (base, spread) in spreads.items():
        noise = np.random.default_rng([zlib.crc32(name.encode()), seed]).standard_normal(out[name].shape)
        drawn = base * np.exp(spread * noise) if base else spread * noise
        out[name] = __import__('jax').numpy.asarray(drawn.astype(out[name].dtype))
    for name, factor in factors.items():
        out[name] = (out[name] * factor).astype(out[name].dtype)
    return out
```

```python
from contextlib import ExitStack

import concourse.bass as bass
from concourse import mybir

F32 = mybir.dt.float32
U32 = mybir.dt.uint32
ALU = mybir.AluOpType
ACT = mybir.ActivationFunctionType
AX = mybir.AxisListType

P = 128
D = 2048
KT = D // P
NQ = 512
EPS = 1e-6
HEADS, HD = 16, 64
OFF_XBC, OFF_DT = 2048, 3584
XBLK, BBLK, NBLK = 8, 10, 12
GROUPS = 4
PH = 8
TOPK = 16
NKEYS = 128
UNITS = 2 * PH
GR = 4
NU = 8
TAILS = 4
MASKED = -1e30
LOWEST = -3.0e38

C_C, C_CTX, C_BMOD, C_GPM, C_GQM, C_GPF, C_GQF, C_CW, C_CB, C_NW = 0, 16, 32, 128, 144, 160, 176, 192, 228, 240
NCOL = 248
K_ID, K_ONE, K_TU, K_TL, K_MF, K_MB, K_ZERO = range(7)
NCST = 7
KIB = 256

RING = ([("mod", n * NQ) for n in range(8)]
        + [("in", OFF_XBC + n * NQ) for n in range(3)]
        + [("in", n * NQ) for n in range(4)]
        + [("out", n * NQ) for n in range(4)]
        + [("query", n * NQ) for n in range(2)])
R_XBC, R_FZ, R_OUT, R_QUERY = 8, 11, 15, 19

STATES = [(2, 0), (3, 0), (3, 1), (2, 1), (0, 0), (1, 1)]


def build(nc, x, ctx_in, w_mod, w_in, w_fmix, w_out, w_query, k1t, k2t, expert_u, expert_v,
          cols_in, rows_in, cst_in, dft_in, iota_in, out):
    with ExitStack() as ctx:
        arena = ctx.enter_context(nc.sbuf_tensor("arena", [P, 207 * KIB], F32))
        PS = ctx.enter_context(nc.psum_tensor("PS", [P, 8, NQ], F32))

        def sem(name):
            return ctx.enter_context(nc.semaphore(name))

        def at(kib, words):
            assert int(kib * KIB) + words <= 207 * KIB
            return arena[:, int(kib * KIB):int(kib * KIB) + words]

        wring = [at(32 * s, 8192).rearrange("p (k n) -> p k n", k=KT) for s in range(2)]
        xrow = [at(64 + 8 * t, D) for t in range(2)]
        fmix = at(64, 2048).rearrange("p (g b n) -> p g b n", g=GROUPS, b=2)
        dt_raw, dt_abs, dt, adt, cum, wst, ecum, dec = [at(72 + 0.5 * i, 128) for i in range(8)]
        dtw = at(76, 512).rearrange("p (k h) -> p k h", k=KT)
        hT = at(80, 8192).rearrange("p (s k t) -> p s k t", s=2, k=KT)
        SFA, SFB, SBA, SBB = [at(96 + 4 * i, 1024) for i in range(4)]
        PQ = at(80, 1024).rearrange("p (b n) -> p b n", b=2)
        AT = at(84, 1024).rearrange("p (b n) -> p b n", b=2)
        catF = at(88, 2048).rearrange("p (k t) -> p k t", k=8)
        tail_slot = [at(112 + 4 * s, 1024) for s in range(TAILS)]
        tail_acc = [at(128 + 4 * s, 1024) for s in range(2)]
        R = at(112, 2048)
        E = [at(120 + 8 * d, 2048) for d in range(2)]
        ctxrow = [at(136 + 8 * t, D) for t in range(2)]
        xn = [at(162 + 8 * t, D) for t in range(2)]
        xs = at(136, 4096).rearrange("p (t c) -> p t c", t=4)
        brow = at(152, 1024).rearrange("p (t g n) -> p t g n", t=4, g=2)
        BT = at(156, 1024).rearrange("p (g t) -> p g t", g=2)
        CT = at(160, 512).rearrange("p (g t) -> p g t", g=2)
        frow = [at(162 + 4 * t, 1024) for t in range(2)]
        zrow = [at(170 + 4 * t, 1024) for t in range(2)]
        catS = at(162, 2048).rearrange("p (k t) -> p k t", k=8)
        yrow = [at(136 + 8 * t, D) for t in range(2)]
        h2row = yrow
        Grow = [at(96, D), at(104, D), at(170, D), at(170, D)]
        h2T = at(80, 4096).rearrange("p (k t) -> p k t", k=KT)
        keys = at(152, 2048).rearrange("p (h n) -> p h n", h=PH)
        qT = at(162, 2048).rearrange("p (h t) -> p h t", h=PH)
        scores = at(96, 4096).rearrange("p (u n) -> p u n", u=UNITS)
        uslot = [at(8 * s, D) for s in range(NU)]
        vslot = [at(k, D) for k in (80, 88, 112, 120, 128, 152, 162, 191)]
        dft = at(178, 1536).rearrange("p (b m n) -> p b m n", b=2, m=3)
        diag_slot = [at(178 + 0.5 * s, P) for s in range(8)]
        cst = at(184, NCST * P).rearrange("p (m n) -> p m n", m=NCST)
        misc = at(187.5, 896)
        temp = at(191, 16 * KIB)
        modrow = [temp[:, 512 * i:512 * i + 512] for i in range(2)]
        convin = [temp[:, 516 * i:516 * i + 516].rearrange("p (s t) -> p s t", s=2) for i in range(2)]
        convmid = [temp[:, 1032 + 512 * i:1544 + 512 * i].rearrange("p (s t) -> p s t", s=2) for i in range(2)]
        convout = [temp[:, 2056 + 512 * i:2568 + 512 * i].rearrange("p (s t) -> p s t", s=2) for i in range(2)]
        wx = [temp[:, 0:1024], temp[:, 1024:2048]]
        yssm = [temp[:, 2048:3072], at(156, 1024)]
        GT = temp[:, 3080:3592].rearrange("p (g c l) -> p g c l", g=2, c=2)
        diag_all = temp[:, 0:2048].rearrange("p (k n) -> p k n", k=KT)
        ex = at(199, 7 * KIB)
        s_cur, s_cut = ex[:, 0:256], ex[:, 256:384]
        onehot = ex[:, 384:640].rearrange("p (a b) -> p a b", a=TOPK)
        cand, cand_cut = ex[:, 640:896], ex[:, 896:1152]

        used = [0]

        def small(n, space=misc, dtype=F32):
            a = used[0]
            used[0] += n
            assert used[0] <= 896
            return space.bitcast(dtype)[:, a:a + n] if dtype != F32 else space[:, a:a + n]

        cols = small(NCOL)
        s2 = small(2 * KT).rearrange("p (k c) -> p k c", c=2)
        modc = small(64).rearrange("p (n c) -> p n c", c=2)
        scl = small(2 * KT).rearrange("p (s k) -> p s k", s=2)
        shf = small(2 * KT).rearrange("p (s k) -> p s k", s=2)
        tailc = small(64).rearrange("p (v k) -> p v k", v=4)
        rowv = small(128)
        ssq, rstd = small(4), small(4)
        gsq, grs = small(4), small(4)
        ysq, yss = small(8), small(2)
        xsq, fsq = small(2), small(2)
        nmax = small(2)
        esum = small(2)
        iota16 = small(16)
        idx = small(32, dtype=U32).rearrange("p (b k) -> p b k", b=2)
        gate = small(32).rearrange("p (b k) -> p b k", b=2)
        dots = small(32).rearrange("p (b k) -> p b k", b=2)
        gelu = small(32).rearrange("p (b k) -> p b k", b=2)
        coef = small(32).rearrange("p (b k) -> p b k", b=2)
        exv = ex[:, 1152:1408]
        exu = exv.bitcast(U32)
        v12 = exv[:, 0:32].rearrange("p (a k) -> p a k", a=2)
        i12 = exu[:, 32:64].rearrange("p (a k) -> p a k", a=2)
        i12f = exv[:, 64:96].rearrange("p (a k) -> p a k", a=2)
        top, pos = exv[:, 96:112], exu[:, 112:128]
        posh = exu[:, 128:160].rearrange("p (a k) -> p a k", a=2)
        e12 = exv[:, 160:192].rearrange("p (a k) -> p a k", a=2)
        eexp = exv[:, 192:208]

        ident, ones, zeros = cst[:, K_ID, :], cst[:, K_ONE, :], cst[:, K_ZERO, :]

        def dth(v):
            return v.rearrange("p (d t h) -> p d t h", d=2, t=4)

        def per_head(v, d, t):
            return dth(v)[:, d, t, :].unsqueeze(2).to_broadcast([P, HEADS, HD])

        def heads(a):
            return a.rearrange("p (h c) -> p h c", h=HEADS)

        small_in = sem("small_in")
        row_in = [sem(f"row_in{t}") for t in range(4)]
        row_back = sem("row_back")
        late_in = sem("late_in")
        keys_in = sem("keys_in")
        ring_in = [sem(f"ring_in{s}") for s in range(2)]
        tail_in = [sem(f"tail_in{s}") for s in range(TAILS)]
        act_order, dve_order, pool_order = sem("act_order"), sem("dve_order"), sem("pool_order")
        s2_ready, ssq_ready, var_ready, std_ready = sem("s2_ready"), sem("ssq_ready"), sem("var_ready"), sem("std_ready")
        xn_ready, xt_ps, ht_evac = sem("xn_ready"), sem("xt_ps"), sem("ht_evac")
        mod_ps, modrow_evac, modT_ps, ht_mod = sem("mod_ps"), sem("modrow_evac"), sem("modT_ps"), sem("ht_mod")
        pads = sem("pads")
        xbc_ps, convin_evac, convmid_ready, cv_ready = sem("xbc_ps"), sem("convin_evac"), sem("convmid_ready"), sem("cv_ready")
        tr_ps, row_evac = sem("tr_ps"), sem("row_evac")
        tail_used, acc_done, col_ps = sem("tail_used"), sem("acc_done"), sem("col_ps")
        dt_ps, dtabs_ready, ln_ready, adt_ready, cum_ps = sem("dt_ps"), sem("dtabs_ready"), sem("ln_ready"), sem("adt_ready"), sem("cum_ps")
        cum_ready, dif_ready, dec_ready, wst_ready = sem("cum_ready"), sem("dif_ready"), sem("dec_ready"), sem("wst_ready")
        h_ps, h_evac, gt_ps, gt_evac = sem("h_ps"), sem("h_evac"), sem("gt_ps"), sem("gt_evac")
        r_ready, b_ps, d_ready, e_ready, m_ready = sem("r_ready"), sem("b_ps"), sem("d_ready"), sem("e_ready"), sem("m_ready")
        w_ready, st_ps, st_used, y_ps, y_used, y_init = sem("w_ready"), sem("st_ps"), sem("st_used"), sem("y_ps"), sem("y_used"), sem("y_init")
        o_ps, o_used = sem("o_ps"), sem("o_used")
        pq_ps, pq_evac, at_ps, at_evac, yf_ps, yf_evac = sem("pq_ps"), sem("pq_evac"), sem("at_ps"), sem("at_evac"), sem("yf_ps"), sem("yf_evac")
        yg_ready, gsq_ready, gvar_ready, gstd_ready, yn_ready, yt_ps, yt_evac = [sem(n) for n in (
            "yg_ready", "gsq_ready", "gvar_ready", "gstd_ready", "yn_ready", "yt_ps", "yt_evac")]
        wo_ps, wo_evac, diag_ready, g_ps, g_evac = sem("wo_ps"), sem("wo_evac"), sem("diag_ready"), sem("g_ps"), sem("g_evac")
        yvar_ready, ystd_ready, x1_ready, xsq_ready, xvar_ready, xstd_ready, h2_ready = [sem(n) for n in (
            "yvar_ready", "ystd_ready", "x1_ready", "xsq_ready", "xvar_ready", "xstd_ready", "h2_ready")]
        h2T_ps, h2T_evac, q_ps, q_evac, keys_zero, sc_ps, sc_evac = [sem(n) for n in (
            "h2T_ps", "h2T_evac", "q_ps", "q_evac", "keys_zero", "sc_ps", "sc_evac")]
        u_in = [sem(f"u_in{s}") for s in range(NU)]
        v_in = [sem(f"v_in{s}") for s in range(NU)]
        nmax_ready, eexp_ready, idx_ready, gate_ready = sem("nmax_ready"), sem("eexp_ready"), sem("idx_ready"), sem("gate_ready")
        u_used, v_used, coef_ready, pool_go = sem("u_used"), sem("v_used"), sem("coef_ready"), sem("pool_go")
        gelu_ready, coef_done, route_copy, route_step, dve_go = [sem(n) for n in (
            "gelu_ready", "coef_done", "route_copy", "route_step", "dve_go")]
        tailc_ready = sem("tailc_ready")
        acc_ps, fsq_ready, fvar_ready, fstd_ready, out_ready, out_done = [sem(n) for n in (
            "acc_ps", "fsq_ready", "fvar_ready", "fstd_ready", "out_ready", "out_done")]

        block = ctx.enter_context(nc.Block())

        def chain(eng, order):
            count = [0]

            def step(ins):
                count[0] += 1
                ins.then_inc(order, 1)
                eng.wait_ge(order, count[0])
            return step

        N_SMALL = 5

        def expert_blocks(eng, unit, after_block):
            unit(eng, 0, 0, 0)
            unit(eng, 1, 1, 0)
            with eng.Fori(2, PH, 2) as u:
                unit(eng, u, 0, 0)
                unit(eng, u + 1, 1, 0)
            after_block(eng, 0)
            with eng.Fori(PH, UNITS - 2, 2) as u:
                unit(eng, u, 0, 1)
                unit(eng, u + 1, 1, 1)
            unit(eng, UNITS - 2, 0, 1)
            unit(eng, UNITS - 1, 1, 1)
            after_block(eng, 1)

        @block.sync
        def _(sp):
            wide = {"mod": w_mod, "in": w_in, "out": w_out, "query": w_query}

            def ring_load(j):
                i = j - 2
                if i >= R_OUT:
                    sp.wait_ge(wo_ps, 2 * (i - R_OUT + 1))
                elif i >= R_FZ:
                    sp.wait_ge(h_ps, 2 * (i - R_FZ + 1))
                elif i >= R_XBC:
                    sp.wait_ge(xbc_ps, 4 * (i - R_XBC + 1))
                elif i >= 0:
                    sp.wait_ge(mod_ps, i + 1)
                name, c0 = RING[j]
                src = wide[name].rearrange("(k p) n -> p k n", p=P)[:, :, c0:c0 + NQ]
                sp.dma_start(wring[j % 2], src).then_inc(ring_in[j % 2], 16)

            ring_load(0)
            for t in range(2):
                sp.dma_start(xrow[t], x[t * P:(t + 1) * P, :]).then_inc(row_in[t], 16)
            for t in range(2):
                sp.dma_start(ctxrow[t], ctx_in[t * P:(t + 1) * P, :]).then_inc(row_in[2 + t], 16)
            ring_load(1)
            sp.wait_ge(xn_ready, 2)
            sp.dma_start(fmix, w_fmix.rearrange("g (b p) n -> p g b n", p=P)).then_inc(late_in, 16)
            sp.dma_start(dtw, w_in.rearrange("(k p) n -> p k n", p=P)[:, :, OFF_DT:OFF_DT + 32]).then_inc(late_in, 16)
            for j in range(2, R_OUT + 2):
                ring_load(j)
            sp.wait_ge(pq_ps, GROUPS)
            sp.wait_ge(yg_ready, 2)
            for t in range(2):
                sp.dma_start(xrow[t], x[t * P:(t + 1) * P, :]).then_inc(row_back, 16)
            sp.wait_ge(keys_zero, 1)
            sp.dma_start(keys[0:64, :, 0:NKEYS], k1t).then_inc(keys_in, 16)
            sp.dma_start(keys[64:P, :, NKEYS:2 * NKEYS], k2t).then_inc(keys_in, 16)
            for j in range(R_OUT + 2, len(RING)):
                ring_load(j)
            for t in range(2):
                sp.wait_ge(out_ready, t + 1)
                sp.dma_start(out[t * P:(t + 1) * P, :], xrow[t]).then_inc(out_done, 16)
            sp.wait_ge(out_done, 32)

        @block.gpsimd
        def _(pool):
            for i in range(2):
                for s in range(2):
                    for t in (0, 257):
                        pool.wait_ge(modT_ps, 8)
                        nc.gpsimd.memset(convin[i][:, s, t:t + 1], 0.0).then_inc(pads, 1)

            def tail_load(s, half, k):
                src = w_mod[bass.ds(k * P, P), bass.ds(half * 1024 + 4096, 1024)]
                nc.gpsimd.dma_start(tail_slot[s], src).then_inc(tail_in[s], 16)

            for s in range(TAILS):
                tail_load(s, 0, s)
            for k in range(TAILS, KT):
                pool.wait_ge(tail_used, k - TAILS + 1)
                tail_load(k % TAILS, 0, k)
            with pool.Fori(1, 6) as half:
                for k in range(KT):
                    pool.wait_ge(tail_used, half * KT + (k - TAILS + 1))
                    pool.sem_inc(pool_go, 1)
                    tail_load(k % TAILS, half, k)

            def weigh(n, t, v, d):
                nc.gpsimd.tensor_tensor(heads(wx[n % 2]), heads(xs[:, t, :]), per_head(v, d, t),
                                        ALU.mult).then_inc(w_ready, 1)

            pool.wait_ge(wst_ready, 1)
            pool.wait_ge(row_evac, BBLK)
            pool.wait_ge(tr_ps, BBLK)
            pool.wait_ge(cv_ready, NBLK)
            weigh(0, 2, wst, 0)
            weigh(1, 3, wst, 0)
            skip = [rowv[:, 64 + 16 * i:80 + 16 * i] for i in range(2)]
            nc.gpsimd.tensor_tensor(skip[0], skip[0], skip[1], ALU.add).then_inc(pool_order, 1)
            pool.wait_ge(pool_order, 1)
            pool.wait_ge(gt_ps, 1)
            for c in range(2):
                nc.gpsimd.tensor_tensor(heads(yssm[c]), heads(xs[:, c, :]),
                                        skip[0].unsqueeze(2).to_broadcast([P, HEADS, HD]), ALU.mult).then_inc(y_init, 1)
            pool.wait_ge(st_ps, 1)
            weigh(2, 3, wst, 1)
            pool.wait_ge(st_ps, 2)
            weigh(3, 2, wst, 1)
            pool.wait_ge(st_ps, 3)
            weigh(4, 0, dt, 0)
            pool.wait_ge(st_ps, 4)
            weigh(5, 0, dt, 1)
            pool.wait_ge(y_ps, 1)
            weigh(6, 0, wst, 0)
            weigh(7, 1, wst, 1)
            pool.wait_ge(st_ps, 5)
            weigh(8, 1, dt, 0)
            pool.wait_ge(st_ps, 6)
            weigh(9, 1, dt, 1)

            pool.wait_ge(yg_ready, 2)
            pool.wait_ge(y_ps, 2)
            for half in (6, 7):
                for k in range(KT):
                    n = half * KT + k
                    if n - 6 * KT >= TAILS:
                        pool.wait_ge(tail_used, n - TAILS + 1)
                    tail_load(k % TAILS, half, k)
            pool.wait_ge(yt_ps, 2)
            nc.gpsimd.memset(keys, 0.0).then_inc(keys_zero, 1)

            pool.wait_ge(g_ps, 4)

            def unit(eng, u, p, blk):
                eng.wait_ge(idx_ready, u + 1)
                for j in range(TOPK):
                    for table, slot, arrived, free in ((expert_u, uslot, u_in, u_used), (expert_v, vslot, v_in, v_used)):
                        if not (type(u) is int and u * TOPK + j < NU):
                            eng.wait_ge(free, u * TOPK + (j - NU + 1))
                            eng.sem_inc(pool_go, 1)
                        nc.gpsimd.indirect_dma_start(slot[j % NU], None, table,
                                                     bass.IndirectOffsetOnAxis(ap=idx[:, p, j:j + 1], axis=0),
                                                     ).then_inc(arrived[j % NU], 16)

            expert_blocks(pool, unit, lambda eng, blk: None)

        @block.scalar
        def _(act):
            step = chain(act, act_order)
            A = nc.scalar.activation
            act.dma_start(cols, cols_in).then_inc(small_in, 16)
            act.dma_start(cst, cst_in).then_inc(small_in, 16)
            act.dma_start(rowv, rows_in.to_broadcast([P, 128])).then_inc(small_in, 16)
            act.dma_start(dft, dft_in).then_inc(small_in, 16)
            act.dma_start(iota16, iota_in).then_inc(small_in, 16)
            act.wait_ge(small_in, 16 * N_SMALL)
            A(s2[:, :, 0], cols[:, C_C:C_C + KT], ACT.Silu).then_inc(s2_ready, 1)
            A(s2[:, :, 1], cols[:, C_CTX:C_CTX + KT], ACT.Silu).then_inc(s2_ready, 1)
            for t in range(4):
                act.wait_ge(row_in[t], 16)
                if t:
                    act.wait_ge(ssq_ready, t)
                A(PS[:, 4:8, :], (xrow + ctxrow)[t].rearrange("p (a b) -> p a b", a=4), ACT.Square,
                  accum_out=ssq[:, t:t + 1]).then_inc(ssq_ready, 1)
            act.wait_ge(var_ready, 1)
            A(rstd, rstd, ACT.Sqrt).then_inc(std_ready, 1)

            def modrow_out(i):
                act.wait_ge(mod_ps, i + 1)
                if i >= 2:
                    act.wait_ge(modT_ps, i - 1)
                A(modrow[i % 2][0:2, :], PS[0:2, 4 + i % 2, :], ACT.Copy).then_inc(modrow_evac, 1)

            def hT_out(t):
                for q in range(4):
                    act.wait_ge(xt_ps, 4 * t + q + 1)
                    A(hT[:, t // 2, 4 * q:4 * q + 4, (t % 2) * P:(t % 2 + 1) * P],
                      PS[:, q, :].rearrange("p (k t) -> p k t", k=4), ACT.Copy).then_inc(ht_evac, 1)

            modrow_out(0)
            modrow_out(1)
            hT_out(0)
            hT_out(1)
            modrow_out(2)
            hT_out(2)
            hT_out(3)
            for i in range(3, 8):
                modrow_out(i)

            act.wait_ge(pads, 8)

            def conv_in(b):
                act.wait_ge(xbc_ps, b + 1)
                if b >= 2:
                    act.wait_ge(convmid_ready, b - 1)
                ns = 2 if b < BBLK else 1
                A(convin[b % 2][:, 0:ns, 1:257], PS[:, b % 2, 0:256 * ns].rearrange("p (s t) -> p s t", s=ns),
                  ACT.Copy).then_inc(convin_evac, 1)

            def conv_silu(b):
                act.wait_ge(convmid_ready, b + 1)
                if 2 <= b < XBLK:
                    act.wait_ge(tr_ps, b - 1)
                if b < XBLK:
                    A(convout[b % 2], convmid[b % 2], ACT.Silu).then_inc(cv_ready, 1)
                elif b < BBLK:
                    A(BT[:, b - XBLK, :].rearrange("p (s t) -> p s t", s=2), convmid[b % 2], ACT.Silu).then_inc(cv_ready, 1)
                else:
                    A(CT[:, b - BBLK, :], convmid[b % 2][:, 0, :], ACT.Silu).then_inc(cv_ready, 1)

            def rows_out(b):
                act.wait_ge(tr_ps, b + 1)
                src = PS[:, 2 + b % 2, :].rearrange("p (t c) -> p t c", t=4)
                dst = xs[:, :, b * P:(b + 1) * P] if b < XBLK else brow[:, :, b - XBLK, :]
                A(dst, src, ACT.Copy).then_inc(row_evac, 1)

            for b in range(NBLK + 2):
                if b < NBLK:
                    conv_in(b)
                if 1 <= b <= NBLK:
                    conv_silu(b - 1)
                if 2 <= b < BBLK + 2:
                    rows_out(b - 2)
                if b == 4:
                    act.wait_ge(dtabs_ready, 1)
                    step(A(dt_abs, dt_abs, ACT.Exp))
                    step(A(rowv[:, 32:64], rowv[:, 32:64], ACT.Exp))
                    A(dt_abs, dt_abs, ACT.Ln, bias=1.0).then_inc(ln_ready, 1)
                if b == 6:
                    act.wait_ge(cum_ps, 1)
                    A(cum, PS[:, 6, 0:128], ACT.Copy).then_inc(cum_ready, 1)
                    act.wait_ge(cum_ready, 1)
                    A(ecum, cum, ACT.Exp).then_inc(dec_ready, 1)
                    act.wait_ge(dif_ready, 1)
                    A(wst, wst, ACT.Exp).then_inc(dec_ready, 1)
                    A(dec, PS[:, 6, 128:256], ACT.Exp).then_inc(dec_ready, 1)

            def fz_out(j):
                t, c = j % 2, (j // 2) % 2
                act.wait_ge(h_ps, j + 1)
                dst = (frow if j < 4 else zrow)[t][:, c * NQ:(c + 1) * NQ]
                A(dst, PS[:, j % 2, :], ACT.Copy if j < 4 else ACT.Silu).then_inc(h_evac, 1)

            def decay_exp(i):
                act.wait_ge(d_ready, i + 1)
                A(E[i % 2], E[i % 2], ACT.Exp).then_inc(e_ready, 1)

            act.wait_ge(gt_ps, 1)
            A(GT, PS[:, 6, :].rearrange("p (g c l) -> p g c l", g=2, c=2), ACT.Copy).then_inc(gt_evac, 1)
            decay_exp(0)
            fz_out(0)
            act.wait_ge(st_ps, 1)
            A(SFA.rearrange("p (a b) -> p a b", a=2), PS[:, 6:8, :], ACT.Copy).then_inc(st_used, 1)
            fz_out(1)
            decay_exp(1)
            fz_out(2)
            act.wait_ge(st_ps, 3)
            A(SBA.rearrange("p (a b) -> p a b", a=2), PS[:, 6:8, :], ACT.Copy).then_inc(st_used, 1)
            fz_out(3)
            fz_out(4)
            fz_out(5)
            decay_exp(2)
            fz_out(6)
            decay_exp(3)
            fz_out(7)

            def pq_out(g):
                act.wait_ge(pq_ps, g + 1)
                if g:
                    act.wait_ge(yf_ps, g)
                A(PQ, PS[:, 0:2, :], ACT.Copy).then_inc(pq_evac, 1)

            def at_out(g):
                act.wait_ge(at_ps, g + 1)
                A(AT, PS[:, 2:4, :], ACT.Copy).then_inc(at_evac, 1)

            def yf_out(g):
                act.wait_ge(yf_ps, g + 1)
                A(catF[:, 2 * g:2 * g + 2, :], PS[:, 4, :].rearrange("p (b t) -> p b t", b=2), ACT.Copy).then_inc(yf_evac, 1)

            def y_squares(c):
                act.wait_ge(yg_ready, c + 1)
                for g in range(2):
                    A(zrow[c][:, g * NQ:(g + 1) * NQ], yssm[c][:, g * NQ:(g + 1) * NQ], ACT.Square,
                      accum_out=gsq[:, 2 * c + g:2 * c + g + 1]).then_inc(gsq_ready, 1)
                act.wait_ge(gvar_ready, c + 1)
                A(grs[:, 2 * c:2 * c + 2], grs[:, 2 * c:2 * c + 2], ACT.Sqrt).then_inc(gstd_ready, 1)

            for g in range(GROUPS):
                pq_out(g)
                at_out(g)
                yf_out(g)
                if g == 0:
                    y_squares(0)
            y_squares(1)

            def wo_out(n, t):
                act.wait_ge(wo_ps, 2 * n + t + 1)
                ps = PS[:, (n % 2) * 2 + t, :]
                dst = yrow[t][:, n * NQ:(n + 1) * NQ]
                step(A(dst, ps, ACT.Square, accum_out=ysq[:, 4 * t + n:4 * t + n + 1]))
                A(dst, ps, ACT.Copy).then_inc(wo_evac, 1)

            def g_out(v):
                act.wait_ge(g_ps, v + 1)
                if v == 3:
                    act.wait_ge(h2_ready, 2)
                A(Grow[v].rearrange("p (a b) -> p a b", a=4), PS[:, 4:8, :], ACT.Copy).then_inc(g_evac, 1)

            act.wait_ge(yt_ps, 2)
            for n in range(4):
                for t in range(2):
                    wo_out(n, t)
                if n < 3:
                    g_out(n)
            for t in range(2):
                act.wait_ge(yvar_ready, t + 1)
                A(yss[:, t:t + 1], yss[:, t:t + 1], ACT.Sqrt).then_inc(ystd_ready, 1)
                act.wait_ge(x1_ready, t + 1)
                A(yrow[t], xrow[t], ACT.Square, accum_out=xsq[:, t:t + 1]).then_inc(xsq_ready, 1)
                act.wait_ge(xvar_ready, t + 1)
                A(xsq[:, t:t + 1], xsq[:, t:t + 1], ACT.Sqrt).then_inc(xstd_ready, 1)
            for t in range(2):
                for q in range(4):
                    act.wait_ge(h2T_ps, 4 * t + q + 1)
                    A(h2T[:, 4 * q:4 * q + 4, t * P:(t + 1) * P], PS[:, q, :].rearrange("p (k t) -> p k t", k=4),
                      ACT.Copy).then_inc(h2T_evac, 1)

            def scores_out(h):
                for t in range(2):
                    act.wait_ge(sc_ps, 2 * h + t + 1)
                    A(scores[:, t * PH + h, :], PS[:, 6 + t, 0:256], ACT.Copy).then_inc(sc_evac, 1)

            for h in range(PH):
                act.wait_ge(q_ps, h + 1)
                A(qT[:, h, :], PS[:, 4 + h % 2, 0:256], ACT.Copy).then_inc(q_evac, 1)
                if h:
                    scores_out(h - 1)
            scores_out(PH - 1)
            g_out(3)

            def softmax_exp(u, p):
                act.wait_ge(nmax_ready, u + 1)
                A(eexp, top, ACT.Exp, bias=nmax[:, p:p + 1], accum_out=esum[:, p:p + 1]).then_inc(eexp_ready, 1)

            def unit(eng, u, p, blk):
                for g in range(TOPK // GR):
                    eng.wait_ge(u_used, u * TOPK + GR * (g + 1))
                    if g == 0:
                        eng.wait_ge(gate_ready, u + 1)
                    A(gelu[:, p, GR * g:GR * g + GR], dots[:, p, GR * g:GR * g + GR], ACT.Gelu).then_inc(gelu_ready, 1)
                    eng.wait_ge(gelu_ready, u * (TOPK // GR) + g + 1)
                    for j in range(GR * g, GR * g + GR):
                        A(coef[:, p, j:j + 1], gelu[:, p, j:j + 1], ACT.Copy, scale=gate[:, p, j:j + 1]).then_inc(coef_done, 1)
                    eng.wait_ge(coef_done, u * TOPK + GR * (g + 1))
                    for j in range(GR * g, GR * g + GR):
                        if not (type(u) is int and u * TOPK + j < 8):
                            eng.wait_ge(v_used, u * TOPK + (j - 7))
                        A(diag_slot[j % 8], ident, ACT.Copy, scale=coef[:, p, j:j + 1]).then_inc(coef_ready, 1)
                    if g == 0 and not (type(u) is int and u == UNITS - 1):
                        softmax_exp(u + 1, 1 - p)

            def after_block(eng, blk):
                eng.wait_ge(acc_ps, blk + 1)
                A(h2row[blk].rearrange("p (a b) -> p a b", a=4), PS[:, 4 * blk:4 * blk + 4, :], ACT.Square,
                  accum_out=fsq[:, blk:blk + 1]).then_inc(fsq_ready, 1)
                eng.wait_ge(fvar_ready, blk + 1)
                A(fsq[:, blk:blk + 1], fsq[:, blk:blk + 1], ACT.Sqrt).then_inc(fstd_ready, 1)

            softmax_exp(0, 0)
            expert_blocks(act, unit, after_block)

        @block.vector
        def _(dve):
            step = chain(dve, dve_order)
            V = nc.vector
            tt, stt, ts = V.tensor_tensor, V.scalar_tensor_tensor, V.tensor_scalar

            dve.wait_ge(ssq_ready, 4)
            ts(rstd, ssq, 1.0 / D, EPS, ALU.mult, ALU.add).then_inc(var_ready, 1)
            dve.wait_ge(std_ready, 1)
            step(V.reciprocal(rstd, rstd))
            for t in range(4):
                if t >= 2:
                    dve.wait_ge(xt_ps, 4 * (t - 1))
                ts(xn[t % 2], (xrow + ctxrow)[t], rstd[:, t:t + 1], None, ALU.mult).then_inc(xn_ready, 1)

            dve.wait_ge(modT_ps, 8)
            dve.wait_ge(small_in, 16 * N_SMALL)
            bm = cols[:, C_BMOD:C_BMOD + 32].unsqueeze(2).to_broadcast([P, 32, 2])
            step(tt(modc, PS[:, 6, 0:64].rearrange("p (n c) -> p n c", c=2), bm, ALU.add))
            for s in range(2):
                step(V.tensor_copy(shf[:, s, :], modc[:, 0:KT, s]))
                step(stt(scl[:, s, :], modc[:, KT:2 * KT, s], 1.0, cols[:, C_GPM:C_GPM + KT], ALU.add, ALU.mult))
            dve.wait_ge(ht_evac, 16)
            for k in range(KT):
                for s in range(2):
                    ts(hT[:, s, k, :], hT[:, s, k, :], scl[:, s, k:k + 1], shf[:, s, k:k + 1],
                       ALU.mult, ALU.add).then_inc(ht_mod, 1)

            def tail_tiles(n0, n1):
                for n in range(n0, n1):
                    half, k = divmod(n, KT)
                    dve.wait_ge(tail_in[n % TAILS], 16 * (n // TAILS + 1))
                    acc = tail_acc[half % 2]
                    if k == 0:
                        if half >= 2:
                            dve.wait_ge(col_ps, half - 1)
                        ins = ts(acc, tail_slot[n % TAILS], s2[:, k, 0:1], None, ALU.mult)
                    else:
                        ins = stt(acc, tail_slot[n % TAILS], s2[:, k, 0:1], acc, ALU.mult, ALU.add)
                    ins.then_inc(tail_used, 1)
                    dve.wait_ge(tail_used, n + 1)

            def conv(b):
                dve.wait_ge(convin_evac, b + 1)
                if b >= 2:
                    dve.wait_ge(cv_ready, b - 1)
                ns = 2 if b < BBLK else 1
                src, mid = convin[b % 2], convmid[b % 2][:, 0:ns, :]
                w = [cols[:, C_CW + 3 * b + i:C_CW + 3 * b + i + 1] for i in range(3)]
                step(ts(mid, src[:, 0:ns, 1:257], w[1], cols[:, C_CB + b:C_CB + b + 1], ALU.mult, ALU.add))
                step(stt(mid, src[:, 0:ns, 0:256], w[0], mid, ALU.mult, ALU.add))
                stt(mid, src[:, 0:ns, 2:258], w[2], mid, ALU.mult, ALU.add).then_inc(convmid_ready, 1)

            for b in range(NBLK):
                conv(b)
                if b == 4:
                    dve.wait_ge(dt_ps, 1)
                    bias = rowv[:, 0:32].rearrange("p (d h) -> p d h", d=2).unsqueeze(2).to_broadcast([P, 2, 4, HEADS])
                    step(V.tensor_copy(dth(dt_raw), PS[:, 7, 0:128].rearrange("p (t d h) -> p d t h", t=4, d=2)))
                    for d in range(2):
                        step(tt(dth(dt_raw)[:, d], dth(dt_raw)[:, d], rowv[:, 16 * d:16 * d + 16].unsqueeze(1).to_broadcast([P, 4, HEADS]), ALU.add))
                    stt(dt_abs, dt_raw, -1.0, dt_raw, ALU.mult, ALU.min).then_inc(dtabs_ready, 1)
                    dve.wait_ge(ln_ready, 1)
                    step(stt(dt, dt_raw, 0.0, dt_abs, ALU.max, ALU.add))
                    for d in range(2):
                        ea = rowv[:, 32 + 16 * d:48 + 16 * d].unsqueeze(1).to_broadcast([P, 4, HEADS])
                        stt(dth(adt)[:, d], dth(dt)[:, d], -1.0, ea, ALU.mult, ALU.mult).then_inc(adt_ready, 1)
                if b == 6:
                    dve.wait_ge(cum_ready, 1)
                    tt(wst, PS[:, 6, 128:256], cum, ALU.subtract).then_inc(dif_ready, 1)
                    dve.wait_ge(dec_ready, 3)
                    tt(wst, wst, dt, ALU.mult).then_inc(wst_ready, 1)
                tail_tiles(8 * b, 8 * b + 8)

            def h3(a):
                return a.rearrange("p (h l) -> p h l", h=HEADS)

            def r_make(i):
                c, d = divmod(i, 2)
                a = dth(adt)[:, d, c, :].unsqueeze(2).to_broadcast([P, HEADS, P])
                tri = cst[:, K_TU + d, :].unsqueeze(1).to_broadcast([P, HEADS, P])
                tt(h3(R), a, tri, ALU.mult).then_inc(r_ready, 1)

            def d_make(i):
                c, d = divmod(i, 2)
                dve.wait_ge(b_ps, i + 1)
                cm = dth(cum)[:, d, c, :].unsqueeze(2).to_broadcast([P, HEADS, P])
                mask = cst[:, K_MF + d, :].unsqueeze(1).to_broadcast([P, HEADS, P])
                step(tt(h3(E[d]), PS[:, 2:6, :].rearrange("p b (h l) -> p (b h) l", l=P), cm, ALU.subtract))
                stt(h3(E[d]), h3(E[d]), 0.0, mask, ALU.min, ALU.add).then_inc(d_ready, 1)

            def m_make(i):
                c, d = divmod(i, 2)
                dve.wait_ge(e_ready, i + 1)
                dve.wait_ge(gt_evac, 1)
                e4 = E[d].rearrange("p (g h l) -> p g h l", g=2, h=8)
                for g in range(2):
                    gt = GT[:, g, c, :].unsqueeze(1).to_broadcast([P, 8, P])
                    tt(e4[:, g], e4[:, g], gt, ALU.mult).then_inc(m_ready, 1)

            def st_update(n, new, old):
                t, d = STATES[n]
                step(tt(heads(new), heads(old), per_head(dec, d, t), ALU.mult))
                dve.wait_ge(st_ps, n + 1)
                n2 = new.rearrange("p (a b) -> p a b", a=2)
                tt(n2, n2, PS[:, 6:8, :], ALU.add).then_inc(st_used, 1)
                dve.wait_ge(st_used, n + 1)

            def y_add(c):
                dve.wait_ge(y_ps, c + 1)
                dve.wait_ge(y_init, c + 1)
                y2 = yssm[c].rearrange("p (a b) -> p a b", a=2)
                tt(y2, y2, PS[:, 6:8, :], ALU.add).then_inc(y_used, 1)
                dve.wait_ge(y_used, c + 1)

            def o_add(i):
                c, d = divmod(i, 2)
                dve.wait_ge(o_ps, i + 1)
                tt(heads(R[:, 0:1024]), PS[:, 6:8, :].rearrange("p b (h c) -> p (b h) c", c=HD),
                   per_head(ecum, d, c), ALU.mult).then_inc(o_used, 1)
                dve.wait_ge(o_used, i + 1)
                if i == 2:
                    dve.wait_ge(y_init, 2)
                step(tt(yssm[c], yssm[c], R[:, 0:1024], ALU.add))

            def y_gate(c):
                dve.wait_ge(h_evac, 8)
                tt(yssm[c], yssm[c], zrow[c], ALU.mult).then_inc(yg_ready, 1)
                dve.wait_ge(gsq_ready, 2 * c + 2)
                rs = grs[:, 2 * c:2 * c + 2]
                ts(rs, gsq[:, 2 * c:2 * c + 2], 1.0 / NQ, EPS, ALU.mult, ALU.add).then_inc(gvar_ready, 1)
                dve.wait_ge(gstd_ready, c + 1)
                step(V.reciprocal(rs, rs))
                for g in range(2):
                    yg = yssm[c][:, g * NQ:(g + 1) * NQ]
                    ts(yg, yg, rs[:, g:g + 1], None, ALU.mult).then_inc(yn_ready, 1)

            r_make(0)
            d_make(0)
            r_make(1)
            m_make(0)
            dve.wait_ge(col_ps, 6)
            tt(tailc[:, 0:3, :], PS[:, 7, 256:304].rearrange("p (v k) -> p v k", v=3),
                    cols[:, C_BMOD + 32:C_BMOD + 80].rearrange("p (v k) -> p v k", v=3), ALU.add).then_inc(tailc_ready, 1)
            dve.wait_ge(tailc_ready, 1)
            dve.wait_ge(st_used, 1)
            st_update(1, SFB, SFA)
            d_make(1)
            m_make(1)
            dve.wait_ge(st_used, 3)
            st_update(3, SBB, SBA)
            r_make(2)
            y_add(0)
            d_make(2)
            r_make(3)
            st_update(4, SFA, SFB)
            st_update(5, SBA, SBB)
            m_make(2)
            d_make(3)
            m_make(3)
            o_add(0)
            o_add(1)
            y_gate(0)
            o_add(2)
            o_add(3)
            y_add(1)
            y_gate(1)

            def yt_out(c):
                dve.wait_ge(yt_ps, c + 1)
                nw = cols[:, C_NW:C_NW + 8].unsqueeze(2).to_broadcast([P, 8, P])
                src = PS[:, 2 - 2 * c:4 - 2 * c, :].rearrange("p b (k t) -> p (b k) t", t=P)
                tt(catS[:, :, c * P:(c + 1) * P], src, nw, ALU.mult).then_inc(yt_evac, 1)

            yt_out(0)
            yt_out(1)

            def diag_make(v, col):
                if v:
                    dve.wait_ge(g_ps, v)
                tt(diag_all, ident.unsqueeze(1).to_broadcast([P, KT, P]), col.unsqueeze(2).to_broadcast([P, KT, P]),
                   ALU.mult).then_inc(diag_ready, 1)

            g1, c1 = tailc[:, 0, :], tailc[:, 2, :]
            step(tt(g1, g1, cols[:, C_GQM:C_GQM + KT], ALU.mult))
            step(stt(c1, c1, 1.0, cols[:, C_GPF:C_GPF + KT], ALU.add, ALU.mult))
            diag_make(0, g1)
            tail_tiles(96, 112)
            diag_make(1, c1)
            tail_tiles(112, 128)
            diag_make(2, tailc[:, 1, :])

            dve.wait_ge(row_back, 32)
            dve.wait_ge(wo_evac, 8)
            dve.wait_ge(g_evac, 3)
            for t in range(2):
                r = yss[:, t:t + 1]
                step(V.tensor_reduce(r, ysq[:, 4 * t:4 * t + 4], AX.X, ALU.add))
                ts(r, r, 1.0 / D, EPS, ALU.mult, ALU.add).then_inc(yvar_ready, 1)
                dve.wait_ge(ystd_ready, t + 1)
                step(V.reciprocal(r, r))
                step(stt(yrow[t], yrow[t], r, Grow[0], ALU.mult, ALU.mult))
                tt(xrow[t], xrow[t], yrow[t], ALU.add).then_inc(x1_ready, 1)
                dve.wait_ge(xsq_ready, t + 1)
                q = xsq[:, t:t + 1]
                ts(q, q, 1.0 / D, EPS, ALU.mult, ALU.add).then_inc(xvar_ready, 1)
                dve.wait_ge(xstd_ready, t + 1)
                step(V.reciprocal(q, q))
                step(stt(h2row[t], xrow[t], q, Grow[1], ALU.mult, ALU.mult))
                tt(h2row[t], h2row[t], Grow[2], ALU.add).then_inc(h2_ready, 1)
            dve.wait_ge(col_ps, 8)
            dve.wait_ge(g_evac, 3)
            gf = tailc[:, 3, :]
            step(tt(gf, PS[:, 0, 0:16], cols[:, C_BMOD + 80:C_BMOD + 96], ALU.add))
            step(tt(gf, gf, cols[:, C_GQF:C_GQF + KT], ALU.mult))
            diag_make(3, gf)

            def top16(vals, inds, src, cut, go):
                go(V.max(vals[:, 0:8], src))
                go(V.max_index(inds[:, 0:8], vals[:, 0:8], src))
                go(V.match_replace(cut, vals[:, 0:8], src, LOWEST))
                go(V.max(vals[:, 8:16], cut))
                go(V.max_index(inds[:, 8:16], vals[:, 8:16], cut))

            def route(eng, u, p):
                if type(u) is int and u == 0:
                    dve.wait_ge(sc_evac, 16)
                elif not (type(u) is int and u == 1):
                    eng.wait_ge(v_in[NU - 1], u * (16 * TOPK // NU) - 16 * TOPK // NU)
                    eng.wait_ge(coef_ready, u * TOPK - TOPK)
                eng.sem_inc(dve_go, 1)
                V.tensor_copy(s_cur.unsqueeze(1), scores[:, u:u + 1, :] if type(u) is int else scores[:, bass.ds(u, 1), :]).then_inc(route_copy, 1)
                eng.wait_ge(route_copy, u + 1)
                eng.sem_inc(dve_go, 1)
                eng.sem_clear(route_step)
                n = [0]

                def go(ins):
                    n[0] += 1
                    ins.then_inc(route_step, 1)
                    eng.wait_ge(route_step, n[0])

                for a in range(2):
                    top16(v12[:, a, :], i12[:, a, :], s_cur[:, a * NKEYS:(a + 1) * NKEYS], s_cut, go)
                go(V.tensor_copy(i12f, i12))
                c3 = cand.rearrange("p (a b) -> p a b", a=TOPK)
                go(tt(c3, v12[:, 0, :].unsqueeze(2).to_broadcast([P, TOPK, TOPK]),
                      v12[:, 1, :].unsqueeze(1).to_broadcast([P, TOPK, TOPK]), ALU.add))
                top16(top, pos, cand, cand_cut, go)
                ts(nmax[:, p:p + 1], top[:, 0:1], -1.0, None, ALU.mult).then_inc(nmax_ready, 1)
                go(ts(posh[:, 0, :], pos, 4, None, ALU.logical_shift_right))
                go(ts(posh[:, 1, :], pos, TOPK - 1, None, ALU.bitwise_and))
                for a in range(2):
                    go(tt(onehot, posh[:, a, :].unsqueeze(2).to_broadcast([P, TOPK, TOPK]),
                          iota16.unsqueeze(1).to_broadcast([P, TOPK, TOPK]), ALU.is_equal))
                    go(tt(onehot, onehot, i12f[:, a, :].unsqueeze(1).to_broadcast([P, TOPK, TOPK]), ALU.mult))
                    go(V.tensor_reduce(e12[:, a, :], onehot, AX.X, ALU.add))
                stt(idx[:, p, :], e12[:, 0, :], float(NKEYS), e12[:, 1, :], ALU.mult, ALU.add).then_inc(idx_ready, 1)
                eng.wait_ge(eexp_ready, u + 1)
                go(V.reciprocal(esum[:, p:p + 1], esum[:, p:p + 1]))
                ts(gate[:, p, :], eexp, esum[:, p:p + 1], None, ALU.mult).then_inc(gate_ready, 1)
                eng.wait_ge(gate_ready, u + 1)

            def unit(eng, u, p, blk):
                for j in range(TOPK):
                    eng.wait_ge(u_in[j % NU], u * (16 * TOPK // NU) + 16 * (j // NU + 1))
                    V.tensor_tensor_reduce(out=uslot[j % NU], in0=uslot[j % NU], in1=h2row[blk], scale=1.0,
                                           scalar=0.0, op0=ALU.mult, op1=ALU.add,
                                           accum_out=dots[:, p, j:j + 1]).then_inc(u_used, 1)
                    if j == GR - 1 and not (type(u) is int and u == UNITS - 1):
                        route(eng, u + 1, 1 - p)

            def after_block(eng, blk):
                f = fsq[:, blk:blk + 1]
                eng.wait_ge(fsq_ready, blk + 1)
                ts(f, f, 1.0 / D, EPS, ALU.mult, ALU.add).then_inc(fvar_ready, 1)
                eng.wait_ge(fstd_ready, blk + 1)
                step(V.reciprocal(f, f))
                eng.wait_ge(g_evac, 4)
                y4 = h2row[blk].rearrange("p (a b) -> p a b", a=4)
                step(stt(y4, PS[:, 4 * blk:4 * blk + 4, :], f, Grow[3].rearrange("p (a b) -> p a b", a=4), ALU.mult, ALU.mult))
                tt(xrow[blk], xrow[blk], h2row[blk], ALU.add).then_inc(out_ready, 1)

            route(dve, 0, 0)
            expert_blocks(dve, unit, after_block)

        @block.tensor
        def _(pe):
            M = nc.tensor.matmul

            def ring_wait(j):
                pe.wait_ge(ring_in[j % 2], 16 * (j // 2 + 1))

            def row_transposes(t):
                pe.wait_ge(xn_ready, t + 1)
                for q in range(4):
                    if t:
                        pe.wait_ge(ht_evac, 4 * (t - 1) + q + 1)
                    for i in range(4):
                        k = 4 * q + i
                        ins = nc.tensor.transpose(PS[:, q, i * P:(i + 1) * P], xn[t % 2][:, k * P:(k + 1) * P], ident)
                    ins.then_inc(xt_ps, 1)

            def mod_transposes(i):
                pe.wait_ge(modrow_evac, i + 1)
                for j in range(4):
                    n = 2 * (4 * i + j)
                    ins = nc.tensor.transpose(PS[:, 6, n:n + 2], modrow[i % 2][0:2, j * P:(j + 1) * P], ident[0:2, 0:2])
                ins.then_inc(modT_ps, 1)

            pe.wait_ge(small_in, 16 * N_SMALL)
            pe.wait_ge(s2_ready, 2)
            pe.wait_ge(ssq_ready, 4)
            for i in range(8):
                ring_wait(i)
                if i >= 2:
                    pe.wait_ge(modrow_evac, i - 1)
                for k in range(KT):
                    ins = M(PS[0:2, 4 + i % 2, :], s2[:, k, :], wring[i % 2][:, k, :], start=(k == 0), stop=(k == KT - 1))
                ins.then_inc(mod_ps, 1)
                if i:
                    mod_transposes(i - 1)
                if i in (1, 2):
                    row_transposes(2 * i - 2)
                    row_transposes(2 * i - 1)
            mod_transposes(7)

            def xbc(b):
                j = R_XBC + b // 4
                ring_wait(j)
                if b >= 2:
                    pe.wait_ge(convin_evac, b - 1)
                ns = 2 if b < BBLK else 1
                dst = PS[:, b % 2, 0:256 * ns]
                for k in range(KT):
                    if b == 0:
                        pe.wait_ge(ht_mod, 2 * k + 2)
                    rhs = hT[:, :, k, :] if ns == 2 else hT[:, 0, k, :]
                    o = dst.rearrange("p (s t) -> p s t", s=2) if ns == 2 else dst
                    ins = M(o, wring[j % 2][:, k, (b % 4) * P:(b % 4 + 1) * P], rhs, start=(k == 0), stop=(k == KT - 1))
                ins.then_inc(xbc_ps, 1)

            def back_transposes(b):
                pe.wait_ge(cv_ready, b + 1)
                if b >= 2:
                    pe.wait_ge(row_evac, b - 1)
                src = convout[b % 2].rearrange("p s t -> p (s t)") if b < XBLK else BT[:, b - XBLK, :]
                for t in range(4):
                    ins = nc.tensor.transpose(PS[:, 2 + b % 2, t * P:(t + 1) * P], src[:, t * P:(t + 1) * P], ident)
                ins.then_inc(tr_ps, 1)

            def column_sums(half, bank=7, first=256):
                pe.wait_ge(tail_used, KT * (half + 1))
                for j in range(8):
                    n = first + (half % 6) * 8 + j
                    ins = M(PS[:, bank, n:n + 1], tail_acc[half % 2][:, j * P:(j + 1) * P], ones[:, 0:1], start=True, stop=True)
                ins.then_inc(col_ps, 1)

            for b in range(NBLK + 2):
                if b < NBLK:
                    xbc(b)
                if 2 <= b < BBLK + 2:
                    back_transposes(b - 2)
                if b == 3:
                    column_sums(0)
                    pe.wait_ge(late_in, 32)
                    for t in range(4):
                        for k in range(KT):
                            ins = M(PS[:, 7, 32 * t:32 * t + 32], hT[:, t // 2, k, (t % 2) * P:(t % 2 + 1) * P],
                                    dtw[:, k, :], start=(k == 0), stop=(k == KT - 1))
                    ins.then_inc(dt_ps, 1)
                if b == 5:
                    pe.wait_ge(adt_ready, 2)
                    M(PS[:, 6, 0:64], cst[:, K_TU, :], adt[:, 0:64], start=True, stop=True)
                    M(PS[:, 6, 64:128], cst[:, K_TL, :], adt[:, 64:128], start=True, stop=True)
                    M(PS[:, 6, 128:256], ones, adt, start=True, stop=True).then_inc(cum_ps, 1)
                if b in (5, 7, 9, 11):
                    column_sums(b // 2 - 1)

            def half_chunk(j):
                c, t = divmod(j, 2)
                ring_wait(R_FZ + c)
                pe.wait_ge(h_evac, j - 1) if j >= 2 else pe.wait_ge(convin_evac, NBLK)
                for k in range(KT):
                    ins = M(PS[:, j % 2, :], hT[:, 0, k, t * P:(t + 1) * P], wring[(R_FZ + c) % 2][:, k, :],
                            start=(k == 0), stop=(k == KT - 1))
                ins.then_inc(h_ps, 1)

            def cum_rows(i):
                pe.wait_ge(r_ready, i + 1)
                if i:
                    pe.wait_ge(d_ready, i)
                for q in range(4):
                    ins = M(PS[:, 2 + q, :], ones, R[:, q * NQ:(q + 1) * NQ], start=True, stop=True)
                ins.then_inc(b_ps, 1)

            def state(n):
                t, d = STATES[n]
                pe.wait_ge(w_ready, {0: 1, 1: 2, 2: 3, 3: 4, 4: 7, 5: 8}[n])
                pe.wait_ge(st_used, n) if n else pe.wait_ge(gt_evac, 1)
                if n == 0:
                    pe.wait_ge(tailc_ready, 1)
                if n == 4:
                    pe.wait_ge(y_used, 1)
                for g in range(2):
                    w = {4: 0, 5: 1}.get(n, n % 2)
                    ins = M(PS[:, 6 + g, :], brow[:, t, g, :], wx[w][:, g * NQ:(g + 1) * NQ], start=True, stop=True)
                ins.then_inc(st_ps, 1)

            def y_inside(c):
                pe.wait_ge(w_ready, 6 if c == 0 else 10)
                pe.wait_ge(m_ready, 4 * c + 4)
                pe.wait_ge(st_used, 4) if c == 0 else pe.wait_ge(o_used, 4)
                for h in range(HEADS):
                    o = PS[:, 6 + h // 8, (h % 8) * HD:(h % 8 + 1) * HD]
                    for d in range(2):
                        ins = M(o, E[d][:, h * P:(h + 1) * P], wx[d][:, h * HD:(h + 1) * HD], start=(d == 0), stop=(d == 1))
                ins.then_inc(y_ps, 1)

            def y_state(i):
                c, d = divmod(i, 2)
                st = [SFB, SBA, SFA, SBB][i]
                pe.wait_ge(st_used, 6)
                if i:
                    pe.wait_ge(o_used, i)
                for g in range(2):
                    ins = M(PS[:, 6 + g, :], CT[:, g, c * P:(c + 1) * P], st[:, g * NQ:(g + 1) * NQ], start=True, stop=True)
                ins.then_inc(o_ps, 1)

            def pq(g):
                if g:
                    pe.wait_ge(pq_evac, g)
                else:
                    pe.wait_ge(h_evac, 8)
                for b in range(2):
                    for m, k in ((0, 0), (0, 1), (2, 0), (2, 1)):
                        ins = M(PS[:, b, 256 * (m // 2):256 * (m // 2) + 256], dft[:, k, m, b * P:(b + 1) * P],
                                fmix[:, g, k, :], start=(k == 0), stop=(k == 1))
                ins.then_inc(pq_ps, 1)

            def at_make(g):
                pe.wait_ge(at_evac, g) if g else pe.wait_ge(d_ready, 4)
                for b in range(2):
                    ch = 256 * g + P * b
                    for k in range(2):
                        ins = M(PS[:, 2 + b, :].rearrange("p (m n) -> p m n", m=2), frow[k][:, ch:ch + P], dft[:, k, 0:2, :],
                                start=(k == 0), stop=(k == 1))
                ins.then_inc(at_ps, 1)

            def yf_make(g):
                pe.wait_ge(at_evac, g + 1)
                pe.wait_ge(pq_evac, g + 1)
                if g:
                    pe.wait_ge(yf_evac, g)
                for b in range(2):
                    for n, (m, k) in enumerate(((0, 0), (0, 1), (1, 0), (1, 1))):
                        ins = M(PS[:, 4, 256 * b:256 * b + 256], PQ[:, k, 256 * m + P * b:256 * m + P * b + P],
                                AT[:, k, 256 * m:256 * m + 256], start=(n == 0), stop=(n == 3))
                ins.then_inc(yf_ps, 1)

            def y_transposes(c):
                pe.wait_ge(yn_ready, 2 * c + 2)
                pe.wait_ge(at_evac, 4) if c == 0 else pe.wait_ge(pq_evac, 4)
                for k in range(8):
                    ins = nc.tensor.transpose(PS[:, 2 - 2 * c + k // 4, (k % 4) * P:(k % 4 + 1) * P],
                                              yssm[c][:, k * P:(k + 1) * P], ident)
                ins.then_inc(yt_ps, 1)

            pe.wait_ge(cv_ready, NBLK)
            pe.wait_ge(dec_ready, 3)
            pe.wait_ge(row_evac, BBLK)
            for g in range(2):
                for c in range(2):
                    ins = M(PS[:, 6, (2 * g + c) * P:(2 * g + c + 1) * P], BT[:, g, c * P:(c + 1) * P],
                            CT[:, g, c * P:(c + 1) * P], start=True, stop=True)
            ins.then_inc(gt_ps, 1)
            cum_rows(0)
            column_sums(5)
            half_chunk(0)
            state(0)
            half_chunk(1)
            cum_rows(1)
            state(1)
            half_chunk(2)
            state(2)
            half_chunk(3)
            state(3)
            half_chunk(4)
            y_inside(0)
            half_chunk(5)
            cum_rows(2)
            state(4)
            half_chunk(6)
            cum_rows(3)
            state(5)
            half_chunk(7)
            pq(0)
            y_state(0)
            at_make(0)
            y_state(1)
            yf_make(0)
            pq(1)
            y_state(2)
            at_make(1)
            y_state(3)
            yf_make(1)
            pq(2)
            y_inside(1)
            at_make(2)
            yf_make(2)
            pq(3)
            at_make(3)
            yf_make(3)
            y_transposes(0)
            y_transposes(1)

            def row_spread(v):
                pe.wait_ge(diag_ready, v + 1)
                if 0 < v < 3:
                    pe.wait_ge(g_evac, v)
                if v == 3:
                    pe.wait_ge(q_evac, PH)
                    pe.wait_ge(sc_evac, UNITS)
                for q in range(4):
                    ins = M(PS[:, 4 + q, :].rearrange("p (k n) -> p k n", k=4), ones, diag_all[:, 4 * q:4 * q + 4, :],
                            start=True, stop=True)
                ins.then_inc(g_ps, 1)

            pe.wait_ge(yf_evac, GROUPS)
            pe.wait_ge(yt_evac, 2)
            for n in range(4):
                j = R_OUT + n
                ring_wait(j)
                for t in range(2):
                    if n >= 2:
                        pe.wait_ge(wo_evac, 2 * (n - 2) + t + 1)
                    for k in range(KT):
                        cat = catF if k < 8 else catS
                        ins = M(PS[:, (n % 2) * 2 + t, :], cat[:, k % 8, t * P:(t + 1) * P], wring[j % 2][:, k, :],
                                start=(k == 0), stop=(k == KT - 1))
                    ins.then_inc(wo_ps, 1)
                if n < 3:
                    row_spread(n)
            pe.wait_ge(wo_evac, 8)
            pe.wait_ge(g_evac, 3)
            for t in range(2):
                pe.wait_ge(h2_ready, t + 1)
                for q in range(4):
                    if t:
                        pe.wait_ge(h2T_evac, q + 1)
                    for i in range(4):
                        k = 4 * q + i
                        ins = nc.tensor.transpose(PS[:, q, i * P:(i + 1) * P], h2row[t][:, k * P:(k + 1) * P], ident)
                    ins.then_inc(h2T_ps, 1)
            pe.wait_ge(h2T_evac, 8)

            def key_scores(h):
                pe.wait_ge(q_evac, h + 1)
                for t in range(2):
                    if h:
                        pe.wait_ge(sc_evac, 2 * (h - 1) + t + 1)
                    M(PS[:, 6 + t, 0:256], qT[:, h, t * P:(t + 1) * P], keys[:, h, :], start=True, stop=True).then_inc(sc_ps, 1)

            for h in range(PH):
                j = R_QUERY + h // 4
                ring_wait(j)
                if h >= 2:
                    pe.wait_ge(q_evac, h - 1)
                for k in range(KT):
                    ins = M(PS[:, 4 + h % 2, 0:256], wring[j % 2][:, k, (h % 4) * P:(h % 4 + 1) * P], h2T[:, k, :],
                            start=(k == 0), stop=(k == KT - 1))
                ins.then_inc(q_ps, 1)
                if h == 0:
                    pe.wait_ge(keys_in, 32)
                else:
                    key_scores(h - 1)
            key_scores(PH - 1)
            column_sums(6, 0, 0)
            column_sums(7, 0, 0)
            row_spread(3)

            def start_block(blk):
                pe.wait_ge(g_evac, 4)
                for b in range(4):
                    M(PS[:, 4 * blk + b, :], zeros, cst[:, 0:4, :], start=True, stop=False)

            def unit(eng, u, p, blk):
                for j in range(TOPK):
                    eng.wait_ge(v_in[j % NU], u * (16 * TOPK // NU) + 16 * (j // NU + 1))
                    eng.wait_ge(coef_ready, u * TOPK + j + 1)
                    for b in range(4):
                        ins = M(PS[:, 4 * blk + b, :], diag_slot[j % 8], vslot[j % NU][:, b * NQ:(b + 1) * NQ],
                                start=False, stop=False)
                    ins.then_inc(v_used, 1)

            def after_block(eng, blk):
                for b in range(4):
                    ins = M(PS[:, 4 * blk + b, :], zeros, cst[:, 0:4, :], start=False, stop=True)
                ins.then_inc(acc_ps, 1)
                if blk == 0:
                    start_block(1)

            start_block(0)
            expert_blocks(pe, unit, after_block)


def _columns(v):
    import numpy as np
    return np.ascontiguousarray(np.asarray(v).reshape(-1, P).T)


def _layout(i):
    import numpy as np
    f = np.float32
    n = np.arange(P)
    upper = (n[:, None] <= n[None, :])
    cst = np.stack([np.eye(P), np.ones((P, P)), upper, upper.T, np.where(upper, 0, MASKED),
                    np.where(upper.T, 0, MASKED), np.zeros((P, P))], axis=1).astype(f)
    m = np.arange(256)
    angle = 2 * np.pi * ((m[:, None] * m[None, :]) % 256) / 256
    waves = np.stack([np.cos(angle), np.sin(angle), -np.sin(angle)], axis=1) / 16
    dft = waves.reshape(2, P, 3, 256).transpose(1, 0, 2, 3).astype(f)
    conv_w = np.asarray(i["conv_w"][0]).reshape(3, NBLK, P).transpose(2, 1, 0).reshape(P, 3 * NBLK)
    cols = np.concatenate([_columns(i["c"]), _columns(i["c_ctx"]), _columns(i["b_mod"]), _columns(i["g_pre_mix"]),
                           _columns(i["g_post_mix"]), _columns(i["g_pre_ffn"]), _columns(i["g_post_ffn"]),
                           conv_w, _columns(i["conv_b"]), _columns(i["ssm_norm_w"])], axis=1)
    rows = np.concatenate([np.asarray(i[k]).reshape(-1) for k in ("dt_bias_f", "dt_bias_b", "a_log_f", "a_log_b",
                                                                  "d_skip_f", "d_skip_b")] + [np.zeros(32, f)])[None]
    keys = [np.asarray(i[k][0]).transpose(2, 0, 1) for k in ("sub_keys_1", "sub_keys_2")]
    arrays = [i["x"][0], i["ctx"][0], i["w_mod"][0], i["w_in"][0], i["w_fmix"][0], i["w_out"][0], i["w_query"][0],
              keys[0], keys[1], i["expert_u"][0], i["expert_v"][0], cols, rows, cst, dft,
              np.broadcast_to(np.arange(TOPK, dtype=f), (P, TOPK))]
    return [np.ascontiguousarray(a) for a in arrays]


NAMES = ["x", "ctx", "w_mod", "w_in", "w_fmix", "w_out", "w_query", "k1t", "k2t", "expert_u", "expert_v",
         "cols", "rows", "cst", "dft", "iota"]


def kernel(**inputs):
    import concourse.bacc as bacc
    from concourse.bass_utils import run_bass_kernel_spmd

    nc = bacc.Bacc("TRN2", target_bir_lowering=False, num_devices=1)
    arrays, args = {}, []
    for name, a in zip(NAMES, _layout(inputs)):
        arrays[f"in_{name}"] = a
        args.append(nc.dram_tensor(f"in_{name}", a.shape, F32, kind="ExternalInput").ap())
    out = nc.dram_tensor("out", (2 * P, D), F32, kind="ExternalOutput").ap()
    build(nc, *args, out)
    result = run_bass_kernel_spmd(nc, [arrays], core_ids=[0])
    return result.results[0]["out"].reshape(1, 2 * P, D)
```

```python
from contextlib import ExitStack

import concourse.bass as bass
from concourse import mybir

F32 = mybir.dt.float32
U32 = mybir.dt.uint32
ALU = mybir.AluOpType
ACT = mybir.ActivationFunctionType
AX = mybir.AxisListType

P = 128
D = 2048
KT = D // P
NQ = 512
EPS = 1e-6
HEADS, HD = 16, 64
OFF_XBC, OFF_DT = 2048, 3584
XBLK, BBLK, NBLK = 8, 10, 12
GROUPS = 4
PH = 8
TOPK = 16
NKEYS = 128
UNITS = 2 * PH
GR = 4
NU = 8
EARLY = 4
PARTS = 4
TAILS = 4
MASKED = -1e30
LOWEST = -3.0e38

C_C, C_CTX, C_BMOD, C_GPM, C_GQM, C_GPF, C_GQF, C_CW, C_CB, C_NW = 0, 16, 32, 128, 144, 160, 176, 192, 228, 240
NCOL = 248
K_ID, K_ONE, K_TU, K_TL, K_MF, K_MB, K_ZERO = range(7)
NCST = 7
KIB = 256

RING = ([("mod", n) for n in range(8)]
        + [("in", OFF_XBC + n * NQ) for n in range(3)]
        + [("in", n * NQ) for n in range(4)]
        + [("out", n * NQ) for n in range(4)]
        + [("query", n * NQ) for n in range(2)])
R_XBC, R_FZ, R_OUT, R_QUERY = 8, 11, 15, 19

SPREAD_AT = [(0, 0), (0, 1), (1, 1)]
SUMS_AT = {(1, 0): [4, 5], (2, 0): [6], (2, 1): [7]}
QUERIES = [(0, 0, 1), (1, 0, 1), (0, 1, 1), (1, 1, 1)] + [(h, 0, 2) for h in range(2, PH)]
SCORED = [(i, (t0 + t) * PH + h) for i, (h, t0, nt) in enumerate(QUERIES) for t in range(nt)]
EXP_AT = [4, 6]
H2T_AT = 1

STATES = [(2, 0), (3, 0), (3, 1), (2, 1), (0, 0), (1, 1)]


def build(nc, x, ctx_in, w_mod, w_in, w_fmix, w_out, w_query, k1t, k2t, expert_u, expert_v,
          cols_in, rows_in, cst_in, dft_in, iota_in, out):
    with ExitStack() as ctx:
        arena = ctx.enter_context(nc.sbuf_tensor("arena", [P, 207 * KIB], F32))
        PS = ctx.enter_context(nc.psum_tensor("PS", [P, 8, NQ], F32))

        def sem(name):
            return ctx.enter_context(nc.semaphore(name))

        def at(kib, words):
            assert int(kib * KIB) + words <= 207 * KIB
            return arena[:, int(kib * KIB):int(kib * KIB) + words]

        wring = [at(32 * s, 8192).rearrange("p (k n) -> p k n", k=KT) for s in range(2)]
        wmod_slot = [at(32 * s, 8192).rearrange("p (k n) -> p k n", k=4) for s in range(2)]
        xrow = [at(64 + 8 * t, D) for t in range(2)]
        fmix = at(64, 2048).rearrange("p (g b n) -> p g b n", g=GROUPS, b=2)
        dt_raw, dt_abs, dt, adt, cum, wst, ecum, dec = [at(72 + 0.5 * i, 128) for i in range(8)]
        dtpart = at(78, 512)
        dtw = at(76, 512).rearrange("p (k h) -> p k h", k=KT)
        hT = at(80, 8192).rearrange("p (s k t) -> p s k t", s=2, k=KT)
        SFA, SFB, SBA, SBB = [at(96 + 4 * i, 1024) for i in range(4)]
        PQ = at(80, 1024).rearrange("p (b n) -> p b n", b=2)
        AT = at(84, 1024).rearrange("p (b n) -> p b n", b=2)
        catF = at(88, 2048).rearrange("p (k t) -> p k t", k=8)
        tail_slot = [at(112 + 4 * s, 1024) for s in range(TAILS)]
        tail_late = [at(136 + 4 * s, 1024) for s in range(TAILS)]
        tail_acc = [at(k, 1024) for k in (128, 132, 128, 132, 152, 132, 128, 132)]
        R = at(112, 2048)
        E = [at(120 + 8 * d, 2048) for d in range(2)]
        ctxrow = [at(136 + 8 * t, D) for t in range(2)]
        xn = [at(162 + 8 * t, D) for t in range(2)]
        xs = at(136, 4096).rearrange("p (t c) -> p t c", t=4)
        brow = at(152, 1024).rearrange("p (t g n) -> p t g n", t=4, g=2)
        BT = at(156, 1024).rearrange("p (g t) -> p g t", g=2)
        CT = at(160, 512).rearrange("p (g t) -> p g t", g=2)
        frow = [at(162 + 4 * t, 1024) for t in range(2)]
        zrow = [at(170 + 4 * t, 1024) for t in range(2)]
        catS = at(162, 2048).rearrange("p (k t) -> p k t", k=8)
        yrow = [at(136 + 8 * t, D) for t in range(2)]
        h2row = yrow
        Grow = [at(96, D), at(104, D), at(170, D), at(162, D)]
        h2T = [at(80 + 8 * t, D).rearrange("p (k t) -> p k t", k=KT) for t in range(2)]
        h2T_both = at(80, 4096).rearrange("p (t k n) -> p t k n", t=2, k=KT)
        keys = at(152, 2048).rearrange("p (h n) -> p h n", h=PH)
        qT = at(191, 2048).rearrange("p (h t) -> p h t", h=PH)
        scores = at(96, 4096).rearrange("p (u n) -> p u n", u=UNITS)
        uslot = [at(8 * s, D) for s in range(NU)]
        early = [at(k, D) for k in (112, 120, 128, 170)]
        vslot = [at(k, D) for k in (80, 88, 152, 191, 112, 120, 128, 170)]
        dft = at(178, 1536).rearrange("p (b m n) -> p b m n", b=2, m=3)
        diag_slot = [at(178 + 0.5 * s, P) for s in range(8)]
        cst = at(184, NCST * P).rearrange("p (m n) -> p m n", m=NCST)
        misc = at(187.5, 896)
        temp = at(191, 16 * KIB)
        modrow = [temp[:, 512 * i:512 * i + 512] for i in range(2)]
        s2pad = temp[:, 1032:1544].rearrange("p (k c) -> p k c", c=32)
        convin = [temp[:, 516 * i:516 * i + 516].rearrange("p (s t) -> p s t", s=2) for i in range(2)]
        convmid = [temp[:, 1032 + 512 * i:1544 + 512 * i].rearrange("p (s t) -> p s t", s=2) for i in range(2)]
        convout = [temp[:, 2056 + 512 * i:2568 + 512 * i].rearrange("p (s t) -> p s t", s=2) for i in range(2)]
        wx = [temp[:, 0:1024], temp[:, 1024:2048]]
        yssm = [temp[:, 2048:3072], at(156, 1024)]
        GT = temp[:, 3080:3592].rearrange("p (g c l) -> p g c l", g=2, c=2)
        diag_all = temp[:, 0:2048].rearrange("p (k n) -> p k n", k=KT)
        ex = at(199, 7 * KIB)
        s_cur, s_cut = ex[:, 0:256], ex[:, 256:384]
        onehot = ex[:, 384:640].rearrange("p (a b) -> p a b", a=TOPK)
        cand, cand_cut = ex[:, 640:896], ex[:, 896:1152]

        used = [0]

        def small(n, space=misc, dtype=F32):
            a = used[0]
            used[0] += n
            assert used[0] <= 896
            return space.bitcast(dtype)[:, a:a + n] if dtype != F32 else space[:, a:a + n]

        cols = small(NCOL)
        s2 = small(2 * KT).rearrange("p (k c) -> p k c", c=2)
        modc = small(64).rearrange("p (n c) -> p n c", c=2)
        scl = small(2 * KT).rearrange("p (s k) -> p s k", s=2)
        shf = small(2 * KT).rearrange("p (s k) -> p s k", s=2)
        tailc = small(64).rearrange("p (v k) -> p v k", v=4)
        rowv = small(128)
        ssq, rstd = small(4), small(4)
        gsq, grs = small(4), small(4)
        ysq, yss = small(8), small(2)
        xsq, fsq = small(2), small(2)
        nmax = small(2)
        esum = small(2)
        fixed = small(48)
        iota16, sel32 = fixed[:, 0:16], fixed[:, 16:48]
        idx = small(32, dtype=U32).rearrange("p (b k) -> p b k", b=2)
        gate = small(32).rearrange("p (b k) -> p b k", b=2)
        dots = small(32).rearrange("p (b k) -> p b k", b=2)
        gelu = small(32).rearrange("p (b k) -> p b k", b=2)
        coef = small(32).rearrange("p (b k) -> p b k", b=2)
        exv = ex[:, 1152:1408]
        exu = exv.bitcast(U32)
        v12 = exv[:, 0:32].rearrange("p (a k) -> p a k", a=2)
        i12 = exu[:, 32:64].rearrange("p (a k) -> p a k", a=2)
        i12f = exv[:, 64:96].rearrange("p (a k) -> p a k", a=2)
        top, pos = exv[:, 96:112], exu[:, 112:128]
        posh = exu[:, 128:160].rearrange("p (a k) -> p a k", a=2)
        e12 = exv[:, 160:192].rearrange("p (a k) -> p a k", a=2)
        eexp = exv[:, 192:208]

        ident, ones, zeros = cst[:, K_ID, :], cst[:, K_ONE, :], cst[:, K_ZERO, :]

        def dth(v):
            return v.rearrange("p (d t h) -> p d t h", d=2, t=4)

        def per_head(v, d, t):
            return dth(v)[:, d, t, :].unsqueeze(2).to_broadcast([P, HEADS, HD])

        def heads(a):
            return a.rearrange("p (h c) -> p h c", h=HEADS)

        small_in = sem("small_in")
        row_in = [sem(f"row_in{t}") for t in range(4)]
        row_back = sem("row_back")
        dtw_in, late_in = sem("dtw_in"), sem("late_in")
        keys_in = sem("keys_in")
        ring_in = [sem(f"ring_in{s}") for s in range(2)]
        tail_in = [sem(f"tail_in{s}") for s in range(TAILS)]
        act_order, dve_order, pool_order = sem("act_order"), sem("dve_order"), sem("pool_order")
        s2_ready, ssq_ready, var_ready, std_ready = sem("s2_ready"), sem("ssq_ready"), sem("var_ready"), sem("std_ready")
        xn_ready, xt_ps, ht_evac = sem("xn_ready"), sem("xt_ps"), sem("ht_evac")
        mod_ps, modrow_evac, modT_ps, ht_mod = sem("mod_ps"), sem("modrow_evac"), sem("modT_ps"), sem("ht_mod")
        pads, s2pad_ready = sem("pads"), sem("s2pad_ready")
        xbc_ps, convin_evac, convmid_ready, cv_ready = sem("xbc_ps"), sem("convin_evac"), sem("convmid_ready"), sem("cv_ready")
        tr_ps, row_evac = sem("tr_ps"), sem("row_evac")
        tail_used, acc_done, col_ps = sem("tail_used"), sem("acc_done"), sem("col_ps")
        dt_ps, dtabs_ready, ln_ready, adt_ready, cum_ps = sem("dt_ps"), sem("dtabs_ready"), sem("ln_ready"), sem("adt_ready"), sem("cum_ps")
        cum_ready, dif_ready, dec_ready, wst_ready = sem("cum_ready"), sem("dif_ready"), sem("dec_ready"), sem("wst_ready")
        h_ps, h_evac, gt_ps, gt_evac = sem("h_ps"), sem("h_evac"), sem("gt_ps"), sem("gt_evac")
        r_ready, b_ps, d_ready, e_ready, m_ready = sem("r_ready"), sem("b_ps"), sem("d_ready"), sem("e_ready"), sem("m_ready")
        w_ready, st_ps, st_used, y_ps, y_used, y_init = sem("w_ready"), sem("st_ps"), sem("st_used"), sem("y_ps"), sem("y_used"), sem("y_init")
        o_ps, o_used = sem("o_ps"), sem("o_used")
        pq_ps, pq_evac, at_ps, at_evac, yf_ps, yf_evac = sem("pq_ps"), sem("pq_evac"), sem("at_ps"), sem("at_evac"), sem("yf_ps"), sem("yf_evac")
        yg_ready, gsq_ready, gvar_ready, gstd_ready, yn_ready, yt_ps, yt_evac = [sem(n) for n in (
            "yg_ready", "gsq_ready", "gvar_ready", "gstd_ready", "yn_ready", "yt_ps", "yt_evac")]
        wo_ps, wo_evac, diag_ready, g_ps, g_evac = sem("wo_ps"), sem("wo_evac"), sem("diag_ready"), sem("g_ps"), sem("g_evac")
        yvar_ready, ystd_ready, x1_ready, xsq_ready, xvar_ready, xstd_ready, h2_ready = [sem(n) for n in (
            "yvar_ready", "ystd_ready", "x1_ready", "xsq_ready", "xvar_ready", "xstd_ready", "h2_ready")]
        h2T_ps, h2T_evac, q_ps, q_evac, keys_zero, sc_ps, sc_evac = [sem(n) for n in (
            "h2T_ps", "h2T_evac", "q_ps", "q_evac", "keys_zero", "sc_ps", "sc_evac")]
        u_in = [sem(f"u_in{s}") for s in range(NU)]
        v_in = [sem(f"v_in{s}") for s in range(NU)]
        early_in = [sem(f"early_in{s}") for s in range(EARLY)]
        nmax_ready, eexp_ready, idx_ready, gate_ready = sem("nmax_ready"), sem("eexp_ready"), sem("idx_ready"), sem("gate_ready")
        u_used, v_used, coef_ready, pool_go = sem("u_used"), sem("v_used"), sem("coef_ready"), sem("pool_go")
        gelu_ready, coef_done, route_copy, route_step, dve_go = [sem(n) for n in (
            "gelu_ready", "coef_done", "route_copy", "route_step", "dve_go")]
        tailc_ready, dtpart_ready = sem("tailc_ready"), sem("dtpart_ready")
        fsq_ready, fvar_ready, fstd_ready, out_ready, out_done = [sem(n) for n in (
            "fsq_ready", "fvar_ready", "fstd_ready", "out_ready", "out_done")]

        block = ctx.enter_context(nc.Block())

        def chain(eng, order):
            count = [0]

            def step(ins):
                count[0] += 1
                ins.then_inc(order, 1)
                eng.wait_ge(order, count[0])
            return step

        N_SMALL = 4

        def expert_blocks(eng, unit, after_block, late):
            unit(eng, 0, 0, 0)
            unit(eng, 1, 1, 0)
            with eng.Fori(2, PH - 3, 2) as u:
                unit(eng, u, 0, 0)
                unit(eng, u + 1, 1, 0)
            unit(eng, PH - 2, 0, 0)
            unit(eng, PH - 1, 1, 0)
            if not late:
                after_block(eng, 0)
            unit(eng, PH, 0, 1)
            if late:
                after_block(eng, 0)
            with eng.Fori(PH + 1, UNITS - 2, 2) as u:
                unit(eng, u, 1, 1)
                unit(eng, u + 1, 0, 1)
            unit(eng, UNITS - 1, 1, 1)
            after_block(eng, 1)

        @block.sync
        def _(sp):
            wide = {"in": w_in, "out": w_out, "query": w_query}

            def ring_load(j):
                i = j - 2
                if i >= R_OUT:
                    sp.wait_ge(wo_ps, 2 * (i - R_OUT + 1))
                elif i >= R_FZ:
                    sp.wait_ge(h_ps, 2 * (i - R_FZ + 1))
                elif i >= R_XBC:
                    sp.wait_ge(xbc_ps, 4 * (i - R_XBC + 1))
                elif i >= 0:
                    sp.wait_ge(mod_ps, i + 1)
                name, c0 = RING[j]
                if name == "mod":
                    v, q = divmod(c0, 4)
                    src = w_mod[4 * P * q:4 * P * (q + 1), v * D:(v + 1) * D].rearrange("(k p) n -> p k n", p=P)
                    sp.dma_start(wmod_slot[j % 2], src).then_inc(ring_in[j % 2], 16)
                    return
                src = wide[name].rearrange("(k p) n -> p k n", p=P)[:, :, c0:c0 + NQ]
                sp.dma_start(wring[j % 2], src).then_inc(ring_in[j % 2], 16)

            for dst, src in ((cols, cols_in), (cst, cst_in), (rowv, rows_in.to_broadcast([P, 128])), (fixed, iota_in)):
                sp.dma_start(dst, src).then_inc(small_in, 16)
            ring_load(0)
            for t in range(2):
                sp.dma_start(xrow[t], x[t * P:(t + 1) * P, :]).then_inc(row_in[t], 16)
            ring_load(1)
            for t in range(2):
                sp.dma_start(ctxrow[t], ctx_in[t * P:(t + 1) * P, :]).then_inc(row_in[2 + t], 16)
            for j in range(2, R_XBC + 2):
                ring_load(j)
            sp.wait_ge(xn_ready, 2)
            sp.dma_start(dtw, w_in.rearrange("(k p) n -> p k n", p=P)[:, :, OFF_DT:OFF_DT + 32]).then_inc(dtw_in, 16)
            sp.dma_start(fmix, w_fmix.rearrange("g (b p) n -> p g b n", p=P)).then_inc(late_in, 16)
            sp.dma_start(dft, dft_in).then_inc(late_in, 16)
            for j in range(R_XBC + 2, R_OUT + 2):
                ring_load(j)
            sp.wait_ge(pq_ps, GROUPS)
            sp.wait_ge(yg_ready, 2)
            for t in range(2):
                sp.dma_start(xrow[t], x[t * P:(t + 1) * P, :]).then_inc(row_back, 16)
            for j in range(R_OUT + 2, len(RING)):
                ring_load(j)
            sp.wait_ge(keys_zero, 1)
            sp.dma_start(keys[0:64, :, 0:NKEYS], k1t).then_inc(keys_in, 16)
            sp.dma_start(keys[64:P, :, NKEYS:2 * NKEYS], k2t).then_inc(keys_in, 16)
            for i in range(2 * PARTS):
                t, q = divmod(i, PARTS)
                part = slice(q * D // PARTS, (q + 1) * D // PARTS)
                sp.wait_ge(out_ready, i + 1)
                sp.dma_start(out[t * P:(t + 1) * P, part], xrow[t][:, part]).then_inc(out_done, 16)
            sp.wait_ge(out_done, 2 * PARTS * 16)

        @block.gpsimd
        def _(pool):
            for i in range(2):
                for s in range(2):
                    for t in (0, 257):
                        pool.wait_ge(modT_ps, 2)
                        nc.gpsimd.memset(convin[i][:, s, t:t + 1], 0.0).then_inc(pads, 1)

            def tail_load(s, half, k, slots=tail_slot):
                src = w_mod[bass.ds(k * P, P), bass.ds(half * 1024 + 4096, 1024)]
                nc.gpsimd.dma_start(slots[s], src).then_inc(tail_in[s], 16)

            for s in range(TAILS):
                tail_load(s, 0, s)
            for k in range(TAILS, KT):
                pool.wait_ge(tail_used, k - TAILS + 1)
                tail_load(k % TAILS, 0, k)
            with pool.Fori(1, 4) as half:
                for k in range(KT):
                    pool.wait_ge(tail_used, half * KT + (k - TAILS + 1))
                    pool.sem_inc(pool_go, 1)
                    tail_load(k % TAILS, half, k)

            def weigh(n, t, v, d):
                nc.gpsimd.tensor_tensor(heads(wx[n % 2]), heads(xs[:, t, :]), per_head(v, d, t),
                                        ALU.mult).then_inc(w_ready, 1)

            pool.wait_ge(wst_ready, 1)
            pool.wait_ge(row_evac, BBLK)
            pool.wait_ge(tr_ps, BBLK)
            pool.wait_ge(cv_ready, NBLK)
            weigh(0, 2, wst, 0)
            weigh(1, 3, wst, 0)
            skip = [rowv[:, 64 + 16 * i:80 + 16 * i] for i in range(2)]
            nc.gpsimd.tensor_tensor(skip[0], skip[0], skip[1], ALU.add).then_inc(pool_order, 1)
            pool.wait_ge(pool_order, 1)
            pool.wait_ge(gt_ps, 1)
            for c in range(2):
                nc.gpsimd.tensor_tensor(heads(yssm[c]), heads(xs[:, c, :]),
                                        skip[0].unsqueeze(2).to_broadcast([P, HEADS, HD]), ALU.mult).then_inc(y_init, 1)
            pool.wait_ge(st_ps, 1)
            weigh(2, 3, wst, 1)
            pool.wait_ge(st_ps, 2)
            weigh(3, 2, wst, 1)
            pool.wait_ge(st_ps, 3)
            weigh(4, 0, dt, 0)
            pool.wait_ge(st_ps, 4)
            weigh(5, 0, dt, 1)
            pool.wait_ge(y_ps, 1)
            weigh(6, 0, wst, 0)
            weigh(7, 1, wst, 1)
            pool.wait_ge(st_ps, 5)
            weigh(8, 1, dt, 0)
            pool.wait_ge(st_ps, 6)
            weigh(9, 1, dt, 1)

            pool.wait_ge(w_ready, 10)
            for k in range(KT):
                if k >= TAILS:
                    pool.wait_ge(tail_used, 4 * KT + k - TAILS + 1)
                tail_load(k % TAILS, 4, k, tail_late)
            pool.wait_ge(yg_ready, 2)
            pool.wait_ge(y_ps, 2)
            with pool.Fori(5, 8) as half:
                for k in range(KT):
                    pool.wait_ge(tail_used, half * KT + (k - TAILS + 1))
                    pool.sem_inc(pool_go, 1)
                    tail_load(k % TAILS, half, k)
            pool.wait_ge(col_ps, 5)
            pool.wait_ge(yt_ps, 2)
            nc.gpsimd.memset(keys, 0.0).then_inc(keys_zero, 1)

            def gather(table, slot, arrived, p, j):
                nc.gpsimd.indirect_dma_start(slot, None, table, bass.IndirectOffsetOnAxis(ap=idx[:, p, j:j + 1], axis=0),
                                             ).then_inc(arrived, 16)

            pool.wait_ge(col_ps, 8)
            for n in range(2 * TOPK):
                if n % TOPK == 0:
                    pool.wait_ge(idx_ready, n // TOPK + 1)
                if n >= EARLY:
                    pool.wait_ge(u_used, n - EARLY + 1)
                gather(expert_u, early[n % EARLY], early_in[n % EARLY], n // TOPK, n % TOPK)
            pool.wait_ge(sc_ps, UNITS)

            def unit(eng, u, p, blk):
                first, last = type(u) is int and u <= 1, type(u) is int and u == UNITS - 1
                for j in range(TOPK):
                    if first and u == 0 and j == NU - EARLY:
                        eng.wait_ge(u_used, 2 * TOPK)
                    if not (first and u == 0 and j < NU):
                        eng.wait_ge(v_used, u * TOPK + (j - NU + 1))
                        eng.sem_inc(pool_go, 1)
                    gather(expert_v, vslot[j % NU], v_in[j % NU], p, j)
                    if j < NU and not first:
                        eng.wait_ge(u_used, u * TOPK + (j + 1))
                        eng.sem_inc(pool_go, 1)
                        gather(expert_u, uslot[j], u_in[j], p, j + NU)
                    if j >= NU and not (first and u == 0) and not last:
                        if j == NU:
                            eng.wait_ge(idx_ready, u + 2)
                        if not first:
                            eng.wait_ge(u_used, u * TOPK + (j + 1))
                        eng.sem_inc(pool_go, 1)
                        gather(expert_u, uslot[j - NU], u_in[j - NU], 1 - p, j - NU)

            expert_blocks(pool, unit, lambda eng, blk: None, False)

        @block.scalar
        def _(act):
            step = chain(act, act_order)
            A = nc.scalar.activation
            act.wait_ge(small_in, 16 * N_SMALL)
            A(s2[:, :, 0], cols[:, C_C:C_C + KT], ACT.Silu).then_inc(s2_ready, 1)
            A(s2[:, :, 1], cols[:, C_CTX:C_CTX + KT], ACT.Silu).then_inc(s2_ready, 1)
            for t in range(4):
                act.wait_ge(row_in[t], 16)
                if t:
                    act.wait_ge(ssq_ready, t)
                A(PS[:, 0:4, :], (xrow + ctxrow)[t].rearrange("p (a b) -> p a b", a=4), ACT.Square,
                  accum_out=ssq[:, t:t + 1]).then_inc(ssq_ready, 1)
            act.wait_ge(var_ready, 1)
            A(rstd, rstd, ACT.Sqrt).then_inc(std_ready, 1)

            def modrow_out(v):
                act.wait_ge(mod_ps, 4 * v + 4)
                A(modrow[v], PS[:, 4 + v, :], ACT.Copy).then_inc(modrow_evac, 1)

            def hT_out(t):
                for q in range(4):
                    act.wait_ge(xt_ps, 4 * t + q + 1)
                    A(hT[:, t // 2, 4 * q:4 * q + 4, (t % 2) * P:(t % 2 + 1) * P],
                      PS[:, q, :].rearrange("p (k t) -> p k t", k=4), ACT.Copy).then_inc(ht_evac, 1)

            for t in range(4):
                hT_out(t)
            modrow_out(0)
            modrow_out(1)

            act.wait_ge(pads, 8)

            def conv_in(b):
                act.wait_ge(xbc_ps, b + 1)
                if b >= 2:
                    act.wait_ge(convmid_ready, b - 1)
                ns = 2 if b < BBLK else 1
                A(convin[b % 2][:, 0:ns, 1:257], PS[:, b % 2, 0:256 * ns].rearrange("p (s t) -> p s t", s=ns),
                  ACT.Copy).then_inc(convin_evac, 1)

            def conv_silu(b):
                act.wait_ge(convmid_ready, b + 1)
                if 2 <= b < XBLK:
                    act.wait_ge(tr_ps, b - 1)
                if b < XBLK:
                    A(convout[b % 2], convmid[b % 2], ACT.Silu).then_inc(cv_ready, 1)
                elif b < BBLK:
                    A(BT[:, b - XBLK, :].rearrange("p (s t) -> p s t", s=2), convmid[b % 2], ACT.Silu).then_inc(cv_ready, 1)
                else:
                    A(CT[:, b - BBLK, :], convmid[b % 2][:, 0, :], ACT.Silu).then_inc(cv_ready, 1)

            def rows_out(b):
                act.wait_ge(tr_ps, b + 1)
                src = PS[:, 2 + b % 2, :].rearrange("p (t c) -> p t c", t=4)
                dst = xs[:, :, b * P:(b + 1) * P] if b < XBLK else brow[:, :, b - XBLK, :]
                A(dst, src, ACT.Copy).then_inc(row_evac, 1)

            for b in range(NBLK + 2):
                if b < NBLK:
                    conv_in(b)
                if 1 <= b <= NBLK:
                    conv_silu(b - 1)
                if 2 <= b < BBLK + 2:
                    rows_out(b - 2)
                if b == 4:
                    act.wait_ge(dt_ps, 1)
                    A(dtpart, PS[:, 7, :], ACT.Copy).then_inc(dtpart_ready, 1)
                    act.wait_ge(dtabs_ready, 1)
                    step(A(dt_abs, dt_abs, ACT.Exp))
                    step(A(rowv[:, 32:64], rowv[:, 32:64], ACT.Exp))
                    A(dt_abs, dt_abs, ACT.Ln, bias=1.0).then_inc(ln_ready, 1)
                if b == 6:
                    act.wait_ge(cum_ps, 1)
                    A(cum, PS[:, 6, 0:128], ACT.Copy).then_inc(cum_ready, 1)
                    act.wait_ge(cum_ready, 1)
                    A(ecum, cum, ACT.Exp).then_inc(dec_ready, 1)
                    act.wait_ge(dif_ready, 1)
                    A(wst, wst, ACT.Exp).then_inc(dec_ready, 1)
                    A(dec, PS[:, 6, 128:256], ACT.Exp).then_inc(dec_ready, 1)

            def fz_out(j):
                t, c = j % 2, (j // 2) % 2
                act.wait_ge(h_ps, j + 1)
                dst = (frow if j < 4 else zrow)[t][:, c * NQ:(c + 1) * NQ]
                A(dst, PS[:, j % 2, :], ACT.Copy if j < 4 else ACT.Silu).then_inc(h_evac, 1)

            def decay_exp(i):
                act.wait_ge(d_ready, i + 1)
                A(E[i % 2], E[i % 2], ACT.Exp).then_inc(e_ready, 1)

            act.wait_ge(gt_ps, 1)
            A(GT, PS[:, 6, :].rearrange("p (g c l) -> p g c l", g=2, c=2), ACT.Copy).then_inc(gt_evac, 1)
            decay_exp(0)
            fz_out(0)
            act.wait_ge(st_ps, 1)
            A(SFA.rearrange("p (a b) -> p a b", a=2), PS[:, 6:8, :], ACT.Copy).then_inc(st_used, 1)
            fz_out(1)
            decay_exp(1)
            fz_out(2)
            act.wait_ge(st_ps, 3)
            A(SBA.rearrange("p (a b) -> p a b", a=2), PS[:, 6:8, :], ACT.Copy).then_inc(st_used, 1)
            fz_out(3)
            fz_out(4)
            fz_out(5)
            decay_exp(2)
            fz_out(6)
            decay_exp(3)
            fz_out(7)

            def pq_out(g):
                act.wait_ge(pq_ps, g + 1)
                if g:
                    act.wait_ge(yf_ps, g)
                A(PQ, PS[:, 0:2, :], ACT.Copy).then_inc(pq_evac, 1)

            def at_out(g):
                act.wait_ge(at_ps, g + 1)
                A(AT, PS[:, 2:4, :], ACT.Copy).then_inc(at_evac, 1)

            def yf_out(g):
                act.wait_ge(yf_ps, g + 1)
                A(catF[:, 2 * g:2 * g + 2, :], PS[:, 4, :].rearrange("p (b t) -> p b t", b=2), ACT.Copy).then_inc(yf_evac, 1)

            def y_squares(c):
                act.wait_ge(yg_ready, c + 1)
                for g in range(2):
                    A(zrow[c][:, g * NQ:(g + 1) * NQ], yssm[c][:, g * NQ:(g + 1) * NQ], ACT.Square,
                      accum_out=gsq[:, 2 * c + g:2 * c + g + 1]).then_inc(gsq_ready, 1)
                act.wait_ge(gvar_ready, c + 1)
                A(grs[:, 2 * c:2 * c + 2], grs[:, 2 * c:2 * c + 2], ACT.Sqrt).then_inc(gstd_ready, 1)

            for g in range(GROUPS):
                pq_out(g)
                at_out(g)
                yf_out(g)
                if g == 0:
                    y_squares(0)
            y_squares(1)

            def wo_out(n, t):
                act.wait_ge(wo_ps, 2 * n + t + 1)
                ps = PS[:, (n % 2) * 2 + t, :]
                dst = yrow[t][:, n * NQ:(n + 1) * NQ]
                step(A(dst, ps, ACT.Square, accum_out=ysq[:, 4 * t + n:4 * t + n + 1]))
                A(dst, ps, ACT.Copy).then_inc(wo_evac, 1)

            def g_out(v):
                act.wait_ge(g_ps, v + 1)
                A(Grow[v].rearrange("p (a b) -> p a b", a=4), PS[:, 4:8, :], ACT.Copy).then_inc(g_evac, 1)

            def y_norm(t):
                act.wait_ge(yvar_ready, t + 1)
                A(yss[:, t:t + 1], yss[:, t:t + 1], ACT.Sqrt).then_inc(ystd_ready, 1)

            def x1_norm(t):
                act.wait_ge(x1_ready, t + 1)
                A(yrow[t], xrow[t], ACT.Square, accum_out=xsq[:, t:t + 1]).then_inc(xsq_ready, 1)
                act.wait_ge(xvar_ready, t + 1)
                A(xsq[:, t:t + 1], xsq[:, t:t + 1], ACT.Sqrt).then_inc(xstd_ready, 1)

            act.wait_ge(yt_ps, 2)
            act.wait_ge(tail_used, 5 * KT)
            for n in range(4):
                for t in range(2):
                    wo_out(n, t)
                    if (n, t) in SPREAD_AT:
                        g_out(SPREAD_AT.index((n, t)))
                    if (n, t) == (3, 0):
                        y_norm(0)
                        x1_norm(0)
            g_out(3)
            y_norm(1)

            def h2T_out(t):
                for q in range(4):
                    act.wait_ge(h2T_ps, 4 * t + q + 1)
                    A(h2T[t][:, 4 * q:4 * q + 4, :], PS[:, q, :].rearrange("p (k t) -> p k t", k=4),
                      ACT.Copy).then_inc(h2T_evac, 1)

            def scores_out(m):
                act.wait_ge(sc_ps, m + 1)
                if m == 0:
                    act.wait_ge(h2_ready, 2)
                A(scores[:, SCORED[m][1], :], PS[:, 6 + m % 2, 0:256], ACT.Copy).then_inc(sc_evac, 1)

            def softmax_exp(u, p):
                act.wait_ge(nmax_ready, u + 1)
                A(eexp, top, ACT.Exp, bias=nmax[:, p:p + 1], accum_out=esum[:, p:p + 1]).then_inc(eexp_ready, 1)

            h2T_out(0)
            x1_norm(1)
            for i, (h, t0, nt) in enumerate(QUERIES):
                act.wait_ge(q_ps, i + 1)
                A(qT[:, h, t0 * P:(t0 + nt) * P], PS[:, 4 + i % 2, 0:nt * P], ACT.Copy).then_inc(q_evac, 1)
                for m, (q, u) in enumerate(SCORED):
                    if i and q == i - 1 and m or i == 0 and m == 0:
                        scores_out(m)
                if i == H2T_AT:
                    h2T_out(1)
                if i in EXP_AT:
                    softmax_exp(EXP_AT.index(i), EXP_AT.index(i))
            for m, (q, u) in enumerate(SCORED):
                if q == len(QUERIES) - 1:
                    scores_out(m)

            def unit(eng, u, p, blk):
                for g in range(TOPK // GR):
                    eng.wait_ge(u_used, u * TOPK + GR * (g + 1))
                    if g == 0:
                        eng.wait_ge(gate_ready, u + 1)
                    A(gelu[:, p, GR * g:GR * g + GR], dots[:, p, GR * g:GR * g + GR], ACT.Gelu).then_inc(gelu_ready, 1)
                    eng.wait_ge(gelu_ready, u * (TOPK // GR) + g + 1)
                    for j in range(GR * g, GR * g + GR):
                        A(coef[:, p, j:j + 1], gelu[:, p, j:j + 1], ACT.Copy, scale=gate[:, p, j:j + 1]).then_inc(coef_done, 1)
                    eng.wait_ge(coef_done, u * TOPK + GR * (g + 1))
                    for j in range(GR * g, GR * g + GR):
                        if not (type(u) is int and u * TOPK + j < 8):
                            eng.wait_ge(v_used, u * TOPK + (j - 7))
                        A(diag_slot[j % 8], ident, ACT.Copy, scale=coef[:, p, j:j + 1]).then_inc(coef_ready, 1)
                    if g == 1 and not (type(u) is int and u in (0, UNITS - 1)):
                        softmax_exp(u + 1, 1 - p)

            def after_block(eng, blk):
                eng.wait_ge(v_used, (blk + 1) * PH * TOPK)
                A(h2row[blk].rearrange("p (a b) -> p a b", a=4), PS[:, 4 * blk:4 * blk + 4, :], ACT.Square,
                  accum_out=fsq[:, blk:blk + 1]).then_inc(fsq_ready, 1)
                eng.wait_ge(fvar_ready, blk + 1)
                A(fsq[:, blk:blk + 1], fsq[:, blk:blk + 1], ACT.Sqrt).then_inc(fstd_ready, 1)

            expert_blocks(act, unit, after_block, True)

        @block.vector
        def _(dve):
            step = chain(dve, dve_order)
            V = nc.vector
            tt, stt, ts = V.tensor_tensor, V.scalar_tensor_tensor, V.tensor_scalar

            step(V.memset(s2pad, 0.0))
            dve.wait_ge(s2_ready, 2)
            V.tensor_copy(s2pad[:, :, 0:2], s2).then_inc(s2pad_ready, 1)
            dve.wait_ge(ssq_ready, 4)
            ts(rstd, ssq, 1.0 / D, EPS, ALU.mult, ALU.add).then_inc(var_ready, 1)
            dve.wait_ge(std_ready, 1)
            step(V.reciprocal(rstd, rstd))
            for t in range(4):
                if t >= 2:
                    dve.wait_ge(xt_ps, 4 * (t - 1))
                ts(xn[t % 2], (xrow + ctxrow)[t], rstd[:, t:t + 1], None, ALU.mult).then_inc(xn_ready, 1)

            dve.wait_ge(modT_ps, 2)
            dve.wait_ge(small_in, 16 * N_SMALL)
            for v in range(2):
                got = PS[:, 6 + v, :].rearrange("p (i j r) -> p j i r", i=4, j=4)
                bm = cols[:, C_BMOD + KT * v:C_BMOD + KT * (v + 1)].rearrange("p (j i) -> p j i", j=4)
                for c in range(2):
                    step(tt(modc[:, KT * v:KT * (v + 1), c].rearrange("p (j i) -> p j i", j=4), got[:, :, :, c], bm, ALU.add))
            for s in range(2):
                step(V.tensor_copy(shf[:, s, :], modc[:, 0:KT, s]))
                step(stt(scl[:, s, :], modc[:, KT:2 * KT, s], 1.0, cols[:, C_GPM:C_GPM + KT], ALU.add, ALU.mult))
            dve.wait_ge(ht_evac, 16)
            for k in range(KT):
                for s in range(2):
                    ts(hT[:, s, k, :], hT[:, s, k, :], scl[:, s, k:k + 1], shf[:, s, k:k + 1],
                       ALU.mult, ALU.add).then_inc(ht_mod, 1)

            def tail_tiles(n0, n1):
                for n in range(n0, n1):
                    half, k = divmod(n, KT)
                    dve.wait_ge(tail_in[n % TAILS], 16 * (n // TAILS + 1))
                    acc, tile = tail_acc[half], (tail_late if half == 4 else tail_slot)[n % TAILS]
                    if k == 0:
                        if half in (2, 3, 7):
                            dve.wait_ge(col_ps, {2: 1, 3: 2, 7: 6}[half])
                        if half == 4:
                            dve.wait_ge(st_ps, 6)
                        ins = ts(acc, tile, s2[:, k, 0:1], None, ALU.mult)
                    else:
                        ins = stt(acc, tile, s2[:, k, 0:1], acc, ALU.mult, ALU.add)
                    ins.then_inc(tail_used, 1)
                    dve.wait_ge(tail_used, n + 1)

            def conv(b):
                dve.wait_ge(convin_evac, b + 1)
                if b >= 2:
                    dve.wait_ge(cv_ready, b - 1)
                ns = 2 if b < BBLK else 1
                src, mid = convin[b % 2], convmid[b % 2][:, 0:ns, :]
                w = [cols[:, C_CW + 3 * b + i:C_CW + 3 * b + i + 1] for i in range(3)]
                step(ts(mid, src[:, 0:ns, 1:257], w[1], cols[:, C_CB + b:C_CB + b + 1], ALU.mult, ALU.add))
                step(stt(mid, src[:, 0:ns, 0:256], w[0], mid, ALU.mult, ALU.add))
                stt(mid, src[:, 0:ns, 2:258], w[2], mid, ALU.mult, ALU.add).then_inc(convmid_ready, 1)

            for b in range(NBLK):
                conv(b)
                if b == 4:
                    dve.wait_ge(dt_ps, 2)
                    bias = rowv[:, 0:32].rearrange("p (d h) -> p d h", d=2).unsqueeze(2).to_broadcast([P, 2, 4, HEADS])
                    step(V.tensor_copy(dth(dt_raw), PS[:, 6, 0:128].rearrange("p (t d h) -> p d t h", t=4, d=2)))
                    for d in range(2):
                        step(tt(dth(dt_raw)[:, d], dth(dt_raw)[:, d], rowv[:, 16 * d:16 * d + 16].unsqueeze(1).to_broadcast([P, 4, HEADS]), ALU.add))
                    stt(dt_abs, dt_raw, -1.0, dt_raw, ALU.mult, ALU.min).then_inc(dtabs_ready, 1)
                    dve.wait_ge(ln_ready, 1)
                    step(stt(dt, dt_raw, 0.0, dt_abs, ALU.max, ALU.add))
                    for d in range(2):
                        ea = rowv[:, 32 + 16 * d:48 + 16 * d].unsqueeze(1).to_broadcast([P, 4, HEADS])
                        stt(dth(adt)[:, d], dth(dt)[:, d], -1.0, ea, ALU.mult, ALU.mult).then_inc(adt_ready, 1)
                if b == 6:
                    dve.wait_ge(cum_ready, 1)
                    tt(wst, PS[:, 6, 128:256], cum, ALU.subtract).then_inc(dif_ready, 1)
                    dve.wait_ge(dec_ready, 3)
                    tt(wst, wst, dt, ALU.mult).then_inc(wst_ready, 1)
                tail_tiles(64 * b // NBLK, 64 * (b + 1) // NBLK)

            def h3(a):
                return a.rearrange("p (h l) -> p h l", h=HEADS)

            def r_make(i):
                c, d = divmod(i, 2)
                a = dth(adt)[:, d, c, :].unsqueeze(2).to_broadcast([P, HEADS, P])
                tri = cst[:, K_TU + d, :].unsqueeze(1).to_broadcast([P, HEADS, P])
                tt(h3(R), a, tri, ALU.mult).then_inc(r_ready, 1)

            def d_make(i):
                c, d = divmod(i, 2)
                dve.wait_ge(b_ps, i + 1)
                cm = dth(cum)[:, d, c, :].unsqueeze(2).to_broadcast([P, HEADS, P])
                mask = cst[:, K_MF + d, :].unsqueeze(1).to_broadcast([P, HEADS, P])
                step(tt(h3(E[d]), PS[:, 2:6, :].rearrange("p b (h l) -> p (b h) l", l=P), cm, ALU.subtract))
                stt(h3(E[d]), h3(E[d]), 0.0, mask, ALU.min, ALU.add).then_inc(d_ready, 1)

            def m_make(i):
                c, d = divmod(i, 2)
                dve.wait_ge(e_ready, i + 1)
                dve.wait_ge(gt_evac, 1)
                e4 = E[d].rearrange("p (g h l) -> p g h l", g=2, h=8)
                for g in range(2):
                    gt = GT[:, g, c, :].unsqueeze(1).to_broadcast([P, 8, P])
                    tt(e4[:, g], e4[:, g], gt, ALU.mult).then_inc(m_ready, 1)

            def st_update(n, new, old):
                t, d = STATES[n]
                step(tt(heads(new), heads(old), per_head(dec, d, t), ALU.mult))
                dve.wait_ge(st_ps, n + 1)
                n2 = new.rearrange("p (a b) -> p a b", a=2)
                tt(n2, n2, PS[:, 6:8, :], ALU.add).then_inc(st_used, 1)
                dve.wait_ge(st_used, n + 1)

            def y_add(c):
                dve.wait_ge(y_ps, c + 1)
                dve.wait_ge(y_init, c + 1)
                y2 = yssm[c].rearrange("p (a b) -> p a b", a=2)
                tt(y2, y2, PS[:, 6:8, :], ALU.add).then_inc(y_used, 1)
                dve.wait_ge(y_used, c + 1)

            def o_add(i):
                c, d = divmod(i, 2)
                dve.wait_ge(o_ps, i + 1)
                tt(heads(R[:, 0:1024]), PS[:, 6:8, :].rearrange("p b (h c) -> p (b h) c", c=HD),
                   per_head(ecum, d, c), ALU.mult).then_inc(o_used, 1)
                dve.wait_ge(o_used, i + 1)
                if i == 2:
                    dve.wait_ge(y_init, 2)
                step(tt(yssm[c], yssm[c], R[:, 0:1024], ALU.add))

            def y_gate(c):
                dve.wait_ge(h_evac, 8)
                tt(yssm[c], yssm[c], zrow[c], ALU.mult).then_inc(yg_ready, 1)
                if c:
                    tail_tiles(64, 80)
                dve.wait_ge(gsq_ready, 2 * c + 2)
                rs = grs[:, 2 * c:2 * c + 2]
                ts(rs, gsq[:, 2 * c:2 * c + 2], 1.0 / NQ, EPS, ALU.mult, ALU.add).then_inc(gvar_ready, 1)
                dve.wait_ge(gstd_ready, c + 1)
                step(V.reciprocal(rs, rs))
                for g in range(2):
                    yg = yssm[c][:, g * NQ:(g + 1) * NQ]
                    ts(yg, yg, rs[:, g:g + 1], None, ALU.mult).then_inc(yn_ready, 1)

            r_make(0)
            d_make(0)
            r_make(1)
            m_make(0)
            dve.wait_ge(col_ps, 4)
            tt(tailc[:, 0:2, :], PS[:, 7, 256:288].rearrange("p (v k) -> p v k", v=2),
               cols[:, C_BMOD + 32:C_BMOD + 64].rearrange("p (v k) -> p v k", v=2), ALU.add).then_inc(tailc_ready, 1)
            dve.wait_ge(tailc_ready, 1)
            dve.wait_ge(st_used, 1)
            st_update(1, SFB, SFA)
            d_make(1)
            m_make(1)
            dve.wait_ge(st_used, 3)
            st_update(3, SBB, SBA)
            r_make(2)
            y_add(0)
            d_make(2)
            r_make(3)
            st_update(4, SFA, SFB)
            st_update(5, SBA, SBB)
            m_make(2)
            d_make(3)
            m_make(3)
            o_add(0)
            o_add(1)
            y_gate(0)
            o_add(2)
            o_add(3)
            y_add(1)
            y_gate(1)

            def yt_out(c):
                dve.wait_ge(yt_ps, c + 1)
                nw = cols[:, C_NW:C_NW + 8].unsqueeze(2).to_broadcast([P, 8, P])
                src = PS[:, 2 - 2 * c:4 - 2 * c, :].rearrange("p b (k t) -> p (b k) t", t=P)
                tt(catS[:, :, c * P:(c + 1) * P], src, nw, ALU.mult).then_inc(yt_evac, 1)

            yt_out(0)
            yt_out(1)

            def diag_make(v, col):
                if v:
                    dve.wait_ge(g_ps, v)
                tt(diag_all, ident.unsqueeze(1).to_broadcast([P, KT, P]), col.unsqueeze(2).to_broadcast([P, KT, P]),
                   ALU.mult).then_inc(diag_ready, 1)

            g1, c1, gf = tailc[:, 0, :], tailc[:, 2, :], tailc[:, 3, :]
            step(tt(g1, g1, cols[:, C_GQM:C_GQM + KT], ALU.mult))
            diag_make(0, g1)
            tail_tiles(80, 92)
            diag_make(1, tailc[:, 1, :])
            tail_tiles(92, 112)
            dve.wait_ge(col_ps, 6)
            step(tt(c1, PS[:, 4, 0:16], cols[:, C_BMOD + 64:C_BMOD + 80], ALU.add))
            step(stt(c1, c1, 1.0, cols[:, C_GPF:C_GPF + KT], ALU.add, ALU.mult))
            diag_make(2, c1)
            tail_tiles(112, 128)
            dve.wait_ge(col_ps, 8)
            step(tt(gf, PS[:, 4, 16:32], cols[:, C_BMOD + 80:C_BMOD + 96], ALU.add))
            step(tt(gf, gf, cols[:, C_GQF:C_GQF + KT], ALU.mult))

            dve.wait_ge(row_back, 32)
            for t in range(2):
                dve.wait_ge(wo_evac, 7 + t)
                r = yss[:, t:t + 1]
                step(V.tensor_reduce(r, ysq[:, 4 * t:4 * t + 4], AX.X, ALU.add))
                ts(r, r, 1.0 / D, EPS, ALU.mult, ALU.add).then_inc(yvar_ready, 1)
                dve.wait_ge(ystd_ready, t + 1)
                dve.wait_ge(g_evac, 3)
                step(V.reciprocal(r, r))
                step(stt(yrow[t], yrow[t], r, Grow[0], ALU.mult, ALU.mult))
                tt(xrow[t], xrow[t], yrow[t], ALU.add).then_inc(x1_ready, 1)
                if t == 0:
                    diag_make(3, gf)
                dve.wait_ge(xsq_ready, t + 1)
                q = xsq[:, t:t + 1]
                ts(q, q, 1.0 / D, EPS, ALU.mult, ALU.add).then_inc(xvar_ready, 1)
                dve.wait_ge(xstd_ready, t + 1)
                step(V.reciprocal(q, q))
                step(stt(h2row[t], xrow[t], q, Grow[2], ALU.mult, ALU.mult))
                tt(h2row[t], h2row[t], Grow[1], ALU.add).then_inc(h2_ready, 1)

            def top16(vals, inds, src, cut, go):
                go(V.max(vals[:, 0:8], src))
                go(V.max_index(inds[:, 0:8], vals[:, 0:8], src))
                go(V.match_replace(cut, vals[:, 0:8], src, LOWEST))
                go(V.max(vals[:, 8:16], cut))
                go(V.max_index(inds[:, 8:16], vals[:, 8:16], cut))

            def route(eng, u, p):
                eng.wait_ge(sc_evac, [v for _, v in SCORED].index(u) + 1 if type(u) is int and u <= 1 else UNITS)
                if not (type(u) is int and u <= 1):
                    eng.wait_ge(v_in[NU - 1], u * (16 * TOPK // NU) - 16 * TOPK // NU)
                    eng.wait_ge(coef_ready, u * TOPK - TOPK)
                eng.sem_inc(dve_go, 1)
                V.tensor_copy(s_cur.unsqueeze(1), scores[:, u:u + 1, :] if type(u) is int else scores[:, bass.ds(u, 1), :]).then_inc(route_copy, 1)
                eng.wait_ge(route_copy, u + 1)
                eng.sem_inc(dve_go, 1)
                eng.sem_clear(route_step)
                n = [0]

                def go(ins):
                    n[0] += 1
                    ins.then_inc(route_step, 1)
                    eng.wait_ge(route_step, n[0])

                for a in range(2):
                    top16(v12[:, a, :], i12[:, a, :], s_cur[:, a * NKEYS:(a + 1) * NKEYS], s_cut, go)
                go(V.tensor_copy(i12f, i12))
                c3 = cand.rearrange("p (a b) -> p a b", a=TOPK)
                go(tt(c3, v12[:, 0, :].unsqueeze(2).to_broadcast([P, TOPK, TOPK]),
                      v12[:, 1, :].unsqueeze(1).to_broadcast([P, TOPK, TOPK]), ALU.add))
                top16(top, pos, cand, cand_cut, go)
                ts(nmax[:, p:p + 1], top[:, 0:1], -1.0, None, ALU.mult).then_inc(nmax_ready, 1)
                go(ts(posh[:, 0, :], pos, 4, None, ALU.logical_shift_right))
                go(ts(posh[:, 1, :], pos, TOPK - 1, None, ALU.bitwise_and))
                for a in range(2):
                    go(tt(onehot, posh[:, a, :].unsqueeze(2).to_broadcast([P, TOPK, TOPK]),
                          iota16.unsqueeze(1).to_broadcast([P, TOPK, TOPK]), ALU.is_equal))
                    go(tt(onehot, onehot, i12f[:, a, :].unsqueeze(1).to_broadcast([P, TOPK, TOPK]), ALU.mult))
                    go(V.tensor_reduce(e12[:, a, :], onehot, AX.X, ALU.add))
                stt(idx[:, p, :], e12[:, 0, :], float(NKEYS), e12[:, 1, :], ALU.mult, ALU.add).then_inc(idx_ready, 1)
                eng.wait_ge(eexp_ready, u + 1)
                go(V.reciprocal(esum[:, p:p + 1], esum[:, p:p + 1]))
                ts(gate[:, p, :], eexp, esum[:, p:p + 1], None, ALU.mult).then_inc(gate_ready, 1)
                eng.wait_ge(gate_ready, u + 1)

            def unit(eng, u, p, blk):
                first, last = type(u) is int and u <= 1, type(u) is int and u == UNITS - 1
                for j in range(TOPK):
                    if first:
                        n = u * TOPK + j
                        rows = early[n % EARLY]
                        eng.wait_ge(early_in[n % EARLY], 16 * (n // EARLY + 1))
                    else:
                        rows = uslot[j % NU]
                        eng.wait_ge(u_in[j % NU], u * (16 * TOPK // NU) + 16 * (j // NU - 3))
                    V.tensor_tensor_reduce(out=rows, in0=rows, in1=h2row[blk], scale=1.0,
                                           scalar=0.0, op0=ALU.mult, op1=ALU.add,
                                           accum_out=dots[:, p, j:j + 1]).then_inc(u_used, 1)
                    if j == (TOPK - 1 if first else NU - 1) and not last and not (first and u == 0):
                        route(eng, u + 1, 1 - p)

            def after_block(eng, blk):
                f = fsq[:, blk:blk + 1]
                eng.wait_ge(fsq_ready, blk + 1)
                ts(f, f, 1.0 / D, EPS, ALU.mult, ALU.add).then_inc(fvar_ready, 1)
                eng.wait_ge(fstd_ready, blk + 1)
                step(V.reciprocal(f, f))
                eng.wait_ge(g_evac, 4)
                for q in range(PARTS):
                    part = slice(q * D // PARTS, (q + 1) * D // PARTS)
                    step(stt(h2row[blk][:, part], PS[:, 4 * blk + q, :], f, Grow[3][:, part], ALU.mult, ALU.mult))
                    tt(xrow[blk][:, part], xrow[blk][:, part], h2row[blk][:, part], ALU.add).then_inc(out_ready, 1)

            route(dve, 0, 0)
            route(dve, 1, 1)
            expert_blocks(dve, unit, after_block, True)

        @block.tensor
        def _(pe):
            M = nc.tensor.matmul

            def ring_wait(j):
                pe.wait_ge(ring_in[j % 2], 16 * (j // 2 + 1))

            def row_transposes(t):
                pe.wait_ge(xn_ready, t + 1)
                for q in range(4):
                    if t:
                        pe.wait_ge(ht_evac, 4 * (t - 1) + q + 1)
                    for i in range(4):
                        k = 4 * q + i
                        ins = nc.tensor.transpose(PS[:, q, i * P:(i + 1) * P], xn[t % 2][:, k * P:(k + 1) * P], ident)
                    ins.then_inc(xt_ps, 1)

            def mod_transposes(v):
                pe.wait_ge(modrow_evac, v + 1)
                for i in range(4):
                    ins = nc.tensor.transpose(PS[:, 6 + v, i * P:(i + 1) * P], modrow[v][:, i * P:(i + 1) * P], ident)
                ins.then_inc(modT_ps, 1)

            pe.wait_ge(small_in, 16 * N_SMALL)
            pe.wait_ge(s2pad_ready, 1)
            for i in range(8):
                v, q = divmod(i, 4)
                ring_wait(i)
                for kk in range(4):
                    k = 4 * q + kk
                    for j in range(4):
                        ins = M(PS[32 * j:32 * j + 32, 4 + v, :], s2pad[:, k, :], wmod_slot[i % 2][:, kk, j * NQ:(j + 1) * NQ],
                                start=(k == 0), stop=(k == KT - 1), tile_position=(0, 32 * j))
                ins.then_inc(mod_ps, 1)
                if i == 2:
                    pe.wait_ge(ssq_ready, 4)
                    row_transposes(0)
                    row_transposes(1)
                if i == 3:
                    row_transposes(2)
                    row_transposes(3)
                if i == 4:
                    mod_transposes(0)
            mod_transposes(1)

            def xbc(b):
                j = R_XBC + b // 4
                ring_wait(j)
                if b >= 2:
                    pe.wait_ge(convin_evac, b - 1)
                ns = 2 if b < BBLK else 1
                dst = PS[:, b % 2, 0:256 * ns]
                for k in range(KT):
                    if b == 0:
                        pe.wait_ge(ht_mod, 2 * k + 2)
                    rhs = hT[:, :, k, :] if ns == 2 else hT[:, 0, k, :]
                    o = dst.rearrange("p (s t) -> p s t", s=2) if ns == 2 else dst
                    ins = M(o, wring[j % 2][:, k, (b % 4) * P:(b % 4 + 1) * P], rhs, start=(k == 0), stop=(k == KT - 1))
                ins.then_inc(xbc_ps, 1)

            def back_transposes(b):
                pe.wait_ge(cv_ready, b + 1)
                if b >= 2:
                    pe.wait_ge(row_evac, b - 1)
                src = convout[b % 2].rearrange("p s t -> p (s t)") if b < XBLK else BT[:, b - XBLK, :]
                for t in range(4):
                    ins = nc.tensor.transpose(PS[:, 2 + b % 2, t * P:(t + 1) * P], src[:, t * P:(t + 1) * P], ident)
                ins.then_inc(tr_ps, 1)

            def column_sums(half, bank=7, first=256):
                pe.wait_ge(tail_used, KT * (half + 1))
                for j in range(8):
                    n = first + (half % 4) * 8 + j
                    ins = M(PS[:, bank, n:n + 1], tail_acc[half][:, j * P:(j + 1) * P], ones[:, 0:1], start=True, stop=True)
                ins.then_inc(col_ps, 1)

            for b in range(NBLK + 2):
                if b < NBLK:
                    xbc(b)
                if 2 <= b < BBLK + 2:
                    back_transposes(b - 2)
                if b == 3:
                    pe.wait_ge(dtw_in, 16)
                    for i in range(4):
                        for j in range(4):
                            k = 4 * i + j
                            ins = M(PS[32 * j:32 * j + 32, 7, :].rearrange("p (s t) -> p s t", s=2), dtw[:, k, :], hT[:, :, k, :],
                                    start=(i == 0), stop=(i == 3), tile_position=(0, 32 * j))
                    ins.then_inc(dt_ps, 1)
                if b == 4:
                    pe.wait_ge(dtpart_ready, 1)
                    for t in range(4):
                        ins = M(PS[:, 6, 32 * t:32 * t + 32], dtpart[:, t * P:(t + 1) * P], sel32, start=True, stop=True)
                    ins.then_inc(dt_ps, 1)
                if b == 5:
                    pe.wait_ge(adt_ready, 2)
                    M(PS[:, 6, 0:64], cst[:, K_TU, :], adt[:, 0:64], start=True, stop=True)
                    M(PS[:, 6, 64:128], cst[:, K_TL, :], adt[:, 64:128], start=True, stop=True)
                    M(PS[:, 6, 128:256], ones, adt, start=True, stop=True).then_inc(cum_ps, 1)
                if b in (5, 8, 11):
                    column_sums(b // 3 - 1)

            def half_chunk(j):
                c, t = divmod(j, 2)
                ring_wait(R_FZ + c)
                pe.wait_ge(h_evac, j - 1) if j >= 2 else pe.wait_ge(convin_evac, NBLK)
                for k in range(KT):
                    ins = M(PS[:, j % 2, :], hT[:, 0, k, t * P:(t + 1) * P], wring[(R_FZ + c) % 2][:, k, :],
                            start=(k == 0), stop=(k == KT - 1))
                ins.then_inc(h_ps, 1)

            def cum_rows(i):
                pe.wait_ge(r_ready, i + 1)
                if i:
                    pe.wait_ge(d_ready, i)
                for q in range(4):
                    ins = M(PS[:, 2 + q, :], ones, R[:, q * NQ:(q + 1) * NQ], start=True, stop=True)
                ins.then_inc(b_ps, 1)

            def state(n):
                t, d = STATES[n]
                pe.wait_ge(w_ready, {0: 1, 1: 2, 2: 3, 3: 4, 4: 7, 5: 8}[n])
                pe.wait_ge(st_used, n) if n else pe.wait_ge(gt_evac, 1)
                if n == 0:
                    pe.wait_ge(tailc_ready, 1)
                if n == 4:
                    pe.wait_ge(y_used, 1)
                for g in range(2):
                    w = {4: 0, 5: 1}.get(n, n % 2)
                    ins = M(PS[:, 6 + g, :], brow[:, t, g, :], wx[w][:, g * NQ:(g + 1) * NQ], start=True, stop=True)
                ins.then_inc(st_ps, 1)

            def y_inside(c):
                pe.wait_ge(w_ready, 6 if c == 0 else 10)
                pe.wait_ge(m_ready, 4 * c + 4)
                pe.wait_ge(st_used, 4) if c == 0 else pe.wait_ge(o_used, 4)
                for h in range(HEADS):
                    o = PS[:, 6 + h // 8, (h % 8) * HD:(h % 8 + 1) * HD]
                    for d in range(2):
                        ins = M(o, E[d][:, h * P:(h + 1) * P], wx[d][:, h * HD:(h + 1) * HD], start=(d == 0), stop=(d == 1))
                ins.then_inc(y_ps, 1)

            def y_state(i):
                c, d = divmod(i, 2)
                st = [SFB, SBA, SFA, SBB][i]
                pe.wait_ge(st_used, 6)
                if i:
                    pe.wait_ge(o_used, i)
                for g in range(2):
                    ins = M(PS[:, 6 + g, :], CT[:, g, c * P:(c + 1) * P], st[:, g * NQ:(g + 1) * NQ], start=True, stop=True)
                ins.then_inc(o_ps, 1)

            def pq(g):
                if g:
                    pe.wait_ge(pq_evac, g)
                else:
                    pe.wait_ge(late_in, 32)
                    pe.wait_ge(h_evac, 8)
                for b in range(2):
                    for m, k in ((0, 0), (0, 1), (2, 0), (2, 1)):
                        ins = M(PS[:, b, 256 * (m // 2):256 * (m // 2) + 256], dft[:, k, m, b * P:(b + 1) * P],
                                fmix[:, g, k, :], start=(k == 0), stop=(k == 1))
                ins.then_inc(pq_ps, 1)

            def at_make(g):
                pe.wait_ge(at_evac, g) if g else pe.wait_ge(d_ready, 4)
                for b in range(2):
                    ch = 256 * g + P * b
                    for k in range(2):
                        ins = M(PS[:, 2 + b, :].rearrange("p (m n) -> p m n", m=2), frow[k][:, ch:ch + P], dft[:, k, 0:2, :],
                                start=(k == 0), stop=(k == 1))
                ins.then_inc(at_ps, 1)

            def yf_make(g):
                pe.wait_ge(at_evac, g + 1)
                pe.wait_ge(pq_evac, g + 1)
                if g:
                    pe.wait_ge(yf_evac, g)
                for b in range(2):
                    for n, (m, k) in enumerate(((0, 0), (0, 1), (1, 0), (1, 1))):
                        ins = M(PS[:, 4, 256 * b:256 * b + 256], PQ[:, k, 256 * m + P * b:256 * m + P * b + P],
                                AT[:, k, 256 * m:256 * m + 256], start=(n == 0), stop=(n == 3))
                ins.then_inc(yf_ps, 1)

            def y_transposes(c):
                pe.wait_ge(yn_ready, 2 * c + 2)
                pe.wait_ge(at_evac, 4) if c == 0 else pe.wait_ge(pq_evac, 4)
                for k in range(8):
                    ins = nc.tensor.transpose(PS[:, 2 - 2 * c + k // 4, (k % 4) * P:(k % 4 + 1) * P],
                                              yssm[c][:, k * P:(k + 1) * P], ident)
                ins.then_inc(yt_ps, 1)

            pe.wait_ge(cv_ready, NBLK)
            pe.wait_ge(dec_ready, 3)
            pe.wait_ge(row_evac, BBLK)
            for g in range(2):
                for c in range(2):
                    ins = M(PS[:, 6, (2 * g + c) * P:(2 * g + c + 1) * P], BT[:, g, c * P:(c + 1) * P],
                            CT[:, g, c * P:(c + 1) * P], start=True, stop=True)
            ins.then_inc(gt_ps, 1)
            half_chunk(0)
            cum_rows(0)
            column_sums(3)
            state(0)
            half_chunk(1)
            cum_rows(1)
            state(1)
            half_chunk(2)
            state(2)
            half_chunk(3)
            state(3)
            half_chunk(4)
            y_inside(0)
            half_chunk(5)
            cum_rows(2)
            state(4)
            half_chunk(6)
            cum_rows(3)
            state(5)
            half_chunk(7)
            pq(0)
            y_state(0)
            at_make(0)
            y_state(1)
            yf_make(0)
            pq(1)
            y_state(2)
            at_make(1)
            y_state(3)
            yf_make(1)
            pq(2)
            y_inside(1)
            at_make(2)
            yf_make(2)
            pq(3)
            at_make(3)
            yf_make(3)
            y_transposes(0)
            y_transposes(1)

            def row_spread(v):
                pe.wait_ge(diag_ready, v + 1)
                if v:
                    pe.wait_ge(g_evac, v)
                for q in range(4):
                    ins = M(PS[:, 4 + q, :].rearrange("p (k n) -> p k n", k=4), ones, diag_all[:, 4 * q:4 * q + 4, :],
                            start=True, stop=True)
                ins.then_inc(g_ps, 1)

            pe.wait_ge(yf_evac, GROUPS)
            pe.wait_ge(yt_evac, 2)
            for n in range(4):
                j = R_OUT + n
                ring_wait(j)
                for t in range(2):
                    if n >= 2:
                        pe.wait_ge(wo_evac, 2 * (n - 2) + t + 1)
                    for k in range(KT):
                        cat = catF if k < 8 else catS
                        ins = M(PS[:, (n % 2) * 2 + t, :], cat[:, k % 8, t * P:(t + 1) * P], wring[j % 2][:, k, :],
                                start=(k == 0), stop=(k == KT - 1))
                    ins.then_inc(wo_ps, 1)
                    if (n, t) in SPREAD_AT:
                        row_spread(SPREAD_AT.index((n, t)))
                    if (n, t) in SUMS_AT:
                        for half in SUMS_AT[n, t]:
                            pe.wait_ge(g_evac, 2 if half < 6 else 3)
                            column_sums(half, 4, 0)

            def h2_transposes(t):
                pe.wait_ge(h2_ready, t + 1)
                for q in range(4):
                    if t:
                        pe.wait_ge(h2T_evac, q + 1)
                    for i in range(4):
                        k = 4 * q + i
                        ins = nc.tensor.transpose(PS[:, q, i * P:(i + 1) * P], h2row[t][:, k * P:(k + 1) * P], ident)
                    ins.then_inc(h2T_ps, 1)

            def query(i):
                h, t0, nt = QUERIES[i]
                j = R_QUERY + h // 4
                ring_wait(j)
                if i == 0:
                    pe.wait_ge(g_evac, 4)
                if i >= 2:
                    pe.wait_ge(q_evac, i - 1)
                for k in range(KT):
                    if (h, nt) == (0, 1) and k % 4 == 0:
                        pe.wait_ge(h2T_evac, 4 * t0 + k // 4 + 1)
                    w = wring[j % 2][:, k, (h % 4) * P:(h % 4 + 1) * P]
                    rhs = h2T[t0][:, k, :] if nt == 1 else h2T_both[:, :, k, :]
                    o = PS[:, 4 + i % 2, 0:nt * P]
                    ins = M(o if nt == 1 else o.rearrange("p (t n) -> p t n", t=2), w, rhs, start=(k == 0), stop=(k == KT - 1))
                ins.then_inc(q_ps, 1)

            def key_scores(m):
                i, u = SCORED[m]
                t, h = divmod(u, PH)
                pe.wait_ge(q_evac, i + 1)
                if m >= 2:
                    pe.wait_ge(sc_evac, m - 1)
                M(PS[:, 6 + m % 2, 0:256], qT[:, h, t * P:(t + 1) * P], keys[:, h, :], start=True, stop=True).then_inc(sc_ps, 1)

            row_spread(3)
            pe.wait_ge(wo_evac, 8)
            pe.wait_ge(keys_in, 32)
            h2_transposes(0)
            for i in range(len(QUERIES)):
                query(i)
                for m, (q, u) in enumerate(SCORED):
                    if i and q == i - 1 and m or i == 0 and m == 0:
                        key_scores(m)
                if i == H2T_AT:
                    h2_transposes(1)
            for m, (q, u) in enumerate(SCORED):
                if q == len(QUERIES) - 1:
                    key_scores(m)

            def unit(eng, u, p, blk):
                for j in range(TOPK):
                    eng.wait_ge(v_in[j % NU], u * (16 * TOPK // NU) + 16 * (j // NU + 1))
                    eng.wait_ge(coef_ready, u * TOPK + j + 1)
                    if type(u) is int and u == PH and j == 0:
                        eng.wait_ge(sc_evac, UNITS)
                    for b in range(4):
                        ins = M(PS[:, 4 * blk + b, :], diag_slot[j % 8], vslot[j % NU][:, b * NQ:(b + 1) * NQ],
                                start=(type(u) is int and u % PH == 0 and j == 0),
                                stop=(type(u) is int and u % PH == PH - 1 and j == TOPK - 1))
                    ins.then_inc(v_used, 1)

            expert_blocks(pe, unit, lambda eng, blk: None, False)


def _columns(v):
    import numpy as np
    return np.ascontiguousarray(np.asarray(v).reshape(-1, P).T)


def _layout(i):
    import numpy as np
    f = np.float32
    n = np.arange(P)
    upper = (n[:, None] <= n[None, :])
    cst = np.stack([np.eye(P), np.ones((P, P)), upper, upper.T, np.where(upper, 0, MASKED),
                    np.where(upper.T, 0, MASKED), np.zeros((P, P))], axis=1).astype(f)
    m = np.arange(256)
    angle = 2 * np.pi * ((m[:, None] * m[None, :]) % 256) / 256
    waves = np.stack([np.cos(angle), np.sin(angle), -np.sin(angle)], axis=1) / 16
    dft = waves.reshape(2, P, 3, 256).transpose(1, 0, 2, 3).astype(f)
    conv_w = np.asarray(i["conv_w"][0]).reshape(3, NBLK, P).transpose(2, 1, 0).reshape(P, 3 * NBLK)
    cols = np.concatenate([_columns(i["c"]), _columns(i["c_ctx"]), _columns(i["b_mod"]), _columns(i["g_pre_mix"]),
                           _columns(i["g_post_mix"]), _columns(i["g_pre_ffn"]), _columns(i["g_post_ffn"]),
                           conv_w, _columns(i["conv_b"]), _columns(i["ssm_norm_w"])], axis=1)
    rows = np.concatenate([np.asarray(i[k]).reshape(-1) for k in ("dt_bias_f", "dt_bias_b", "a_log_f", "a_log_b",
                                                                  "d_skip_f", "d_skip_b")] + [np.zeros(32, f)])[None]
    keys = [np.asarray(i[k][0]).transpose(2, 0, 1) for k in ("sub_keys_1", "sub_keys_2")]
    arrays = [i["x"][0], i["ctx"][0], i["w_mod"][0], i["w_in"][0], i["w_fmix"][0], i["w_out"][0], i["w_query"][0],
              keys[0], keys[1], i["expert_u"][0], i["expert_v"][0], cols, rows, cst, dft,
              np.concatenate([np.broadcast_to(np.arange(TOPK, dtype=f), (P, TOPK)), (n[:, None] % 32 == np.arange(32)).astype(f)], axis=1)]
    return [np.ascontiguousarray(a) for a in arrays]


NAMES = ["x", "ctx", "w_mod", "w_in", "w_fmix", "w_out", "w_query", "k1t", "k2t", "expert_u", "expert_v",
         "cols", "rows", "cst", "dft", "iota"]


def kernel(**inputs):
    import concourse.bacc as bacc
    from concourse.bass_utils import run_bass_kernel_spmd

    nc = bacc.Bacc("TRN2", target_bir_lowering=False, num_devices=1)
    arrays, args = {}, []
    for name, a in zip(NAMES, _layout(inputs)):
        arrays[f"in_{name}"] = a
        args.append(nc.dram_tensor(f"in_{name}", a.shape, F32, kind="ExternalInput").ap())
    out = nc.dram_tensor("out", (2 * P, D), F32, kind="ExternalOutput").ap()
    build(nc, *args, out)
    result = run_bass_kernel_spmd(nc, [arrays], core_ids=[0])
    return result.results[0]["out"].reshape(1, 2 * P, D)
```

```python
from contextlib import ExitStack

import concourse.bass as bass
from concourse import mybir

F32 = mybir.dt.float32
U32 = mybir.dt.uint32
ALU = mybir.AluOpType
ACT = mybir.ActivationFunctionType
AX = mybir.AxisListType

P = 128
D = 2048
KT = D // P
NQ = 512
EPS = 1e-6
HEADS, HD = 16, 64
OFF_XBC, OFF_DT = 2048, 3584
XBLK, BBLK, NBLK = 8, 10, 12
GROUPS = 4
PH = 8
TOPK = 16
NKEYS = 128
UNITS = 2 * PH
GR = 4
NU = 8
EARLY = 4
PARTS = 4
TAILS, MORE_TAILS = 4, 8
MASKED = -1e30
LOWEST = -3.0e38

C_C, C_CTX, C_BMOD, C_GPM, C_GQM, C_GPF, C_GQF, C_CW, C_CB, C_NW = 0, 16, 32, 128, 144, 160, 176, 192, 228, 240
NCOL = 248
K_ID, K_ONE, K_TU, K_TL, K_MF, K_MB = range(6)
NCST = 6
KIB = 256

RING = ([("scale", n) for n in range(4)]
        + [("in", OFF_XBC + n * NQ) for n in range(3)]
        + [("in", n * NQ) for n in range(4)]
        + [("out", n * NQ) for n in range(4)]
        + [("query", n * NQ) for n in range(2)])
R_XBC, R_FZ, R_OUT, R_QUERY = 4, 7, 11, 15
AHEAD = 4
SHIFTS = 8
SHIFT_AFTER = [3, 2, 3]
PIECES = 4
DT_AT = AHEAD + 1
TAIL_QUOTA = [2, 3, 5, 7, 7, 7, 7, 6, 6, 6, 5, 3]

SPREAD_AT = [(0, 0), (0, 1), (1, 1)]
SUMS_AT = {(1, 0): [4, 5], (2, 0): [6], (3, 0): [7]}
H2T_AT = 4
EXP_AT = [2, 10]

STATES = [(2, 0), (3, 0), (3, 1), (2, 1), (0, 0), (1, 1)]


def build(nc, x, ctx_in, w_mod, w_in, w_fmix, w_out, w_query, k1t, k2t, expert_u, expert_v,
          cols_in, rows_in, cst_in, dft_in, iota_in, out):
    with ExitStack() as ctx:
        arena = ctx.enter_context(nc.sbuf_tensor("arena", [P, 207 * KIB], F32))
        PS = ctx.enter_context(nc.psum_tensor("PS", [P, 8, NQ], F32))

        def sem(name):
            return ctx.enter_context(nc.semaphore(name))

        def at(kib, words):
            assert int(kib * KIB) + words <= 207 * KIB
            return arena[:, int(kib * KIB):int(kib * KIB) + words]

        wring = [at(32 * s, 8192).rearrange("p (k n) -> p k n", k=KT) for s in range(2)]
        wmod_slot = [at(32 * s, 8192).rearrange("p (k n) -> p k n", k=4) for s in range(2)]
        shift_slot = [at(k, 4096).rearrange("p (k n) -> p k n", k=2) for k in (162, 32, 48)]
        xrow = [at(64 + 8 * t, D) for t in range(2)]
        fmix = at(64, 2048).rearrange("p (g b n) -> p g b n", g=GROUPS, b=2)
        dt_raw, dt_abs, dt, adt, cum, wst, ecum, dec = [at(72 + 0.5 * i, 128) for i in range(8)]
        dtpart = betapart = at(78, 512)
        dtw = at(76, 512).rearrange("p (k h) -> p k h", k=KT)
        hT = at(80, 8192).rearrange("p (s k t) -> p s k t", s=2, k=KT)
        SFA, SFB, SBA, SBB = [at(96 + 4 * i, 1024) for i in range(4)]
        PQ = at(80, 1024).rearrange("p (b n) -> p b n", b=2)
        AT = at(84, 1024).rearrange("p (b n) -> p b n", b=2)
        catF = at(88, 2048).rearrange("p (k t) -> p k t", k=8)
        tail_slot = [at(k + 4 * s, 1024) for k in (112, 162) for s in range(TAILS)]
        tail_late = [at(136 + 4 * s, 1024) for s in range(TAILS)]
        tail_acc = [at(k, 1024) for k in (128, 132, 128, 132, 152, 132, 128, 132)]
        R = at(112, 2048)
        E = [at(120 + 8 * d, 2048) for d in range(2)]
        ctxrow = [at(136 + 8 * t, D) for t in range(2)]
        xn = [at(162 + 8 * t, D) for t in range(2)]
        xs = at(136, 4096).rearrange("p (t c) -> p t c", t=4)
        brow = at(152, 1024).rearrange("p (t g n) -> p t g n", t=4, g=2)
        BT = at(156, 1024).rearrange("p (g t) -> p g t", g=2)
        CT = at(160, 512).rearrange("p (g t) -> p g t", g=2)
        frow = [at(162 + 4 * t, 1024) for t in range(2)]
        zrow = [at(170 + 4 * t, 1024) for t in range(2)]
        catS = at(162, 2048).rearrange("p (k t) -> p k t", k=8)
        yrow = [at(136 + 8 * t, D) for t in range(2)]
        h2row = yrow
        Grow = [at(96, D), at(104, D), at(170, D), at(162, D)]
        h2T = [at(80 + 8 * t, D).rearrange("p (k t) -> p k t", k=KT) for t in range(2)]
        keys = at(152, 2048).rearrange("p (h n) -> p h n", h=PH)
        qT = at(162, 2048).rearrange("p (h t) -> p h t", h=PH)
        scores = at(96, 4096).rearrange("p (u n) -> p u n", u=UNITS)
        uslot = [at(8 * s, D) for s in range(NU)]
        early = [at(k, D) for k in (112, 120, 128, 170)]
        vslot = [at(k, D) for k in (80, 88, 152, 191, 112, 120, 128, 170)]
        dft = at(178, 1536).rearrange("p (b m n) -> p b m n", b=2, m=3)
        diag_slot = [at(178 + 0.5 * s, P) for s in range(8)]
        cst = at(184, NCST * P).rearrange("p (m n) -> p m n", m=NCST)
        misc = at(187.5, 896)
        temp = at(191, 16 * KIB)
        modrow = [temp[:, 512 * i:512 * i + 512] for i in range(2)]
        s2pad = temp[:, 1032:1544].rearrange("p (k c) -> p k c", c=32)
        convin = [temp[:, 516 * i:516 * i + 516].rearrange("p (s t) -> p s t", s=2) for i in range(2)]
        convmid = [temp[:, 1032 + 512 * i:1544 + 512 * i].rearrange("p (s t) -> p s t", s=2) for i in range(2)]
        convout = [temp[:, 2056 + 512 * i:2568 + 512 * i].rearrange("p (s t) -> p s t", s=2) for i in range(2)]
        wx = [temp[:, 0:1024], temp[:, 1024:2048]]
        yssm = [temp[:, 2048:3072], at(156, 1024)]
        GT = temp[:, 3080:3592].rearrange("p (g c l) -> p g c l", g=2, c=2)
        diag_all = temp[:, 0:2048].rearrange("p (k n) -> p k n", k=KT)
        ex = at(199, 7 * KIB)
        s_cur, s_cut = ex[:, 0:256], ex[:, 256:384]
        onehot = ex[:, 384:640].rearrange("p (a b) -> p a b", a=TOPK)
        cand, cand_cut = ex[:, 640:896], ex[:, 896:1152]

        used = [0]

        def small(n, space=misc, dtype=F32):
            a = used[0]
            used[0] += n
            assert used[0] <= 896
            return space.bitcast(dtype)[:, a:a + n] if dtype != F32 else space[:, a:a + n]

        cols = small(NCOL)
        s2 = small(2 * KT).rearrange("p (k c) -> p k c", c=2)
        modc = small(64).rearrange("p (n c) -> p n c", c=2)
        scl = small(2 * KT).rearrange("p (s k) -> p s k", s=2)
        shf = small(2 * KT).rearrange("p (s k) -> p s k", s=2)
        tailc = small(64).rearrange("p (v k) -> p v k", v=4)
        rowv = small(128)
        ssq, rstd = small(4), small(4)
        gsq, grs = small(4), small(4)
        ysq, yss = small(8), small(2)
        xsq, fsq, fss = small(2), small(8), small(2)
        warm = small(1)
        nmax = small(2)
        esum = small(2)
        beta = small(2 * AHEAD).rearrange("p (b s) -> p b s", s=2)
        fixed = small(48)
        iota16, sel32 = fixed[:, 0:16], fixed[:, 16:48]
        idx = small(32, dtype=U32).rearrange("p (b k) -> p b k", b=2)
        gate = small(32).rearrange("p (b k) -> p b k", b=2)
        dots = small(32).rearrange("p (b k) -> p b k", b=2)
        gelu = small(32).rearrange("p (b k) -> p b k", b=2)
        coef = small(32).rearrange("p (b k) -> p b k", b=2)
        exv = ex[:, 1152:1408]
        exu = exv.bitcast(U32)
        v12 = exv[:, 0:32].rearrange("p (a k) -> p a k", a=2)
        i12 = exu[:, 32:64].rearrange("p (a k) -> p a k", a=2)
        i12f = exv[:, 64:96].rearrange("p (a k) -> p a k", a=2)
        tops, pos = [exv[:, 96:112], exv[:, 224:240]], exu[:, 112:128]
        posh = exu[:, 128:160].rearrange("p (a k) -> p a k", a=2)
        e12 = exv[:, 160:192].rearrange("p (a k) -> p a k", a=2)
        eexp = [exv[:, 192:208], exv[:, 208:224]]

        ident, ones = cst[:, K_ID, :], cst[:, K_ONE, :]

        def dth(v):
            return v.rearrange("p (d t h) -> p d t h", d=2, t=4)

        def per_head(v, d, t):
            return dth(v)[:, d, t, :].unsqueeze(2).to_broadcast([P, HEADS, HD])

        def heads(a):
            return a.rearrange("p (h c) -> p h c", h=HEADS)

        small_in = sem("small_in")
        row_in = [sem(f"row_in{t}") for t in range(4)]
        mid_in, late_in = sem("mid_in"), sem("late_in")
        keys_in = sem("keys_in")
        ring_in = [sem(f"ring_in{s}") for s in range(2)]
        piece_in = [sem(f"piece_in{i}") for i in range(2)]
        tail_in = [sem(f"tail_in{s}") for s in range(MORE_TAILS)]
        act_order, dve_order, pool_order = sem("act_order"), sem("dve_order"), sem("pool_order")
        s2_ready, ssq_ready, var_ready, std_ready = sem("s2_ready"), sem("ssq_ready"), sem("var_ready"), sem("std_ready")
        xn_ready, xt_ps, ht_evac = sem("xn_ready"), sem("xt_ps"), sem("ht_evac")
        mod_ps, modrow_evac, modT_ps, ht_mod = sem("mod_ps"), sem("modrow_evac"), sem("modT_ps"), sem("ht_mod")
        pads, s2pad_ready = sem("pads"), sem("s2pad_ready")
        shift_in = [sem(f"shift_in{s}") for s in range(3)]
        shf_ready, betapart_ready = sem("shf_ready"), sem("betapart_ready")
        shift_ps, ht_shift, beta_ps, beta_ready = sem("shift_ps"), sem("ht_shift"), sem("beta_ps"), sem("beta_ready")
        xbc_ps, convin_evac, convmid_ready, cv_ready = sem("xbc_ps"), sem("convin_evac"), sem("convmid_ready"), sem("cv_ready")
        tr_ps, row_evac = sem("tr_ps"), sem("row_evac")
        tail_used, col_ps = sem("tail_used"), sem("col_ps")
        dt_ps, dtabs_ready, ln_ready, adt_ready, cum_ps = sem("dt_ps"), sem("dtabs_ready"), sem("ln_ready"), sem("adt_ready"), sem("cum_ps")
        cum_ready, dif_ready, dec_ready, wst_ready = sem("cum_ready"), sem("dif_ready"), sem("dec_ready"), sem("wst_ready")
        h_ps, h_evac, gt_ps, gt_evac = sem("h_ps"), sem("h_evac"), sem("gt_ps"), sem("gt_evac")
        r_ready, b_ps, d_ready, e_ready, m_ready = sem("r_ready"), sem("b_ps"), sem("d_ready"), sem("e_ready"), sem("m_ready")
        w_ready, st_ps, st_used, y_ps, y_used, y_init = sem("w_ready"), sem("st_ps"), sem("st_used"), sem("y_ps"), sem("y_used"), sem("y_init")
        o_ps, o_used = sem("o_ps"), sem("o_used")
        pq_ps, pq_evac, at_ps, at_evac, yf_ps, yf_evac = sem("pq_ps"), sem("pq_evac"), sem("at_ps"), sem("at_evac"), sem("yf_ps"), sem("yf_evac")
        yg_ready, gsq_ready, gvar_ready, gstd_ready, yn_ready, yt_ps, yt_evac = [sem(n) for n in (
            "yg_ready", "gsq_ready", "gvar_ready", "gstd_ready", "yn_ready", "yt_ps", "yt_evac")]
        wo_ps, wo_evac, diag_ready, g_ps, g_evac = sem("wo_ps"), sem("wo_evac"), sem("diag_ready"), sem("g_ps"), sem("g_evac")
        yvar_ready, ystd_ready, x1_ready, xsq_ready, xvar_ready, xstd_ready, h2_ready = [sem(n) for n in (
            "yvar_ready", "ystd_ready", "x1_ready", "xsq_ready", "xvar_ready", "xstd_ready", "h2_ready")]
        h2T_ps, h2T_evac, q_ps, q_evac, keys_zero, sc_ps, sc_evac = [sem(n) for n in (
            "h2T_ps", "h2T_evac", "q_ps", "q_evac", "keys_zero", "sc_ps", "sc_evac")]
        u_in = [sem(f"u_in{s}") for s in range(NU)]
        v_in = [sem(f"v_in{s}") for s in range(NU)]
        early_in = [sem(f"early_in{s}") for s in range(EARLY)]
        nmax_ready, eexp_ready, idx_ready, gate_ready = sem("nmax_ready"), sem("eexp_ready"), sem("idx_ready"), sem("gate_ready")
        u_used, v_used, coef_ready, pool_go = sem("u_used"), sem("v_used"), sem("coef_ready"), sem("pool_go")
        gelu_ready, esum_ready, coef_done, route_copy, route_step, dve_go = [sem(n) for n in (
            "gelu_ready", "esum_ready", "coef_done", "route_copy", "route_step", "dve_go")]
        tailc_ready, dtpart_ready = sem("tailc_ready"), sem("dtpart_ready")
        acc_ps, fsq_ready, out_ready, out_done = [sem(n) for n in (
            "acc_ps", "fsq_ready", "out_ready", "out_done")]

        block = ctx.enter_context(nc.Block())

        def chain(eng, order):
            count = [0]

            def step(ins):
                count[0] += 1
                ins.then_inc(order, 1)
                eng.wait_ge(order, count[0])
            return step

        N_SMALL = 4

        def expert_blocks(eng, unit, after_block, late):
            unit(eng, 0, 0, 0)
            unit(eng, 1, 1, 0)
            with eng.Fori(2, PH - 3, 2) as u:
                unit(eng, u, 0, 0)
                unit(eng, u + 1, 1, 0)
            unit(eng, PH - 2, 0, 0)
            unit(eng, PH - 1, 1, 0)
            if not late:
                after_block(eng, 0)
            unit(eng, PH, 0, 1)
            if late:
                after_block(eng, 0)
            with eng.Fori(PH + 1, UNITS - 2, 2) as u:
                unit(eng, u, 1, 1)
                unit(eng, u + 1, 0, 1)
            unit(eng, UNITS - 1, 1, 1)
            after_block(eng, 1)

        @block.sync
        def _(sp):
            wide = {"in": w_in, "out": w_out, "query": w_query}

            def ring_load(j):
                i = j - 2
                if i >= R_OUT:
                    sp.wait_ge(wo_ps, 2 * (i - R_OUT + 1))
                elif i >= R_FZ:
                    sp.wait_ge(h_ps, 2 * (i - R_FZ + 1))
                elif i == R_XBC:
                    sp.wait_ge(beta_ps, 1)
                elif i > R_XBC:
                    sp.wait_ge(xbc_ps, 4 * (i - R_XBC + 1))
                elif j == R_XBC + 1:
                    sp.wait_ge(shift_ps, SHIFTS)
                elif i >= 0:
                    sp.wait_ge(mod_ps, i + 1)
                name, c0 = RING[j]
                if name == "scale":
                    src = w_mod[4 * P * c0:4 * P * (c0 + 1), D:2 * D].rearrange("(k p) n -> p k n", p=P)
                    for i in range(PIECES):
                        sp.dma_start(wmod_slot[j % 2][:, i:i + 1], src[:, i:i + 1]).then_inc(ring_in[j % 2], 16)
                    return
                src = wide[name].rearrange("(k p) n -> p k n", p=P)[:, :, c0:c0 + NQ]
                for i in range(PIECES):
                    part = slice(i * KT // PIECES, (i + 1) * KT // PIECES)
                    sp.dma_start(wring[j % 2][:, part], src[:, part]).then_inc(piece_in[min(i, 1)] if j == R_XBC else ring_in[j % 2], 16)

            for dst, src in ((cols, cols_in), (cst[:, 0:K_TU], cst_in[:, 0:K_TU]), (rowv, rows_in.to_broadcast([P, 128])), (fixed, iota_in)):
                sp.dma_start(dst, src).then_inc(small_in, 16)
            ring_load(0)
            for t in range(2):
                sp.dma_start(xrow[t], x[t * P:(t + 1) * P, :]).then_inc(row_in[t], 16)
            ring_load(1)
            for t in range(2):
                sp.dma_start(ctxrow[t], ctx_in[t * P:(t + 1) * P, :]).then_inc(row_in[2 + t], 16)
            for j in range(2, R_XBC + 1):
                ring_load(j)
            for i in range(SHIFTS):
                if i >= 3:
                    sp.wait_ge(shift_ps, i - 2)
                elif i:
                    sp.wait_ge(mod_ps, 4)
                else:
                    sp.wait_ge(xt_ps, 16)
                src = w_mod[2 * P * i:2 * P * (i + 1), 0:D].rearrange("(k p) n -> p k n", p=P)
                sp.dma_start(shift_slot[i % 3], src).then_inc(shift_in[i % 3], 16)
            ring_load(R_XBC + 1)
            sp.wait_ge(xn_ready, 2)
            sp.dma_start(dtw, w_in.rearrange("(k p) n -> p k n", p=P)[:, :, OFF_DT:OFF_DT + 32]).then_inc(mid_in, 16)
            sp.dma_start(cst[:, K_TU:], cst_in[:, K_TU:]).then_inc(mid_in, 16)
            for j in range(R_XBC + 2, R_FZ + 1):
                ring_load(j)
            sp.dma_start(fmix, w_fmix.rearrange("g (b p) n -> p g b n", p=P)).then_inc(late_in, 16)
            sp.dma_start(dft, dft_in).then_inc(late_in, 16)
            for j in range(R_FZ + 1, R_OUT + 2):
                ring_load(j)
            sp.wait_ge(pq_ps, GROUPS)
            sp.wait_ge(yg_ready, 2)
            for t in range(2):
                sp.dma_start(xrow[t], x[t * P:(t + 1) * P, :]).then_inc(row_in[t], 16)
            for j in range(R_OUT + 2, R_QUERY):
                ring_load(j)
            sp.wait_ge(keys_zero, 1)
            sp.dma_start(keys[0:64, :, 0:NKEYS], k1t).then_inc(keys_in, 16)
            sp.dma_start(keys[64:P, :, NKEYS:2 * NKEYS], k2t).then_inc(keys_in, 16)
            for j in range(R_QUERY, len(RING)):
                ring_load(j)
            for i in range(2 * PARTS):
                t, q = divmod(i, PARTS)
                part = slice(q * D // PARTS, (q + 1) * D // PARTS)
                sp.wait_ge(out_ready, i + 1)
                sp.dma_start(out[t * P:(t + 1) * P, part], xrow[t][:, part]).then_inc(out_done, 16)
            sp.wait_ge(out_done, 2 * PARTS * 16)

        @block.gpsimd
        def _(pool):
            for i in range(2):
                for s in range(2):
                    for t in (0, 257):
                        pool.wait_ge(modT_ps, 2)
                        nc.gpsimd.memset(convin[i][:, s, t:t + 1], 0.0).then_inc(pads, 1)

            def tail_load(s, half, k, slots=tail_slot):
                src = w_mod[bass.ds(k * P, P), bass.ds(half * 1024 + 4096, 1024)]
                nc.gpsimd.dma_start(slots[s], src).then_inc(tail_in[s], 16)

            pool.wait_ge(shift_ps, SHIFTS)
            for k in range(KT):
                if k >= MORE_TAILS:
                    pool.wait_ge(tail_used, k - MORE_TAILS + 1)
                tail_load(k % MORE_TAILS, 0, k)
            with pool.Fori(1, 4) as half:
                for k in range(KT):
                    pool.wait_ge(tail_used, half * KT + (k - MORE_TAILS + 1))
                    pool.sem_inc(pool_go, 1)
                    tail_load(k % MORE_TAILS, half, k)

            def weigh(n, t, v, d):
                nc.gpsimd.tensor_tensor(heads(wx[n % 2]), heads(xs[:, t, :]), per_head(v, d, t),
                                        ALU.mult).then_inc(w_ready, 1)

            pool.wait_ge(wst_ready, 1)
            pool.wait_ge(row_evac, BBLK)
            pool.wait_ge(tr_ps, BBLK)
            pool.wait_ge(cv_ready, NBLK)
            weigh(0, 2, wst, 0)
            weigh(1, 3, wst, 0)
            skip = [rowv[:, 64 + 16 * i:80 + 16 * i] for i in range(2)]
            nc.gpsimd.tensor_tensor(skip[0], skip[0], skip[1], ALU.add).then_inc(pool_order, 1)
            pool.wait_ge(pool_order, 1)
            pool.wait_ge(gt_ps, 1)
            for c in range(2):
                nc.gpsimd.tensor_tensor(heads(yssm[c]), heads(xs[:, c, :]),
                                        skip[0].unsqueeze(2).to_broadcast([P, HEADS, HD]), ALU.mult).then_inc(y_init, 1)
            pool.wait_ge(st_ps, 1)
            weigh(2, 3, wst, 1)
            pool.wait_ge(st_ps, 2)
            weigh(3, 2, wst, 1)
            pool.wait_ge(st_ps, 3)
            weigh(4, 0, dt, 0)
            pool.wait_ge(st_ps, 4)
            weigh(5, 0, dt, 1)
            pool.wait_ge(y_ps, 1)
            weigh(6, 0, wst, 0)
            weigh(7, 1, wst, 1)
            pool.wait_ge(st_ps, 5)
            weigh(8, 1, dt, 0)
            pool.wait_ge(st_ps, 6)
            weigh(9, 1, dt, 1)

            pool.wait_ge(w_ready, 10)
            for k in range(KT):
                if k >= TAILS:
                    pool.wait_ge(tail_used, 4 * KT + k - TAILS + 1)
                tail_load(k % TAILS, 4, k, tail_late)
            pool.wait_ge(yg_ready, 2)
            pool.wait_ge(y_ps, 2)
            with pool.Fori(5, 8) as half:
                for k in range(KT):
                    pool.wait_ge(tail_used, half * KT + (k - TAILS + 1))
                    pool.sem_inc(pool_go, 1)
                    tail_load(k % TAILS, half, k)
            pool.wait_ge(col_ps, 5)
            pool.wait_ge(yt_ps, 2)
            nc.gpsimd.memset(keys, 0.0).then_inc(keys_zero, 1)

            def gather(table, slot, arrived, p, j):
                nc.gpsimd.indirect_dma_start(slot, None, table, bass.IndirectOffsetOnAxis(ap=idx[:, p, j:j + 1], axis=0),
                                             ).then_inc(arrived, 16)

            pool.wait_ge(col_ps, 8)
            for n in range(2 * TOPK):
                if n % TOPK == 0:
                    pool.wait_ge(idx_ready, n // TOPK + 1)
                if n == EARLY - 1:
                    pool.wait_ge(h2_ready, 2)
                if n >= EARLY:
                    pool.wait_ge(u_used, n - EARLY + 1)
                gather(expert_u, early[n % EARLY], early_in[n % EARLY], n // TOPK, n % TOPK)
            pool.wait_ge(g_ps, 4)

            def unit(eng, u, p, blk):
                first, last = type(u) is int and u <= 1, type(u) is int and u == UNITS - 1
                for j in range(TOPK):
                    if first and u == 0 and j == NU - EARLY:
                        eng.wait_ge(u_used, 2 * TOPK)
                    if not (first and u == 0 and j < NU):
                        eng.wait_ge(v_used, u * TOPK + (j - NU + 1))
                        eng.sem_inc(pool_go, 1)
                    gather(expert_v, vslot[j % NU], v_in[j % NU], p, j)
                    if j < NU and not first:
                        eng.wait_ge(u_used, u * TOPK + (j + 1))
                        eng.sem_inc(pool_go, 1)
                        gather(expert_u, uslot[j], u_in[j], p, j + NU)
                    if j >= NU and not (first and u == 0) and not last:
                        if j == NU:
                            eng.wait_ge(idx_ready, u + 2)
                        if not first:
                            eng.wait_ge(u_used, u * TOPK + (j + 1))
                        eng.sem_inc(pool_go, 1)
                        gather(expert_u, uslot[j - NU], u_in[j - NU], 1 - p, j - NU)

            expert_blocks(pool, unit, lambda eng, blk: None, False)

        @block.scalar
        def _(act):
            step = chain(act, act_order)
            A = nc.scalar.activation
            act.wait_ge(small_in, 16 * N_SMALL)
            A(s2[:, :, 0], cols[:, C_C:C_C + KT], ACT.Silu).then_inc(s2_ready, 1)
            A(s2[:, :, 1], cols[:, C_CTX:C_CTX + KT], ACT.Silu).then_inc(s2_ready, 1)
            for t in range(4):
                act.wait_ge(row_in[t], 16)
                if t:
                    act.wait_ge(ssq_ready, t)
                A(PS[:, 0:4, :], (xrow + ctxrow)[t].rearrange("p (a b) -> p a b", a=4), ACT.Square,
                  accum_out=ssq[:, t:t + 1]).then_inc(ssq_ready, 1)
            act.wait_ge(var_ready, 1)
            A(rstd, rstd, ACT.Sqrt).then_inc(std_ready, 1)

            def modrow_out(v):
                act.wait_ge(mod_ps, 4) if v else act.wait_ge(shift_ps, SHIFTS)
                A(modrow[v], PS[:, 4 + v, :], ACT.Copy).then_inc(modrow_evac, 1)

            def hT_out(t):
                for q in range(4):
                    act.wait_ge(xt_ps, 4 * t + q + 1)
                    A(hT[:, t // 2, 4 * q:4 * q + 4, (t % 2) * P:(t % 2 + 1) * P],
                      PS[:, q, :].rearrange("p (k t) -> p k t", k=4), ACT.Copy).then_inc(ht_evac, 1)

            for t in range(4):
                hT_out(t)
            modrow_out(1)
            modrow_out(0)
            act.wait_ge(beta_ps, 1)
            A(betapart, PS[:, 5, :], ACT.Copy).then_inc(betapart_ready, 1)

            act.wait_ge(pads, 8)

            def conv_in(b):
                act.wait_ge(xbc_ps, b + 1)
                if b >= 2:
                    act.wait_ge(convmid_ready, b - 1)
                ns = 2 if b < BBLK else 1
                if b < AHEAD:
                    act.wait_ge(beta_ready, 1)
                    for s in range(2):
                        ins = A(convin[b % 2][:, s, 1:257], PS[:, b, 256 * s:256 * s + 256], ACT.Identity, bias=beta[:, b, s:s + 1])
                    ins.then_inc(convin_evac, 1)
                    return
                A(convin[b % 2][:, 0:ns, 1:257], PS[:, b % 2, 0:256 * ns].rearrange("p (s t) -> p s t", s=ns),
                  ACT.Copy).then_inc(convin_evac, 1)

            def conv_silu(b):
                act.wait_ge(convmid_ready, b + 1)
                if 2 <= b < XBLK:
                    act.wait_ge(tr_ps, b - 1)
                if b < XBLK:
                    A(convout[b % 2], convmid[b % 2], ACT.Silu).then_inc(cv_ready, 1)
                elif b < BBLK:
                    A(BT[:, b - XBLK, :].rearrange("p (s t) -> p s t", s=2), convmid[b % 2], ACT.Silu).then_inc(cv_ready, 1)
                else:
                    A(CT[:, b - BBLK, :], convmid[b % 2][:, 0, :], ACT.Silu).then_inc(cv_ready, 1)

            def rows_out(b):
                act.wait_ge(tr_ps, b + 1)
                src = PS[:, 2 + b % 2, :].rearrange("p (t c) -> p t c", t=4)
                dst = xs[:, :, b * P:(b + 1) * P] if b < XBLK else brow[:, :, b - XBLK, :]
                A(dst, src, ACT.Copy).then_inc(row_evac, 1)

            for b in range(NBLK + 2):
                if b < NBLK:
                    conv_in(b)
                if 1 <= b <= NBLK:
                    conv_silu(b - 1)
                if 2 <= b < BBLK + 2:
                    rows_out(b - 2)
                if b == DT_AT + 1:
                    act.wait_ge(dt_ps, 1)
                    A(dtpart, PS[:, 7, :], ACT.Copy).then_inc(dtpart_ready, 1)
                    act.wait_ge(dtabs_ready, 1)
                    step(A(dt_abs, dt_abs, ACT.Exp))
                    step(A(rowv[:, 32:64], rowv[:, 32:64], ACT.Exp))
                    A(dt_abs, dt_abs, ACT.Ln, bias=1.0).then_inc(ln_ready, 1)
                if b == DT_AT + 3:
                    act.wait_ge(cum_ps, 1)
                    A(cum, PS[:, 6, 0:128], ACT.Copy).then_inc(cum_ready, 1)
                    act.wait_ge(cum_ready, 1)
                    A(ecum, cum, ACT.Exp).then_inc(dec_ready, 1)
                    act.wait_ge(dif_ready, 1)
                    A(wst, wst, ACT.Exp).then_inc(dec_ready, 1)
                    A(dec, PS[:, 6, 128:256], ACT.Exp).then_inc(dec_ready, 1)

            def fz_out(j):
                t, c = j % 2, (j // 2) % 2
                if j == 0:
                    act.wait_ge(tail_used, 4 * KT)
                act.wait_ge(h_ps, j + 1)
                dst = (frow if j < 4 else zrow)[t][:, c * NQ:(c + 1) * NQ]
                A(dst, PS[:, j % 2, :], ACT.Copy if j < 4 else ACT.Silu).then_inc(h_evac, 1)

            def decay_exp(i):
                act.wait_ge(d_ready, i + 1)
                A(E[i % 2], E[i % 2], ACT.Exp).then_inc(e_ready, 1)

            act.wait_ge(gt_ps, 1)
            A(GT, PS[:, 6, :].rearrange("p (g c l) -> p g c l", g=2, c=2), ACT.Copy).then_inc(gt_evac, 1)
            decay_exp(0)
            fz_out(0)
            act.wait_ge(st_ps, 1)
            A(SFA.rearrange("p (a b) -> p a b", a=2), PS[:, 6:8, :], ACT.Copy).then_inc(st_used, 1)
            fz_out(1)
            decay_exp(1)
            fz_out(2)
            act.wait_ge(st_ps, 3)
            A(SBA.rearrange("p (a b) -> p a b", a=2), PS[:, 6:8, :], ACT.Copy).then_inc(st_used, 1)
            fz_out(3)
            fz_out(4)
            fz_out(5)
            decay_exp(2)
            fz_out(6)
            decay_exp(3)
            fz_out(7)

            def pq_out(g):
                act.wait_ge(pq_ps, g + 1)
                if g:
                    act.wait_ge(yf_ps, g)
                A(PQ, PS[:, 0:2, :], ACT.Copy).then_inc(pq_evac, 1)

            def at_out(g):
                act.wait_ge(at_ps, g + 1)
                A(AT, PS[:, 2:4, :], ACT.Copy).then_inc(at_evac, 1)

            def yf_out(g):
                act.wait_ge(yf_ps, g + 1)
                A(catF[:, 2 * g:2 * g + 2, :], PS[:, 4, :].rearrange("p (b t) -> p b t", b=2), ACT.Copy).then_inc(yf_evac, 1)

            def y_squares(c):
                act.wait_ge(yg_ready, c + 1)
                for g in range(2):
                    A(zrow[c][:, g * NQ:(g + 1) * NQ], yssm[c][:, g * NQ:(g + 1) * NQ], ACT.Square,
                      accum_out=gsq[:, 2 * c + g:2 * c + g + 1]).then_inc(gsq_ready, 1)
                act.wait_ge(gvar_ready, c + 1)
                A(grs[:, 2 * c:2 * c + 2], grs[:, 2 * c:2 * c + 2], ACT.Sqrt).then_inc(gstd_ready, 1)

            for g in range(GROUPS):
                pq_out(g)
                at_out(g)
                yf_out(g)
                if g == 0:
                    y_squares(0)
            y_squares(1)

            def wo_out(n, t):
                act.wait_ge(wo_ps, 2 * n + t + 1)
                ps = PS[:, (n % 2) * 2 + t, :]
                dst = yrow[t][:, n * NQ:(n + 1) * NQ]
                step(A(dst, ps, ACT.Square, accum_out=ysq[:, 4 * t + n:4 * t + n + 1]))
                A(dst, ps, ACT.Copy).then_inc(wo_evac, 1)

            def g_out(v):
                act.wait_ge(g_ps, v + 1)
                A(Grow[v].rearrange("p (a b) -> p a b", a=4), PS[:, 4:8, :], ACT.Copy).then_inc(g_evac, 1)

            def y_norm(t):
                act.wait_ge(yvar_ready, t + 1)
                A(yss[:, t:t + 1], yss[:, t:t + 1], ACT.Sqrt).then_inc(ystd_ready, 1)

            def x1_norm(t):
                act.wait_ge(x1_ready, t + 1)
                A(yrow[t], xrow[t], ACT.Square, accum_out=xsq[:, t:t + 1]).then_inc(xsq_ready, 1)
                act.wait_ge(xvar_ready, t + 1)
                A(xsq[:, t:t + 1], xsq[:, t:t + 1], ACT.Sqrt).then_inc(xstd_ready, 1)

            act.wait_ge(yt_ps, 2)
            act.wait_ge(tail_used, 5 * KT)
            for n in range(4):
                for t in range(2):
                    wo_out(n, t)
                    if (n, t) in SPREAD_AT:
                        g_out(SPREAD_AT.index((n, t)))
                    if (n, t) == (3, 0):
                        y_norm(0)
                        x1_norm(0)
            y_norm(1)

            def h2T_out(t):
                for q in range(4):
                    act.wait_ge(h2T_ps, 4 * t + q + 1)
                    A(h2T[t][:, 4 * q:4 * q + 4, :], PS[:, q, :].rearrange("p (k t) -> p k t", k=4),
                      ACT.Copy).then_inc(h2T_evac, 1)

            def scores_out(u):
                act.wait_ge(sc_ps, u + 1)
                if u % PH == 0:
                    act.wait_ge(h2_ready, 2) if u else act.wait_ge(x1_ready, 2)
                A(scores[:, u, :], PS[:, 6 + u % 2, 0:256], ACT.Copy).then_inc(sc_evac, 1)

            def softmax_exp(u, p):
                act.wait_ge(nmax_ready, u + 1)
                A(eexp[p], tops[p], ACT.Exp, bias=nmax[:, p:p + 1], accum_out=esum[:, p:p + 1]).then_inc(eexp_ready, 1)

            h2T_out(0)
            for u in range(UNITS):
                t, h = divmod(u, PH)
                act.wait_ge(q_ps, u + 1)
                A(qT[:, h, t * P:(t + 1) * P], PS[:, 4 + u % 2, 0:P], ACT.Copy).then_inc(q_evac, 1)
                if u != 1:
                    scores_out(max(u - 1, 0))
                if u == 0:
                    x1_norm(1)
                if u == H2T_AT:
                    h2T_out(1)
                if u in EXP_AT:
                    softmax_exp(EXP_AT.index(u), EXP_AT.index(u))
            scores_out(UNITS - 1)
            g_out(3)

            def unit(eng, u, p, blk):
                for g in range(TOPK // GR):
                    eng.wait_ge(u_used, u * TOPK + GR * (g + 1))
                    if g == 0:
                        eng.wait_ge(gate_ready, u + 1)
                    A(gelu[:, p, GR * g:GR * g + GR], dots[:, p, GR * g:GR * g + GR], ACT.Gelu).then_inc(gelu_ready, 1)
                    eng.wait_ge(gelu_ready, u * (TOPK // GR) + g + 1)
                    for j in range(GR * g, GR * g + GR):
                        A(coef[:, p, j:j + 1], gelu[:, p, j:j + 1], ACT.Copy, scale=gate[:, p, j:j + 1]).then_inc(coef_done, 1)
                    eng.wait_ge(coef_done, u * TOPK + GR * (g + 1))
                    for j in range(GR * g, GR * g + GR):
                        if not (type(u) is int and u * TOPK + j < 8):
                            eng.wait_ge(v_used, u * TOPK + (j - 7))
                        A(diag_slot[j % 8], ident, ACT.Copy, scale=coef[:, p, j:j + 1]).then_inc(coef_ready, 1)
                    if g == 1 and not (type(u) is int and u in (0, UNITS - 1)):
                        softmax_exp(u + 1, 1 - p)

            def after_block(eng, blk):
                if blk:
                    A(warm, ones[:, 0:1], ACT.Sqrt)
                for b in range(4):
                    eng.wait_ge(acc_ps, 3 * blk + b + 1) if b < 3 else eng.wait_ge(v_used, (blk + 1) * PH * TOPK)
                    A(h2row[blk][:, b * NQ:(b + 1) * NQ], PS[:, 4 * blk + b, :], ACT.Square,
                      accum_out=fsq[:, 4 * blk + b:4 * blk + b + 1]).then_inc(fsq_ready, 1)
                eng.wait_ge(xvar_ready, blk + 3)
                A(fss[:, blk:blk + 1], fss[:, blk:blk + 1], ACT.Sqrt).then_inc(xstd_ready, 1)

            expert_blocks(act, unit, after_block, True)

        @block.vector
        def _(dve):
            step = chain(dve, dve_order)
            V = nc.vector
            tt, stt, ts = V.tensor_tensor, V.scalar_tensor_tensor, V.tensor_scalar

            step(V.memset(s2pad, 0.0))
            dve.wait_ge(s2_ready, 2)
            V.tensor_copy(s2pad[:, :, 0:2], s2).then_inc(s2pad_ready, 1)
            dve.wait_ge(ssq_ready, 4)
            ts(rstd, ssq, 1.0 / D, EPS, ALU.mult, ALU.add).then_inc(var_ready, 1)
            dve.wait_ge(std_ready, 1)
            step(V.reciprocal(rstd, rstd))
            for t in range(4):
                if t >= 2:
                    dve.wait_ge(xt_ps, 4 * (t - 1))
                ts(xn[t % 2], (xrow + ctxrow)[t], rstd[:, t:t + 1], None, ALU.mult).then_inc(xn_ready, 1)

            dve.wait_ge(small_in, 16 * N_SMALL)

            def mod_column(v):
                got = PS[:, 6 + v, :].rearrange("p (i j r) -> p j i r", i=4, j=4)
                bm = cols[:, C_BMOD + KT * v:C_BMOD + KT * (v + 1)].rearrange("p (j i) -> p j i", j=4)
                for c in range(2):
                    step(tt(modc[:, KT * v:KT * (v + 1), c].rearrange("p (j i) -> p j i", j=4), got[:, :, :, c], bm, ALU.add))

            dve.wait_ge(modT_ps, 1)
            mod_column(1)
            for s in range(2):
                step(stt(scl[:, s, :], modc[:, KT:2 * KT, s], 1.0, cols[:, C_GPM:C_GPM + KT], ALU.add, ALU.mult))
            dve.wait_ge(ht_evac, 16)
            for k in range(KT):
                for s in range(2):
                    ts(hT[:, s, k, :], hT[:, s, k, :], scl[:, s, k:k + 1], None, ALU.mult).then_inc(ht_mod, 1)
            dve.wait_ge(modT_ps, 2)
            mod_column(0)
            for s in range(2):
                V.tensor_copy(shf[:, s, :], modc[:, 0:KT, s]).then_inc(shf_ready, 1)
                V.tensor_copy(s2pad[:, :, s], modc[:, 0:KT, s]).then_inc(shf_ready, 1)

            def tail_tiles(n0, n1):
                for n in range(n0, n1):
                    half, k = divmod(n, KT)
                    slot = n % (MORE_TAILS if half < 4 else TAILS)
                    times = n // MORE_TAILS + 1 if half < 4 else 4 * KT // MORE_TAILS + (n - 4 * KT) // TAILS + 1
                    dve.wait_ge(tail_in[slot], 16 * times)
                    acc, tile = tail_acc[half], (tail_late if half == 4 else tail_slot)[slot]
                    if k == 0:
                        if half in (2, 3, 7):
                            dve.wait_ge(col_ps, {2: 1, 3: 2, 7: 6}[half])
                        if half == 4:
                            dve.wait_ge(st_ps, 6)
                        ins = ts(acc, tile, s2[:, k, 0:1], None, ALU.mult)
                    else:
                        ins = stt(acc, tile, s2[:, k, 0:1], acc, ALU.mult, ALU.add)
                    ins.then_inc(tail_used, 1)
                    dve.wait_ge(tail_used, n + 1)

            def conv(b):
                dve.wait_ge(convin_evac, b + 1)
                if b >= 2:
                    dve.wait_ge(cv_ready, b - 1)
                ns = 2 if b < BBLK else 1
                src, mid = convin[b % 2], convmid[b % 2][:, 0:ns, :]
                w = [cols[:, C_CW + 3 * b + i:C_CW + 3 * b + i + 1] for i in range(3)]
                step(ts(mid, src[:, 0:ns, 1:257], w[1], cols[:, C_CB + b:C_CB + b + 1], ALU.mult, ALU.add))
                step(stt(mid, src[:, 0:ns, 0:256], w[0], mid, ALU.mult, ALU.add))
                stt(mid, src[:, 0:ns, 2:258], w[2], mid, ALU.mult, ALU.add).then_inc(convmid_ready, 1)

            dve.wait_ge(xbc_ps, AHEAD)
            dve.wait_ge(shf_ready, 4)
            for k in range(KT):
                for s in range(2):
                    ts(hT[:, s, k, :], hT[:, s, k, :], shf[:, s, k:k + 1], None, ALU.add).then_inc(ht_shift, 1)
                if k == KT // 2 - 1:
                    dve.wait_ge(beta_ps, 2)
                    V.tensor_copy(beta, PS[:, 6, 0:P].rearrange("p (b s) -> p b s", b=AHEAD)[:, :, 0:2]).then_inc(beta_ready, 1)
            for b in range(NBLK):
                conv(b)
                if b == DT_AT + 1:
                    dve.wait_ge(dt_ps, 2)
                    bias = rowv[:, 0:32].rearrange("p (d h) -> p d h", d=2).unsqueeze(2).to_broadcast([P, 2, 4, HEADS])
                    step(V.tensor_copy(dth(dt_raw), PS[:, 6, 0:128].rearrange("p (t d h) -> p d t h", t=4, d=2)))
                    for d in range(2):
                        step(tt(dth(dt_raw)[:, d], dth(dt_raw)[:, d], rowv[:, 16 * d:16 * d + 16].unsqueeze(1).to_broadcast([P, 4, HEADS]), ALU.add))
                    stt(dt_abs, dt_raw, -1.0, dt_raw, ALU.mult, ALU.min).then_inc(dtabs_ready, 1)
                    dve.wait_ge(ln_ready, 1)
                    step(stt(dt, dt_raw, 0.0, dt_abs, ALU.max, ALU.add))
                    for d in range(2):
                        ea = rowv[:, 32 + 16 * d:48 + 16 * d].unsqueeze(1).to_broadcast([P, 4, HEADS])
                        stt(dth(adt)[:, d], dth(dt)[:, d], -1.0, ea, ALU.mult, ALU.mult).then_inc(adt_ready, 1)
                if b == DT_AT + 3:
                    dve.wait_ge(cum_ready, 1)
                    tt(wst, PS[:, 6, 128:256], cum, ALU.subtract).then_inc(dif_ready, 1)
                    dve.wait_ge(dec_ready, 3)
                    tt(wst, wst, dt, ALU.mult).then_inc(wst_ready, 1)
                tail_tiles(sum(TAIL_QUOTA[:b]), sum(TAIL_QUOTA[:b + 1]))

            def h3(a):
                return a.rearrange("p (h l) -> p h l", h=HEADS)

            def r_make(i):
                c, d = divmod(i, 2)
                a = dth(adt)[:, d, c, :].unsqueeze(2).to_broadcast([P, HEADS, P])
                tri = cst[:, K_TU + d, :].unsqueeze(1).to_broadcast([P, HEADS, P])
                tt(h3(R), a, tri, ALU.mult).then_inc(r_ready, 1)

            def d_make(i):
                c, d = divmod(i, 2)
                dve.wait_ge(b_ps, i + 1)
                cm = dth(cum)[:, d, c, :].unsqueeze(2).to_broadcast([P, HEADS, P])
                mask = cst[:, K_MF + d, :].unsqueeze(1).to_broadcast([P, HEADS, P])
                step(tt(h3(E[d]), PS[:, 2:6, :].rearrange("p b (h l) -> p (b h) l", l=P), cm, ALU.subtract))
                stt(h3(E[d]), h3(E[d]), 0.0, mask, ALU.min, ALU.add).then_inc(d_ready, 1)

            def m_make(i):
                c, d = divmod(i, 2)
                dve.wait_ge(e_ready, i + 1)
                dve.wait_ge(gt_evac, 1)
                e4 = E[d].rearrange("p (g h l) -> p g h l", g=2, h=8)
                for g in range(2):
                    gt = GT[:, g, c, :].unsqueeze(1).to_broadcast([P, 8, P])
                    tt(e4[:, g], e4[:, g], gt, ALU.mult).then_inc(m_ready, 1)

            def st_update(n, new, old):
                t, d = STATES[n]
                step(tt(heads(new), heads(old), per_head(dec, d, t), ALU.mult))
                dve.wait_ge(st_ps, n + 1)
                n2 = new.rearrange("p (a b) -> p a b", a=2)
                tt(n2, n2, PS[:, 6:8, :], ALU.add).then_inc(st_used, 1)
                dve.wait_ge(st_used, n + 1)

            def y_add(c):
                dve.wait_ge(y_ps, c + 1)
                dve.wait_ge(y_init, c + 1)
                y2 = yssm[c].rearrange("p (a b) -> p a b", a=2)
                tt(y2, y2, PS[:, 6:8, :], ALU.add).then_inc(y_used, 1)
                dve.wait_ge(y_used, c + 1)

            def o_add(i):
                c, d = divmod(i, 2)
                dve.wait_ge(o_ps, i + 1)
                tt(heads(R[:, 0:1024]), PS[:, 6:8, :].rearrange("p b (h c) -> p (b h) c", c=HD),
                   per_head(ecum, d, c), ALU.mult).then_inc(o_used, 1)
                dve.wait_ge(o_used, i + 1)
                if i == 2:
                    dve.wait_ge(y_init, 2)
                step(tt(yssm[c], yssm[c], R[:, 0:1024], ALU.add))

            def y_gate(c):
                dve.wait_ge(h_evac, 8)
                tt(yssm[c], yssm[c], zrow[c], ALU.mult).then_inc(yg_ready, 1)
                if c:
                    tail_tiles(64, 80)
                dve.wait_ge(gsq_ready, 2 * c + 2)
                rs = grs[:, 2 * c:2 * c + 2]
                ts(rs, gsq[:, 2 * c:2 * c + 2], 1.0 / NQ, EPS, ALU.mult, ALU.add).then_inc(gvar_ready, 1)
                dve.wait_ge(gstd_ready, c + 1)
                step(V.reciprocal(rs, rs))
                for g in range(2):
                    yg = yssm[c][:, g * NQ:(g + 1) * NQ]
                    ts(yg, yg, rs[:, g:g + 1], None, ALU.mult).then_inc(yn_ready, 1)

            dve.wait_ge(mid_in, 32)
            r_make(0)
            dve.wait_ge(col_ps, 4)
            tt(tailc[:, 0:2, :], PS[:, 7, 256:288].rearrange("p (v k) -> p v k", v=2),
               cols[:, C_BMOD + 32:C_BMOD + 64].rearrange("p (v k) -> p v k", v=2), ALU.add).then_inc(tailc_ready, 1)
            dve.wait_ge(tailc_ready, 1)
            d_make(0)
            r_make(1)
            m_make(0)
            dve.wait_ge(st_used, 1)
            st_update(1, SFB, SFA)
            d_make(1)
            m_make(1)
            dve.wait_ge(st_used, 3)
            st_update(3, SBB, SBA)
            r_make(2)
            y_add(0)
            d_make(2)
            r_make(3)
            st_update(4, SFA, SFB)
            st_update(5, SBA, SBB)
            m_make(2)
            d_make(3)
            m_make(3)
            o_add(0)
            o_add(1)
            y_gate(0)
            o_add(2)
            o_add(3)
            y_add(1)
            y_gate(1)

            def yt_out(c):
                dve.wait_ge(yt_ps, c + 1)
                nw = cols[:, C_NW:C_NW + 8].unsqueeze(2).to_broadcast([P, 8, P])
                src = PS[:, 2 + 4 * c:4 + 4 * c, :].rearrange("p b (k t) -> p (b k) t", t=P)
                tt(catS[:, :, c * P:(c + 1) * P], src, nw, ALU.mult).then_inc(yt_evac, 1)

            yt_out(0)
            yt_out(1)

            def diag_make(v, col):
                if v:
                    dve.wait_ge(g_ps, v)
                tt(diag_all, ident.unsqueeze(1).to_broadcast([P, KT, P]), col.unsqueeze(2).to_broadcast([P, KT, P]),
                   ALU.mult).then_inc(diag_ready, 1)

            g1, c1, gf = tailc[:, 0, :], tailc[:, 2, :], tailc[:, 3, :]
            step(tt(g1, g1, cols[:, C_GQM:C_GQM + KT], ALU.mult))
            diag_make(0, g1)
            tail_tiles(80, 88)
            diag_make(1, tailc[:, 1, :])
            tail_tiles(88, 104)
            dve.wait_ge(col_ps, 6)
            step(tt(c1, PS[:, 4, 0:16], cols[:, C_BMOD + 64:C_BMOD + 80], ALU.add))
            step(stt(c1, c1, 1.0, cols[:, C_GPF:C_GPF + KT], ALU.add, ALU.mult))
            diag_make(2, c1)
            tail_tiles(104, 128)
            dve.wait_ge(col_ps, 8)
            step(tt(gf, PS[:, 4, 16:32], cols[:, C_BMOD + 80:C_BMOD + 96], ALU.add))
            step(tt(gf, gf, cols[:, C_GQF:C_GQF + KT], ALU.mult))

            for t in range(2):
                dve.wait_ge(row_in[t], 32)
            def x1_make(t):
                dve.wait_ge(wo_evac, 7 + t)
                r = yss[:, t:t + 1]
                step(V.tensor_reduce(r, ysq[:, 4 * t:4 * t + 4], AX.X, ALU.add))
                ts(r, r, 1.0 / D, EPS, ALU.mult, ALU.add).then_inc(yvar_ready, 1)
                dve.wait_ge(ystd_ready, t + 1)
                dve.wait_ge(g_evac, 3)
                step(V.reciprocal(r, r))
                step(stt(yrow[t], yrow[t], r, Grow[0], ALU.mult, ALU.mult))
                tt(xrow[t], xrow[t], yrow[t], ALU.add).then_inc(x1_ready, 1)

            def x1_variance(t):
                dve.wait_ge(xsq_ready, t + 1)
                ts(xsq[:, t:t + 1], xsq[:, t:t + 1], 1.0 / D, EPS, ALU.mult, ALU.add).then_inc(xvar_ready, 1)

            def h2_make(t):
                q = xsq[:, t:t + 1]
                dve.wait_ge(xstd_ready, t + 1)
                step(V.reciprocal(q, q))
                step(stt(h2row[t], xrow[t], q, Grow[2], ALU.mult, ALU.mult))
                tt(h2row[t], h2row[t], Grow[1], ALU.add).then_inc(h2_ready, 1)

            x1_make(0)
            diag_make(3, gf)
            x1_variance(0)
            h2_make(0)
            x1_make(1)

            def top16(vals, inds, src, cut, go):
                go(V.max(vals[:, 0:8], src))
                go(V.max_index(inds[:, 0:8], vals[:, 0:8], src))
                go(V.match_replace(cut, vals[:, 0:8], src, LOWEST))
                go(V.max(vals[:, 8:16], cut))
                go(V.max_index(inds[:, 8:16], vals[:, 8:16], cut))

            def in_order(eng):
                eng.sem_clear(route_step)
                n = [0]

                def go(ins):
                    n[0] += 1
                    ins.then_inc(route_step, 1)
                    eng.wait_ge(route_step, n[0])
                return go

            def pick_keys(eng, u, p):
                eng.wait_ge(sc_evac, u + 1 if type(u) is int and u <= 1 else UNITS)
                if not (type(u) is int and u <= 1):
                    eng.wait_ge(v_in[NU - 1], u * (16 * TOPK // NU) - 16 * TOPK // NU)
                    eng.wait_ge(coef_ready, u * TOPK - TOPK)
                eng.sem_inc(dve_go, 1)
                V.tensor_copy(s_cur.unsqueeze(1), scores[:, u:u + 1, :] if type(u) is int else scores[:, bass.ds(u, 1), :]).then_inc(route_copy, 1)
                eng.wait_ge(route_copy, u + 1)
                eng.sem_inc(dve_go, 1)
                go = in_order(eng)
                for a in range(2):
                    top16(v12[:, a, :], i12[:, a, :], s_cur[:, a * NKEYS:(a + 1) * NKEYS], s_cut, go)
                go(V.tensor_copy(i12f, i12))
                c3 = cand.rearrange("p (a b) -> p a b", a=TOPK)
                go(tt(c3, v12[:, 0, :].unsqueeze(2).to_broadcast([P, TOPK, TOPK]),
                      v12[:, 1, :].unsqueeze(1).to_broadcast([P, TOPK, TOPK]), ALU.add))

            def pick_pairs(eng, u, p):
                top, go = tops[p], in_order(eng)
                top16(top, pos, cand, cand_cut, go)
                ts(nmax[:, p:p + 1], top[:, 0:1], -1.0, None, ALU.mult).then_inc(nmax_ready, 1)
                go(ts(posh[:, 0, :], pos, 4, None, ALU.logical_shift_right))
                go(ts(posh[:, 1, :], pos, TOPK - 1, None, ALU.bitwise_and))
                for a in range(2):
                    go(tt(onehot, posh[:, a, :].unsqueeze(2).to_broadcast([P, TOPK, TOPK]),
                          iota16.unsqueeze(1).to_broadcast([P, TOPK, TOPK]), ALU.is_equal))
                    go(tt(onehot, onehot, i12f[:, a, :].unsqueeze(1).to_broadcast([P, TOPK, TOPK]), ALU.mult))
                    go(V.tensor_reduce(e12[:, a, :], onehot, AX.X, ALU.add))
                stt(idx[:, p, :], e12[:, 0, :], float(NKEYS), e12[:, 1, :], ALU.mult, ALU.add).then_inc(idx_ready, 1)

            def weights(eng, u, p):
                eng.wait_ge(eexp_ready, u + 1)
                V.reciprocal(esum[:, p:p + 1], esum[:, p:p + 1]).then_inc(esum_ready, 1)
                eng.wait_ge(esum_ready, u + 1)
                ts(gate[:, p, :], eexp[p], esum[:, p:p + 1], None, ALU.mult).then_inc(gate_ready, 1)
                eng.wait_ge(gate_ready, u + 1)

            def unit(eng, u, p, blk):
                first, last = type(u) is int and u <= 1, type(u) is int and u == UNITS - 1
                for j in range(TOPK):
                    if first:
                        n = u * TOPK + j
                        rows = early[n % EARLY]
                        eng.wait_ge(early_in[n % EARLY], 16 * (n // EARLY + 1))
                    else:
                        rows = uslot[j % NU]
                        eng.wait_ge(u_in[j % NU], u * (16 * TOPK // NU) + 16 * (j // NU - 3))
                    V.tensor_tensor_reduce(out=rows, in0=rows, in1=h2row[blk], scale=1.0,
                                           scalar=0.0, op0=ALU.mult, op1=ALU.add,
                                           accum_out=dots[:, p, j:j + 1]).then_inc(u_used, 1)
                    if j == (TOPK - 1 if first else NU - 1) and not last and not (first and u == 0):
                        pick_keys(eng, u + 1, 1 - p)
                        pick_pairs(eng, u + 1, 1 - p)
                        weights(eng, u + 1, 1 - p)
                    if first and u == 0:
                        if j == 3:
                            weights(eng, 0, 0)
                        if j == 4:
                            pick_keys(eng, 1, 1)
                        if j == 10:
                            pick_pairs(eng, 1, 1)
                        if j == TOPK - 1:
                            weights(eng, 1, 1)

            def after_block(eng, blk):
                f = fss[:, blk:blk + 1]
                eng.wait_ge(fsq_ready, 4 * (blk + 1))
                step(V.tensor_reduce(f, fsq[:, 4 * blk:4 * blk + 4], AX.X, ALU.add))
                ts(f, f, 1.0 / D, EPS, ALU.mult, ALU.add).then_inc(xvar_ready, 1)
                eng.wait_ge(xstd_ready, blk + 3)
                step(V.reciprocal(f, f))
                eng.wait_ge(g_evac, 4)
                for q in range(PARTS):
                    part = slice(q * D // PARTS, (q + 1) * D // PARTS)
                    step(stt(h2row[blk][:, part], PS[:, 4 * blk + q, :], f, Grow[3][:, part], ALU.mult, ALU.mult))
                    tt(xrow[blk][:, part], xrow[blk][:, part], h2row[blk][:, part], ALU.add).then_inc(out_ready, 1)

            pick_keys(dve, 0, 0)
            pick_pairs(dve, 0, 0)
            x1_variance(1)
            h2_make(1)
            expert_blocks(dve, unit, after_block, True)

        @block.tensor
        def _(pe):
            M = nc.tensor.matmul

            def ring_wait(j):
                n = len([i for i in range(j % 2, j + 1, 2) if i != R_XBC])
                pe.wait_ge(ring_in[j % 2], 16 * PIECES * n)

            def row_transposes(t):
                pe.wait_ge(xn_ready, t + 1)
                for q in range(4):
                    if t:
                        pe.wait_ge(ht_evac, 4 * (t - 1) + q + 1)
                    for i in range(4):
                        k = 4 * q + i
                        ins = nc.tensor.transpose(PS[:, q, i * P:(i + 1) * P], xn[t % 2][:, k * P:(k + 1) * P], ident)
                    ins.then_inc(xt_ps, 1)

            def mod_transposes(v):
                pe.wait_ge(modrow_evac, 2 - v)
                for i in range(4):
                    ins = nc.tensor.transpose(PS[:, 6 + v, i * P:(i + 1) * P], modrow[v][:, i * P:(i + 1) * P], ident)
                ins.then_inc(modT_ps, 1)

            pe.wait_ge(small_in, 16 * N_SMALL)
            pe.wait_ge(s2pad_ready, 1)
            def mod_product(v, k, w):
                for j in range(4):
                    ins = M(PS[32 * j:32 * j + 32, 4 + v, :], s2pad[:, k, :], w[:, j * NQ:(j + 1) * NQ],
                            start=(k == 0), stop=(k == KT - 1), tile_position=(0, 32 * j))
                return ins

            for i in range(4):
                ring_wait(i)
                for kk in range(4):
                    ins = mod_product(1, 4 * i + kk, wmod_slot[i % 2][:, kk, :])
                ins.then_inc(mod_ps, 1)
                if i == 2:
                    pe.wait_ge(ssq_ready, 4)
                    for t in range(4):
                        row_transposes(t)
            mod_transposes(1)

            def shift_piece(i):
                pe.wait_ge(shift_in[i % 3], 16 * (i // 3 + 1))
                for kk in range(2):
                    ins = mod_product(0, 2 * i + kk, shift_slot[i % 3][:, kk, :])
                ins.then_inc(shift_ps, 1)

            def xbc(b):
                j = R_XBC + b // 4
                if j > R_XBC:
                    ring_wait(j)
                if b >= AHEAD:
                    pe.wait_ge(convin_evac, b - 3 if b < AHEAD + 2 else b - 1)
                ns = 2 if b < BBLK else 1
                dst = PS[:, b if b < AHEAD else b % 2, 0:256 * ns]
                for k in range(KT):
                    if b == 0:
                        pe.wait_ge(ht_mod, 2 * k + 2)
                        if k == 0:
                            pe.wait_ge(piece_in[0], 16)
                        if k == KT // PIECES:
                            pe.wait_ge(piece_in[1], 16 * (PIECES - 1))
                    if b == AHEAD:
                        pe.wait_ge(ht_shift, 2 * k + 2)
                    rhs = hT[:, :, k, :] if ns == 2 else hT[:, 0, k, :]
                    o = dst.rearrange("p (s t) -> p s t", s=2) if ns == 2 else dst
                    ins = M(o, wring[j % 2][:, k, (b % 4) * P:(b % 4 + 1) * P], rhs, start=(k == 0), stop=(k == KT - 1))
                ins.then_inc(xbc_ps, 1)

            def shift_bias():
                pe.wait_ge(shf_ready, 4)
                for i in range(4):
                    for j in range(4):
                        k = 4 * i + j
                        ins = M(PS[32 * j:32 * j + 32, 5, :], s2pad[:, k, :], wring[R_XBC % 2][:, k, :],
                                start=(i == 0), stop=(i == 3), tile_position=(0, 32 * j))
                ins.then_inc(beta_ps, 1)
                pe.wait_ge(betapart_ready, 1)
                for b in range(AHEAD):
                    ins = M(PS[:, 6, 32 * b:32 * b + 32], betapart[:, b * P:(b + 1) * P], sel32, start=True, stop=True)
                ins.then_inc(beta_ps, 1)

            def back_transposes(b):
                pe.wait_ge(cv_ready, b + 1)
                pe.wait_ge(row_evac, b - 1) if b >= 2 else pe.wait_ge(convin_evac, b + 3)
                src = convout[b % 2].rearrange("p s t -> p (s t)") if b < XBLK else BT[:, b - XBLK, :]
                for t in range(4):
                    ins = nc.tensor.transpose(PS[:, 2 + b % 2, t * P:(t + 1) * P], src[:, t * P:(t + 1) * P], ident)
                ins.then_inc(tr_ps, 1)

            def column_sums(half, bank=7, first=256):
                pe.wait_ge(tail_used, KT * (half + 1))
                for j in range(8):
                    n = first + (half % 4) * 8 + j
                    ins = M(PS[:, bank, n:n + 1], tail_acc[half][:, j * P:(j + 1) * P], ones[:, 0:1], start=True, stop=True)
                ins.then_inc(col_ps, 1)

            back = {4: [0], 5: [1, 2], 6: [3, 4]}
            for b in range(NBLK + 2):
                if b < NBLK:
                    xbc(b)
                if b < len(SHIFT_AFTER):
                    for i in range(sum(SHIFT_AFTER[:b]), sum(SHIFT_AFTER[:b + 1])):
                        shift_piece(i)
                    if b == len(SHIFT_AFTER) - 1:
                        mod_transposes(0)
                if b == AHEAD - 1:
                    shift_bias()
                if AHEAD <= b < BBLK + 2:
                    for i in back.get(b, [b - 2]):
                        back_transposes(i)
                if b == DT_AT:
                    pe.wait_ge(mid_in, 32)
                    for i in range(4):
                        for j in range(4):
                            k = 4 * i + j
                            ins = M(PS[32 * j:32 * j + 32, 7, :].rearrange("p (s t) -> p s t", s=2), dtw[:, k, :], hT[:, :, k, :],
                                    start=(i == 0), stop=(i == 3), tile_position=(0, 32 * j))
                    ins.then_inc(dt_ps, 1)
                if b == DT_AT + 1:
                    pe.wait_ge(dtpart_ready, 1)
                    for t in range(4):
                        ins = M(PS[:, 6, 32 * t:32 * t + 32], dtpart[:, t * P:(t + 1) * P], sel32, start=True, stop=True)
                    ins.then_inc(dt_ps, 1)
                if b == DT_AT + 2:
                    pe.wait_ge(adt_ready, 2)
                    M(PS[:, 6, 0:64], cst[:, K_TU, :], adt[:, 0:64], start=True, stop=True)
                    M(PS[:, 6, 64:128], cst[:, K_TL, :], adt[:, 64:128], start=True, stop=True)
                    M(PS[:, 6, 128:256], ones, adt, start=True, stop=True).then_inc(cum_ps, 1)
                if b in (7, 9, 11):
                    column_sums((b - 7) // 2)

            def half_chunk(j):
                c, t = divmod(j, 2)
                ring_wait(R_FZ + c)
                pe.wait_ge(h_evac, j - 1) if j >= 2 else pe.wait_ge(convin_evac, NBLK)
                for k in range(KT):
                    ins = M(PS[:, j % 2, :], hT[:, 0, k, t * P:(t + 1) * P], wring[(R_FZ + c) % 2][:, k, :],
                            start=(k == 0), stop=(k == KT - 1))
                ins.then_inc(h_ps, 1)

            def cum_rows(i):
                pe.wait_ge(r_ready, i + 1)
                if i:
                    pe.wait_ge(d_ready, i)
                for q in range(4):
                    ins = M(PS[:, 2 + q, :], ones, R[:, q * NQ:(q + 1) * NQ], start=True, stop=True)
                ins.then_inc(b_ps, 1)

            def state(n):
                t, d = STATES[n]
                pe.wait_ge(w_ready, {0: 1, 1: 2, 2: 3, 3: 4, 4: 7, 5: 8}[n])
                pe.wait_ge(st_used, n) if n else pe.wait_ge(gt_evac, 1)
                if n == 0:
                    pe.wait_ge(tailc_ready, 1)
                if n == 4:
                    pe.wait_ge(y_used, 1)
                for g in range(2):
                    w = {4: 0, 5: 1}.get(n, n % 2)
                    ins = M(PS[:, 6 + g, :], brow[:, t, g, :], wx[w][:, g * NQ:(g + 1) * NQ], start=True, stop=True)
                ins.then_inc(st_ps, 1)

            def y_inside(c):
                pe.wait_ge(w_ready, 6 if c == 0 else 10)
                pe.wait_ge(m_ready, 4 * c + 4)
                pe.wait_ge(st_used, 4) if c == 0 else pe.wait_ge(o_used, 4)
                for h in range(HEADS):
                    o = PS[:, 6 + h // 8, (h % 8) * HD:(h % 8 + 1) * HD]
                    for d in range(2):
                        ins = M(o, E[d][:, h * P:(h + 1) * P], wx[d][:, h * HD:(h + 1) * HD], start=(d == 0), stop=(d == 1))
                ins.then_inc(y_ps, 1)

            def y_state(i):
                c, d = divmod(i, 2)
                st = [SFB, SBA, SFA, SBB][i]
                pe.wait_ge(st_used, 6)
                if i:
                    pe.wait_ge(o_used, i)
                for g in range(2):
                    ins = M(PS[:, 6 + g, :], CT[:, g, c * P:(c + 1) * P], st[:, g * NQ:(g + 1) * NQ], start=True, stop=True)
                ins.then_inc(o_ps, 1)

            def pq(g):
                if g:
                    pe.wait_ge(pq_evac, g)
                else:
                    pe.wait_ge(late_in, 32)
                    pe.wait_ge(h_evac, 8)
                for b in range(2):
                    for m, k in ((0, 0), (0, 1), (2, 0), (2, 1)):
                        ins = M(PS[:, b, 256 * (m // 2):256 * (m // 2) + 256], dft[:, k, m, b * P:(b + 1) * P],
                                fmix[:, g, k, :], start=(k == 0), stop=(k == 1))
                ins.then_inc(pq_ps, 1)

            def at_make(g):
                pe.wait_ge(at_evac, g) if g else pe.wait_ge(d_ready, 4)
                for b in range(2):
                    ch = 256 * g + P * b
                    for k in range(2):
                        ins = M(PS[:, 2 + b, :].rearrange("p (m n) -> p m n", m=2), frow[k][:, ch:ch + P], dft[:, k, 0:2, :],
                                start=(k == 0), stop=(k == 1))
                ins.then_inc(at_ps, 1)

            def yf_make(g):
                pe.wait_ge(at_evac, g + 1)
                pe.wait_ge(pq_evac, g + 1)
                if g:
                    pe.wait_ge(yf_evac, g)
                for b in range(2):
                    for n, (m, k) in enumerate(((0, 0), (0, 1), (1, 0), (1, 1))):
                        ins = M(PS[:, 4, 256 * b:256 * b + 256], PQ[:, k, 256 * m + P * b:256 * m + P * b + P],
                                AT[:, k, 256 * m:256 * m + 256], start=(n == 0), stop=(n == 3))
                ins.then_inc(yf_ps, 1)

            def y_transposes(c):
                pe.wait_ge(yn_ready, 2 * c + 2)
                pe.wait_ge(at_evac, 4) if c == 0 else pe.wait_ge(y_used, 2)
                for k in range(8):
                    ins = nc.tensor.transpose(PS[:, 2 + 4 * c + k // 4, (k % 4) * P:(k % 4 + 1) * P],
                                              yssm[c][:, k * P:(k + 1) * P], ident)
                ins.then_inc(yt_ps, 1)

            pe.wait_ge(dec_ready, 3)
            pe.wait_ge(row_evac, BBLK)
            half_chunk(0)
            pe.wait_ge(cv_ready, NBLK)
            for g in range(2):
                for c in range(2):
                    ins = M(PS[:, 6, (2 * g + c) * P:(2 * g + c + 1) * P], BT[:, g, c * P:(c + 1) * P],
                            CT[:, g, c * P:(c + 1) * P], start=True, stop=True)
            ins.then_inc(gt_ps, 1)
            column_sums(3)
            cum_rows(0)
            state(0)
            half_chunk(1)
            cum_rows(1)
            state(1)
            half_chunk(2)
            state(2)
            half_chunk(3)
            state(3)
            half_chunk(4)
            y_inside(0)
            half_chunk(5)
            cum_rows(2)
            state(4)
            half_chunk(6)
            cum_rows(3)
            state(5)
            half_chunk(7)
            pq(0)
            y_state(0)
            at_make(0)
            y_state(1)
            yf_make(0)
            pq(1)
            y_state(2)
            at_make(1)
            y_state(3)
            yf_make(1)
            pq(2)
            y_inside(1)
            at_make(2)
            yf_make(2)
            pq(3)
            at_make(3)
            yf_make(3)
            y_transposes(0)

            def row_spread(v):
                pe.wait_ge(diag_ready, v + 1)
                if v:
                    pe.wait_ge(g_evac, v)
                if v == 3:
                    pe.wait_ge(q_evac, UNITS)
                    pe.wait_ge(sc_evac, UNITS)
                for q in range(4):
                    ins = M(PS[:, 4 + q, :].rearrange("p (k n) -> p k n", k=4), ones, diag_all[:, 4 * q:4 * q + 4, :],
                            start=True, stop=True)
                ins.then_inc(g_ps, 1)

            def w_out(n, t, k0, k1):
                for k in range(k0, k1):
                    cat = catF if k < 8 else catS
                    ins = M(PS[:, (n % 2) * 2 + t, :], cat[:, k % 8, t * P:(t + 1) * P], wring[(R_OUT + n) % 2][:, k, :],
                            start=(k == 0), stop=(k == KT - 1))
                return ins

            pe.wait_ge(yf_evac, GROUPS)
            for n in range(4):
                ring_wait(R_OUT + n)
                if n == 0:
                    pe.wait_ge(pq_evac, GROUPS)
                    w_out(0, 0, 0, 8)
                    w_out(0, 1, 0, 8)
                    y_transposes(1)
                    pe.wait_ge(yt_evac, 2)
                for t in range(2):
                    if n >= 2:
                        pe.wait_ge(wo_evac, 2 * (n - 2) + t + 1)
                    ins = w_out(n, t, 0 if n else 8, KT)
                    ins.then_inc(wo_ps, 1)
                    if (n, t) in SPREAD_AT:
                        row_spread(SPREAD_AT.index((n, t)))
                    if (n, t) in SUMS_AT:
                        for half in SUMS_AT[n, t]:
                            pe.wait_ge(g_evac, 2 if half < 6 else 3)
                            column_sums(half, 4, 0)

            def h2_transposes(t):
                pe.wait_ge(h2_ready, t + 1)
                for q in range(4):
                    if t:
                        pe.wait_ge(h2T_evac, q + 1)
                    for i in range(4):
                        k = 4 * q + i
                        ins = nc.tensor.transpose(PS[:, q, i * P:(i + 1) * P], h2row[t][:, k * P:(k + 1) * P], ident)
                    ins.then_inc(h2T_ps, 1)

            def query(u):
                t, h = divmod(u, PH)
                j = R_QUERY + h // 4
                ring_wait(j)
                if u == 0:
                    pe.wait_ge(g_evac, 3)
                if u >= 2:
                    pe.wait_ge(q_evac, u - 1)
                for k in range(KT):
                    if h == 0 and k % 4 == 0:
                        pe.wait_ge(h2T_evac, 4 * t + k // 4 + 1)
                    ins = M(PS[:, 4 + u % 2, 0:P], wring[j % 2][:, k, (h % 4) * P:(h % 4 + 1) * P], h2T[t][:, k, :],
                            start=(k == 0), stop=(k == KT - 1))
                ins.then_inc(q_ps, 1)

            def key_scores(u):
                t, h = divmod(u, PH)
                pe.wait_ge(q_evac, u + 1)
                if u >= 2:
                    pe.wait_ge(sc_evac, u - 1)
                M(PS[:, 6 + u % 2, 0:256], qT[:, h, t * P:(t + 1) * P], keys[:, h, :], start=True, stop=True).then_inc(sc_ps, 1)

            pe.wait_ge(wo_evac, 8)
            h2_transposes(0)
            for u in range(UNITS):
                query(u)
                if u == 0:
                    pe.wait_ge(keys_in, 32)
                if u != 1:
                    key_scores(max(u - 1, 0))
                if u == H2T_AT:
                    h2_transposes(1)
            key_scores(UNITS - 1)
            row_spread(3)

            def unit(eng, u, p, blk):
                for j in range(TOPK):
                    eng.wait_ge(v_in[j % NU], u * (16 * TOPK // NU) + 16 * (j // NU + 1))
                    eng.wait_ge(coef_ready, u * TOPK + j + 1)
                    if type(u) is int and u == PH and j == 0:
                        eng.wait_ge(g_evac, 4)
                    for b in range(4):
                        ins = M(PS[:, 4 * blk + b, :], diag_slot[j % 8], vslot[j % NU][:, b * NQ:(b + 1) * NQ],
                                start=(type(u) is int and u % PH == 0 and j == 0),
                                stop=(type(u) is int and u % PH == PH - 1 and j == TOPK - 1))
                        if type(u) is int and u % PH == PH - 1 and j == TOPK - 1 and b < 3:
                            ins.then_inc(acc_ps, 1)
                    ins.then_inc(v_used, 1)

            expert_blocks(pe, unit, lambda eng, blk: None, False)


def _columns(v):
    import numpy as np
    return np.ascontiguousarray(np.asarray(v).reshape(-1, P).T)


def _layout(i):
    import numpy as np
    f = np.float32
    n = np.arange(P)
    upper = (n[:, None] <= n[None, :])
    cst = np.stack([np.eye(P), np.ones((P, P)), upper, upper.T, np.where(upper, 0, MASKED),
                    np.where(upper.T, 0, MASKED)], axis=1).astype(f)
    m = np.arange(256)
    angle = 2 * np.pi * ((m[:, None] * m[None, :]) % 256) / 256
    waves = np.stack([np.cos(angle), np.sin(angle), -np.sin(angle)], axis=1) / 16
    dft = waves.reshape(2, P, 3, 256).transpose(1, 0, 2, 3).astype(f)
    conv_w = np.asarray(i["conv_w"][0]).reshape(3, NBLK, P).transpose(2, 1, 0).reshape(P, 3 * NBLK)
    cols = np.concatenate([_columns(i["c"]), _columns(i["c_ctx"]), _columns(i["b_mod"]), _columns(i["g_pre_mix"]),
                           _columns(i["g_post_mix"]), _columns(i["g_pre_ffn"]), _columns(i["g_post_ffn"]),
                           conv_w, _columns(i["conv_b"]), _columns(i["ssm_norm_w"])], axis=1)
    rows = np.concatenate([np.asarray(i[k]).reshape(-1) for k in ("dt_bias_f", "dt_bias_b", "a_log_f", "a_log_b",
                                                                  "d_skip_f", "d_skip_b")] + [np.zeros(32, f)])[None]
    keys = [np.asarray(i[k][0]).transpose(2, 0, 1) for k in ("sub_keys_1", "sub_keys_2")]
    arrays = [i["x"][0], i["ctx"][0], i["w_mod"][0], i["w_in"][0], i["w_fmix"][0], i["w_out"][0], i["w_query"][0],
              keys[0], keys[1], i["expert_u"][0], i["expert_v"][0], cols, rows, cst, dft,
              np.concatenate([np.broadcast_to(np.arange(TOPK, dtype=f), (P, TOPK)), (n[:, None] % 32 == np.arange(32)).astype(f)], axis=1)]
    return [np.ascontiguousarray(a) for a in arrays]


NAMES = ["x", "ctx", "w_mod", "w_in", "w_fmix", "w_out", "w_query", "k1t", "k2t", "expert_u", "expert_v",
         "cols", "rows", "cst", "dft", "iota"]


def kernel(**inputs):
    import concourse.bacc as bacc
    from concourse.bass_utils import run_bass_kernel_spmd

    nc = bacc.Bacc("TRN2", target_bir_lowering=False, num_devices=1)
    arrays, args = {}, []
    for name, a in zip(NAMES, _layout(inputs)):
        arrays[f"in_{name}"] = a
        args.append(nc.dram_tensor(f"in_{name}", a.shape, F32, kind="ExternalInput").ap())
    out = nc.dram_tensor("out", (2 * P, D), F32, kind="ExternalOutput").ap()
    build(nc, *args, out)
    result = run_bass_kernel_spmd(nc, [arrays], core_ids=[0])
    return result.results[0]["out"].reshape(1, 2 * P, D)
```
